# Optimizing a Trainium2 kernel written in Bass

```python
import math, functools
import jax, jax.numpy as jnp
from jax import lax
import numpy as np

D_MODEL = 1024
BATCH = 1
SEQ = 1024
DEPTH = 1
DEC_BATCH = 1
DEC_SEQ = 64
PAST_LEN = 256

CHUNK = 64
D_MIX = D_MODEL
HEAD_DIM = 64
N_HEADS = (D_MIX // 2) // HEAD_DIM
N_KV_HEADS = 2
WINDOW = 128
N_PREV_CHUNKS = WINDOW // CHUNK
C_CONV = D_MIX - N_HEADS * HEAD_DIM
CONV_WIDTH = 31
N_GROUPS = 4
EXPERTS_PER_GROUP = 8
N_EXPERTS = N_GROUPS * EXPERTS_PER_GROUP
TOP_K = 2
D_EXPERT = D_MODEL // 2
PLE_DIM = 256
MOE_BLOCK = 128
EPS = 1e-6
Q_W = N_HEADS * HEAD_DIM
KV_W = N_KV_HEADS * HEAD_DIM
D_IN = Q_W + 2 * KV_W + 2 * C_CONV
IN_SPLITS = (Q_W, Q_W + KV_W, Q_W + 2 * KV_W, Q_W + 2 * KV_W + C_CONV)

kernel_name = 'hybrid_swa_conformer_hmoe_stream_step'

def rms_norm(x, g):
    xf = x.astype(jnp.float32)
    y = xf * lax.rsqrt(jnp.mean(xf * xf, axis=-1, keepdims=True) + EPS)
    return (y * g.astype(jnp.float32)).astype(x.dtype)

def layer_norm(x, g, b):
    xf = x.astype(jnp.float32)
    mu = jnp.mean(xf, axis=-1, keepdims=True)
    var = jnp.mean(jnp.square(xf - mu), axis=-1, keepdims=True)
    y = (xf - mu) * lax.rsqrt(var + EPS)
    return (y * g.astype(jnp.float32) + b.astype(jnp.float32)).astype(x.dtype)

def alibi_slopes(n):
    return jnp.array([2.0 ** (-8.0 * (i + 1) / n) for i in range(n)], jnp.float32)

def mixer_project(x, lp):
    B, T, _ = x.shape
    z = rms_norm(x, lp['g_mix']) @ lp['w_in']
    q, k, v, a, b = jnp.split(z, IN_SPLITS, axis=-1)
    q = rms_norm(q.reshape(B, T, N_HEADS, HEAD_DIM), lp['g_q'])
    k = rms_norm(k.reshape(B, T, N_KV_HEADS, HEAD_DIM), lp['g_k'])
    v = v.reshape(B, T, N_KV_HEADS, HEAD_DIM)
    u = a * jax.nn.sigmoid(b)
    return q, k, v, u

def chunk_band(t):
    B, T = t.shape[:2]
    nc = T // CHUNK
    tc = t.reshape(B, nc, CHUNK, t.shape[2], t.shape[3])
    tp = jnp.pad(tc, ((0, 0), (N_PREV_CHUNKS, 0), (0, 0), (0, 0), (0, 0)))
    return jnp.concatenate([tp[:, j:j + nc] for j in range(N_PREV_CHUNKS + 1)], axis=2)

def band_attention(q, k, v, q_pos, k_pos, k_valid, sinks):
    B, NB, QL = q.shape[:3]
    G = N_HEADS // N_KV_HEADS
    qg = q.reshape(B, NB, QL, N_KV_HEADS, G, HEAD_DIM)
    s = jnp.einsum('bnqhgd,bnkhd->bnhgqk', qg, k).astype(jnp.float32) * (HEAD_DIM ** -0.5)
    slopes = alibi_slopes(N_HEADS).reshape(N_KV_HEADS, G)
    dist = jnp.abs(q_pos[:, :, None] - k_pos[:, None, :]).astype(jnp.float32)
    s = s - slopes[None, None, :, :, None, None] * dist[None, :, None, None]
    s = jnp.where(k_valid[None, :, None, None, None, :], s, -jnp.inf)
    sink = jnp.broadcast_to(sinks.astype(jnp.float32).reshape(1, 1, N_KV_HEADS, G, 1, 1), s.shape[:-1] + (1,))
    pr = jax.nn.softmax(jnp.concatenate([s, sink], axis=-1), axis=-1)[..., :-1]
    o = jnp.einsum('bnhgqk,bnkhd->bnqhgd', pr.astype(v.dtype), v)
    return o.reshape(B, NB, QL, N_HEADS * HEAD_DIM)

def causal_depthwise(u_ext, w, b):
    C = u_ext.shape[-1]
    y = lax.conv_general_dilated(u_ext, w[:, None, :].astype(u_ext.dtype), (1,), 'VALID',
                                 dimension_numbers=('NWC', 'WIO', 'NWC'), feature_group_count=C)
    return y + b

def hier_route(h, w_coarse, b_coarse, w_fine, b_fine):
    lc = (h @ w_coarse).astype(jnp.float32) + b_coarse.astype(jnp.float32)
    grp = jnp.argmax(lc, axis=-1).astype(jnp.int32)
    g1 = jnp.take_along_axis(jax.nn.softmax(lc, axis=-1), grp[:, None], axis=-1)
    lf = jnp.einsum('nd,gde->nge', h, w_fine).astype(jnp.float32) + b_fine.astype(jnp.float32)
    lf = jnp.take_along_axis(lf, grp[:, None, None], axis=1)[:, 0]
    tv, ti = lax.top_k(lf, TOP_K)
    wts = g1 * jax.nn.softmax(tv, axis=-1)
    idx = grp[:, None] * EXPERTS_PER_GROUP + ti.astype(jnp.int32)
    return idx, wts

def moe_ffn(h, idx, wts, w_g, w_u, w_d):
    N, D = h.shape
    K = idx.shape[1]
    E = w_g.shape[0]
    A = N * K
    n_blocks = (A + E * (MOE_BLOCK - 1) + MOE_BLOCK - 1) // MOE_BLOCK
    S = n_blocks * MOE_BLOCK
    flat_e = idx.reshape(A)
    flat_t = jnp.repeat(jnp.arange(N, dtype=jnp.int32), K)
    flat_w = wts.reshape(A)
    order = jnp.argsort(flat_e)
    se, st, sw = flat_e[order], flat_t[order], flat_w[order]
    counts = jnp.bincount(flat_e, length=E)
    start = jnp.cumsum(counts) - counts
    padded = (counts + MOE_BLOCK - 1) // MOE_BLOCK * MOE_BLOCK
    pend = jnp.cumsum(padded)
    pstart = pend - padded
    dest = pstart[se] + (jnp.arange(A) - start[se])
    slot_tok = jnp.full((S,), N, jnp.int32).at[dest].set(st)
    slot_w = jnp.zeros((S,), sw.dtype).at[dest].set(sw)
    block_e = jnp.minimum(jnp.searchsorted(pend, jnp.arange(n_blocks) * MOE_BLOCK, side='right'), E - 1)
    h_pad = jnp.concatenate([h, jnp.zeros((1, D), h.dtype)], axis=0)
    xs = h_pad[slot_tok].reshape(n_blocks, MOE_BLOCK, D)

    def expert_block(args):
        xb, e = args
        return (jax.nn.silu(xb @ w_g[e]) * (xb @ w_u[e])) @ w_d[e]

    ys = lax.map(expert_block, (xs, block_e)).reshape(S, D)
    out = jnp.zeros((N + 1, D), h.dtype).at[slot_tok].add(ys * slot_w[:, None].astype(ys.dtype))
    return out[:N]

def finish_layer(x, p, o_attn, c, lp):
    B, T, D = x.shape
    c = jax.nn.silu(layer_norm(c, lp['g_cn'], lp['b_cn'])) @ lp['w_pw'] + lp['b_pw']
    mixed = jnp.concatenate([rms_norm(o_attn, lp['g_oa']), rms_norm(c, lp['g_oc'])], axis=-1) @ lp['w_out']
    x = x + mixed
    h = rms_norm(x, lp['g_ffn']).reshape(B * T, D)
    idx, wts = hier_route(h, lp['w_coarse'], lp['b_coarse'], lp['w_fine'], lp['b_fine'])
    x = x + moe_ffn(h, idx, wts, lp['w_e_gate'], lp['w_e_up'], lp['w_e_down']).reshape(B, T, D)
    gate = jax.nn.sigmoid(rms_norm(x, lp['g_ple']) @ lp['w_ple_gate'])
    return x + gate * (p @ lp['w_ple_proj'])

def setup_inputs(seed: int = 0) -> dict:
    key = jax.random.key(seed)
    ks = jax.random.split(key, 40)
    f32 = jnp.float32

    def nrm(k, shape, scale=1.0):
        return scale * jax.random.normal(k, shape, f32)

    def gain(k, shape):
        return 1.0 + nrm(k, shape, 0.1)

    w_cache = min(WINDOW, PAST_LEN)
    L = DEPTH
    return {
        'x_prompt': nrm(ks[0], (BATCH, SEQ, D_MODEL)),
        'x_sample': nrm(ks[1], (DEC_BATCH, DEC_SEQ, D_MODEL)),
        'p_prompt': nrm(ks[2], (DEPTH, BATCH, SEQ, PLE_DIM)),
        'p_sample': nrm(ks[3], (DEPTH, DEC_BATCH, DEC_SEQ, PLE_DIM)),
        'cache_k': nrm(ks[4], (DEPTH, DEC_BATCH, w_cache, N_KV_HEADS, HEAD_DIM)),
        'cache_v': nrm(ks[5], (DEPTH, DEC_BATCH, w_cache, N_KV_HEADS, HEAD_DIM)),
        'state_conv': nrm(ks[6], (DEPTH, DEC_BATCH, CONV_WIDTH - 1, C_CONV), 0.5),
        'g_mix': gain(ks[7], (L, D_MODEL)),
        'w_in': nrm(ks[8], (L, D_MODEL, D_IN), D_MODEL ** -0.5),
        'g_q': gain(ks[9], (L, HEAD_DIM)),
        'g_k': gain(ks[10], (L, HEAD_DIM)),
        'sinks': nrm(ks[11], (L, N_HEADS), 0.5),
        'w_dw': nrm(ks[12], (L, CONV_WIDTH, C_CONV), CONV_WIDTH ** -0.5),
        'b_dw': nrm(ks[13], (L, C_CONV), 0.02),
        'g_cn': gain(ks[14], (L, C_CONV)),
        'b_cn': nrm(ks[15], (L, C_CONV), 0.02),
        'w_pw': nrm(ks[16], (L, C_CONV, C_CONV), C_CONV ** -0.5),
        'b_pw': nrm(ks[17], (L, C_CONV), 0.02),
        'g_oa': gain(ks[18], (L, Q_W)),
        'g_oc': gain(ks[19], (L, C_CONV)),
        'w_out': nrm(ks[20], (L, D_MIX, D_MODEL), D_MIX ** -0.5),
        'g_ffn': gain(ks[21], (L, D_MODEL)),
        'w_coarse': nrm(ks[22], (L, D_MODEL, N_GROUPS), D_MODEL ** -0.5),
        'b_coarse': nrm(ks[23], (L, N_GROUPS), 0.01),
        'w_fine': nrm(ks[24], (L, N_GROUPS, D_MODEL, EXPERTS_PER_GROUP), D_MODEL ** -0.5),
        'b_fine': nrm(ks[25], (L, N_GROUPS, EXPERTS_PER_GROUP), 0.01),
        'w_e_gate': nrm(ks[26], (L, N_EXPERTS, D_MODEL, D_EXPERT), D_MODEL ** -0.5),
        'w_e_up': nrm(ks[27], (L, N_EXPERTS, D_MODEL, D_EXPERT), D_MODEL ** -0.5),
        'w_e_down': nrm(ks[28], (L, N_EXPERTS, D_EXPERT, D_MODEL), D_EXPERT ** -0.5),
        'g_ple': gain(ks[29], (L, D_MODEL)),
        'w_ple_gate': nrm(ks[30], (L, D_MODEL, D_MODEL), D_MODEL ** -0.5),
        'w_ple_proj': nrm(ks[31], (L, PLE_DIM, D_MODEL), PLE_DIM ** -0.5),
    }

def reference(x_prompt, x_sample, p_prompt, p_sample, cache_k, cache_v, state_conv,
              g_mix, w_in, g_q, g_k, sinks, w_dw, b_dw, g_cn, b_cn, w_pw, b_pw, g_oa, g_oc,
              w_out, g_ffn, w_coarse, b_coarse, w_fine, b_fine, w_e_gate, w_e_up, w_e_down,
              g_ple, w_ple_gate, w_ple_proj):
    yp, ys = x_prompt, x_sample
    nkp, nvp, ncp, nks, nvs, ncs = [], [], [], [], [], []
    for l in range(DEPTH):
        lp = {'g_mix': g_mix[l], 'w_in': w_in[l], 'g_q': g_q[l], 'g_k': g_k[l], 'sinks': sinks[l],
              'w_dw': w_dw[l], 'b_dw': b_dw[l], 'g_cn': g_cn[l], 'b_cn': b_cn[l], 'w_pw': w_pw[l],
              'b_pw': b_pw[l], 'g_oa': g_oa[l], 'g_oc': g_oc[l], 'w_out': w_out[l], 'g_ffn': g_ffn[l],
              'w_coarse': w_coarse[l], 'b_coarse': b_coarse[l], 'w_fine': w_fine[l], 'b_fine': b_fine[l],
              'w_e_gate': w_e_gate[l], 'w_e_up': w_e_up[l], 'w_e_down': w_e_down[l],
              'g_ple': g_ple[l], 'w_ple_gate': w_ple_gate[l], 'w_ple_proj': w_ple_proj[l]}

        B, T, _ = yp.shape
        nc = T // CHUNK
        q, k, v, u = mixer_project(yp, lp)
        band_len = (N_PREV_CHUNKS + 1) * CHUNK
        q_pos = jnp.arange(T, dtype=jnp.int32).reshape(nc, CHUNK)
        k_pos = (jnp.arange(nc, dtype=jnp.int32)[:, None] - N_PREV_CHUNKS) * CHUNK + jnp.arange(band_len, dtype=jnp.int32)[None]
        o = band_attention(q.reshape(B, nc, CHUNK, N_HEADS, HEAD_DIM), chunk_band(k), chunk_band(v),
                           q_pos, k_pos, k_pos >= 0, lp['sinks']).reshape(B, T, Q_W)
        c = causal_depthwise(jnp.pad(u, ((0, 0), (CONV_WIDTH - 1, 0), (0, 0))), lp['w_dw'], lp['b_dw'])
        w_keep = min(WINDOW, T)
        nkp.append(k[:, T - w_keep:])
        nvp.append(v[:, T - w_keep:])
        ncp.append(u[:, T - (CONV_WIDTH - 1):])
        yp = finish_layer(yp, p_prompt[l], o, c, lp)

        DB, DS, _ = ys.shape
        W = cache_k.shape[2]
        q, k, v, u = mixer_project(ys, lp)
        k_all = jnp.concatenate([cache_k[l].astype(k.dtype), k], axis=1)
        v_all = jnp.concatenate([cache_v[l].astype(v.dtype), v], axis=1)
        q_pos = (W + jnp.arange(DS, dtype=jnp.int32))[None]
        k_pos = jnp.arange(W + DS, dtype=jnp.int32)[None]
        o = band_attention(q[:, None], k_all[:, None], v_all[:, None], q_pos, k_pos,
                           jnp.ones((1, W + DS), bool), lp['sinks'])[:, 0]
        u_all = jnp.concatenate([state_conv[l].astype(u.dtype), u], axis=1)
        c = causal_depthwise(u_all, lp['w_dw'], lp['b_dw'])
        nks.append(k_all[:, k_all.shape[1] - W:])
        nvs.append(v_all[:, v_all.shape[1] - W:])
        ncs.append(u_all[:, u_all.shape[1] - (CONV_WIDTH - 1):])
        ys = finish_layer(ys, p_sample[l], o, c, lp)

    return (yp, ys, jnp.stack(nkp), jnp.stack(nvp), jnp.stack(ncp), jnp.stack(nks), jnp.stack(nvs), jnp.stack(ncs))


_drawn_inputs = setup_inputs


def setup_inputs(seed=0):
    import zlib

    import numpy as np

    out = dict(_drawn_inputs(seed))
    spreads = {}
    factors = {'b_cn': 3.022, 'b_coarse': 8.0, 'b_fine': 7.246, 'g_ple': 4.253}
    for name, (base, spread) in spreads.items():
        noise = np.random.default_rng([zlib.crc32(name.encode()), seed]).standard_normal(out[name].shape)
        drawn = base * np.exp(spread * noise) if base else spread * noise
        out[name] = __import__('jax').numpy.asarray(drawn.astype(out[name].dtype))
    for name, factor in factors.items():
        out[name] = (out[name] * factor).astype(out[name].dtype)
    return out
```

```python
from contextlib import ExitStack

import concourse.bass as bass
from concourse import mybir

ALU = mybir.AluOpType
ACT = mybir.ActivationFunctionType
AX = mybir.AxisListType
F32 = mybir.dt.float32
F32R = mybir.dt.float32r
BF16 = mybir.dt.bfloat16
I32 = mybir.dt.int32

P = 128
D = 1024
SEQ, SAMPLE = 1024, 64
TOKENS = SEQ + SAMPLE
NT = SEQ // P + 1
TS = NT - 1
KD = D // P
HD = 64
NH, NKV = 8, 2
QW, KVW = NH * HD, NKV * HD
C = 512
KC = C // P
TAPS = 31
HALO = TAPS - 1
DE = 512
KE = DE // P
NG, EPG = 4, 8
NE = NG * EPG
NR = NG + NE
NOVF = (2 * TOKENS) // (P + 1)
NBLK = NE + NOVF
PLE = 256
EPS = 1e-6
NEG = -1e30
CH = 2048
LOV = 1280
UW = HALO + SEQ + HALO + SAMPLE
U_SAMPLE = HALO + SEQ
SPLIT_JOBS = 13


def rows_of(t):
    return P if t < TS else SAMPLE


def build_step(nc, a, o):
    ctx = ExitStack()
    with ctx:
        def sem(name):
            return ctx.enter_context(nc.semaphore(name))

        CONST, B_SIZE = 1500, 8596
        RAW_MOE = 6 * CH
        mem = ctx.enter_context(nc.sbuf_tensor("mem", [P, CONST + NT * D + RAW_MOE + B_SIZE], F32))
        whl = ctx.enter_context(nc.sbuf_tensor("whl", [P, 2, 4 * CH], F32R))
        ahl = ctx.enter_context(nc.sbuf_tensor("ahl", [P, 2, 2, D], F32R))
        hhl = ctx.enter_context(nc.sbuf_tensor("hhl", [P, 2, DE], F32R))
        ps = ctx.enter_context(nc.psum_tensor("ps", [P, 8, 512], F32))

        top = [0]

        def take(n):
            v = mem[:, top[0]:top[0] + n]
            top[0] += n
            return v

        def bank(b, n=512):
            return ps[:, b, 0:n]

        def banks2(b):
            return ps[:, b:b + 2, :].rearrange("p b n -> p (b n)")

        ident = take(P)
        convw = take(KC * 32).rearrange("p (c j) -> p c j", c=KC)
        kcache = take(NKV * P)
        wr = take(KD * NR).rearrange("p (k r) -> p k r", k=KD)
        rbias = take(NR)
        lg = take(NT * NR).rearrange("p (t r) -> p t r", t=NT)
        idx_gather = take(NBLK)
        idx_scatter = take(NBLK)
        wtab = take(NBLK)
        ebk = take(NOVF)
        novf = take(1)
        idxg_cur = [take(1) for _ in range(2)]
        idxs_cur = [take(1) for _ in range(2)]
        w_cur = [take(1) for _ in range(2)]
        neghalf = take(12)
        ssx, rsx = take(NT), take(NT)
        ms = take(12)
        ss10, r10 = take(10), take(10)
        sink = take(NH)
        negm, msink, esink = take(NH), take(NH), take(NH)
        mx = take(NH)
        den, rden = take(NH), take(NH)
        ss1, r1 = take(1), take(1)
        bnst, bnag = take(6), take(2)
        assert top[0] <= CONST, top[0]
        top[0] = CONST
        R = take(NT * D).rearrange("p (t n) -> p t n", t=NT)
        A0 = top[0]
        raw1 = [take(CH) for _ in range(2)]
        uT = take(KC * UW).rearrange("p (c n) -> p c n", c=KC)
        S = take(4 * 2 * P)
        qT = take(NH * P)
        pT = take(D)
        u2 = take(C)
        assert top[0] <= A0 + RAW_MOE, top[0] - A0
        raw = [mem[:, A0 + CH * i:A0 + CH * (i + 1)] for i in range(6)]
        B0 = top[0] = A0 + RAW_MOE
        xb = [take(D) for _ in range(2)]
        gmix = take(D)
        gqk = take(QW + KVW)
        bias = take(NH * 2 * P).rearrange("p (h k) -> p h k", h=NH)
        kTb = take(2 * NKV * 2 * P).rearrange("p (b g k) -> p b g k", b=2, g=NKV)
        vb = take(4 * KVW).rearrange("p (s n) -> p s n", s=4)
        qkn = take(QW + 2 * KVW)
        goa = take(C)
        assert top[0] <= B0 + B_SIZE, top[0] - B0
        top[0] = B0 + 2 * D
        gcn, bcn, bpw, goc = take(C), take(C), take(C), take(C)
        gffn = take(D)
        hb = [take(D) for _ in range(2)]
        hT = take(D)
        assert top[0] <= B0 + B_SIZE
        c1 = [hb[0][:, 0:C], hb[0][:, C:2 * C]]
        c2 = [hb[1][:, 0:C], hb[1][:, C:2 * C]]
        top[0] = B0
        iota = take(P)
        rev8, thr8 = take(8), take(8)
        ones = take(P)
        tri = take(P)
        dc, eqc, og = take(NT * NG), take(NT * NG), take(NT * NG)
        gmx, se, m1, m2, mt, e2, rw = (take(NT) for _ in range(7))
        lsel, eqf, o1, o2 = (take(NT * EPG) for _ in range(4))
        A1, A2 = take(NT * NE), take(NT * NE)
        A12 = take((NT + 1) * NE)
        pos = take((NT + 1) * NE)
        prod = take(NT * NE)
        lt = take(NE * NE)
        ovf8 = take(NE * 8)
        ovf, start, end = take(NE), take(NE), take(NE)
        pk, ek, stk, bk, sk, vk, wk, idk = ([take(NT), take(NT)] for _ in range(8))
        cmp9 = take(NT * 8)
        oh = take(NT * NBLK)
        V = take(NT * 2 * NBLK)
        Ph = take(NT * P)
        tmp48 = take(NBLK)
        eb = take(NOVF * NE)
        idmask = take(NT)
        tab = take(2 * NBLK)
        assert top[0] <= B0 + B_SIZE, top[0] - B0
        top[0] = B0
        xs = [take(D) for _ in range(2)]
        th = take(DE)
        y = take(D)
        graw = take(CH)
        wproj = take(CH)
        assert top[0] <= B0 + B_SIZE
        top[0] = A0
        yb = [[take(D) for _ in range(2)] for _ in range(2)]
        xn3 = [take(D) for _ in range(2)]
        tg = take(D)
        fin = [take(D) for _ in range(2)]
        pin = [take(PLE) for _ in range(2)]
        pT3 = take(PLE)
        assert top[0] <= A0 + RAW_MOE
        gple = xs[0]

        H = nc.dram_tensor("h_rows", (TOKENS, D), F32).ap()
        Y = nc.dram_tensor("y_rows", (2 * TOKENS, D), F32).ap()

        s_id = sem("identity_made")
        s_const = sem("constants_made")
        s_ld = sem("small_inputs_in")
        s_ld2 = sem("late_gains_in")
        s_st = sem("conv_state_in")
        s_gm = sem("mixer_gain_in")
        s_uo = sem("conv_state_out")
        s_cv = sem("cache_v_in")
        s_x = [sem("x_in_0"), sem("x_in_1")]
        s_raw = [sem("chunk_in_0"), sem("chunk_in_1")]
        s_whi = sem("weights_hi")
        s_wlv = sem("weights_lo_vector")
        s_wlp = sem("weights_lo_pool")
        s_ss = sem("sum_squares_x")
        s_rs = sem("rstd_x")
        s_xn = sem("x_normed")
        s_xt = sem("x_transposed")
        s_xh = sem("x_hi")
        s_xl = sem("x_lo")
        s_z = sem("projected")
        s_th = sem("glu_tanh")
        s_u = sem("glu_out")
        s_ut = sem("glu_transposed")
        s_uT = sem("glu_in_conv_buffer")
        s_stt = sem("state_transposed")
        s_uout = sem("glu_rows_out")
        s_conv = sem("conv_ops")
        s_zero = sem("conv_pad_zero")
        s_sq = sem("qk_squared")
        s_v = sem("v_copied")
        s_ssq = sem("qk_sums")
        s_r10 = sem("qk_rstd")
        s_zev = sem("qk_scaled")
        s_qkn = sem("qk_normed")
        s_qkt = sem("qk_transposed")
        s_qT = sem("qT_ready")
        s_kT = sem("kT_ready")
        s_sc = sem("scores")
        s_sb = sem("scores_biased")
        s_nm = sem("neg_max")
        s_ex = sem("exps")
        s_pt = sem("probs_transposed")
        s_pT = sem("pT_ready")
        s_pv = sem("attended")
        s_oe = sem("attention_out")
        s_osq = sem("attention_sum_squares")
        s_ors = sem("attention_rstd")
        s_o = sem("attention_normed")
        s_ct = sem("conv_transposed")
        s_bn = sem("conv_stats")
        s_crs = sem("conv_rstd")
        s_cn = sem("conv_centred")
        s_cg = sem("conv_layer_normed")
        s_cth = sem("conv_tanh")
        s_c2 = sem("conv_swished")
        s_c2t = sem("swish_transposed")
        s_ch = sem("swish_hi")
        s_cl = sem("swish_lo")
        s_pw = sem("pointwise")
        s_c3 = sem("pointwise_biased")
        s_c3s = sem("pointwise_sum_squares")
        s_c3r = sem("pointwise_rstd")
        s_c4 = sem("pointwise_normed")
        s_w = sem("mixed")
        s_x1 = sem("mixer_residual")
        s_hs = sem("h_sum_squares")
        s_hr = sem("h_rstd")
        s_h = sem("h_ready")
        s_hst = [sem("h_rows_out_0"), sem("h_rows_out_1")]
        s_ht = sem("h_transposed")
        s_hT = sem("hT_ready")
        s_rl = sem("router_products")
        s_lg = sem("router_logits")
        s_rt = sem("routing_step")
        s_rta = sem("routing_exps")
        s_rtp = sem("routing_products")
        s_tab = sem("slot_table_ready")
        s_mraw = [sem(f"expert_chunk_in_{c}") for c in range(6)]
        s_mhi = sem("expert_hi")
        s_mlv = sem("expert_lo_vector")
        s_mlp = sem("expert_lo_pool")
        s_use = sem("expert_chunk_used")
        s_g = [sem("gathered_0"), sem("gathered_1")]
        s_idx = sem("slot_indices")
        s_idx0 = sem("first_indices")
        s_xst = sem("slots_transposed")
        s_xsh = sem("slots_hi")
        s_xsl = sem("slots_lo")
        s_mth = sem("expert_tanh")
        s_mg = sem("expert_gated")
        s_mh = sem("expert_hidden")
        s_mht = sem("hidden_transposed")
        s_hh = sem("hidden_hi")
        s_hl = sem("hidden_lo")
        s_y0 = sem("expert_out_left")
        s_y1 = sem("expert_out_right")
        s_sc_d = sem("scattered")
        s_moe = sem("experts_done")
        s_go = sem("pool_passed")
        g_idx, g_gath, g_raw, g_use = sem("ovf_indices"), sem("ovf_gathered"), sem("ovf_chunk_in"), sem("ovf_chunk_used")
        g_pe, g_act, g_dve, g_scat = sem("ovf_pe"), sem("ovf_act"), sem("ovf_vector"), sem("ovf_scattered")
        s_y = [sem("y_in_0"), sem("y_in_1")]
        s_p = [sem("p_in_0"), sem("p_in_1")]
        s_gp = sem("ple_inputs_in")
        s_x2 = sem("moe_residual")
        s_3s = sem("x2_sum_squares")
        s_3r = sem("x2_rstd")
        s_3n = sem("x2_normed")
        s_3t = sem("x2_transposed")
        s_3h = sem("x2_hi")
        s_3l = sem("x2_lo")
        s_3g = sem("ple_gate_products")
        s_3th = sem("ple_tanh")
        s_3pt = sem("p_transposed")
        s_3pT = sem("pT3_ready")
        s_3p = sem("ple_proj_products")
        s_3m = sem("ple_gated")
        s_3f = sem("y_ready")
        s_out = [sem("y_out_0"), sem("y_out_1")]
        s_kv = sem("cache_rows_out")
        chains = {e: sem(f"chain_{e}") for e in ("pool", "act", "dve")}
        chain_at = dict.fromkeys(chains, 0)

        def link(eng, name, ins):
            chain_at[name] += 1
            ins.then_inc(chains[name], 1)
            eng.wait_ge(chains[name], chain_at[name])

        w_in = a["w_in"][0].rearrange("(k p) n -> p k n", p=P)
        w_pw = a["w_pw"][0].rearrange("(k p) n -> p k n", p=P)
        w_out = a["w_out"][0].rearrange("(k p) n -> p k n", p=P)
        GLU0 = QW + 2 * KVW
        PW0 = KD * GLU0
        mixer_chunks = (
            [(w_in[:, 2 * i:2 * i + 2, GLU0:], 2 * i * D) for i in range(4)]
            + [(w_in[:, 2 * i:2 * i + 2, 0:GLU0], 2 * i * GLU0) for i in range(4)]
            + [(w_pw, PW0)]
            + [(w_out[:, 2 * i:2 * i + 2, :], 2 * i * D) for i in range(4)])
        J_QKV, J_PW, J_OUT = 4, 8, 9

        def chunk_size(j):
            return 2 * GLU0 if J_QKV <= j < J_PW else CH

        def lo_cut(j):
            return chunk_size(j) * 5 // 8 if chunk_size(j) < CH else LOV

        def region_free(eng, j):
            if J_QKV <= j < J_OUT:
                eng.wait_ge(s_z, NT)
            elif j >= J_OUT:
                eng.wait_ge(s_z, 2 * NT)
                if j == SPLIT_JOBS - 1:
                    eng.wait_ge(s_pw, NT)

        def mixer_hi(eng, j):
            eng.wait_ge(s_raw[j % 2], 16 * (j // 2 + 1))
            region_free(eng, j)
            n, at = chunk_size(j), mixer_chunks[j][1]
            nc.scalar.activation(whl[:, 0, at:at + n], raw1[j % 2][:, 0:n], ACT.Copy).then_inc(s_whi, 1)

        def lo_part(which, out, hi, full):
            return which.tensor_tensor(out, full, hi.bitcast(F32), ALU.subtract)

        def mixer_lo(eng, which, signal, j, first, last):
            eng.wait_ge(s_whi, j + 1)
            at = mixer_chunks[j][1]
            lo_part(which, whl[:, 1, at + first:at + last], whl[:, 0, at + first:at + last],
                    raw1[j % 2][:, first:last]).then_inc(signal, 1)

        def weights_ready(eng, j):
            eng.wait_ge(s_wlv, j + 1)
            eng.wait_ge(s_wlp, j + 1)

        def split_product(out, act_hi, act_lo, w_at, first, last):
            nc.tensor.matmul(out, act_hi, whl[:, 0, w_at], start=first, stop=False)
            nc.tensor.matmul(out, act_hi, whl[:, 1, w_at], start=False, stop=False)
            return nc.tensor.matmul(out, act_lo, whl[:, 0, w_at], start=False, stop=last)

        def act_tile(buf, k):
            return ahl[:, buf, 0, k * P:(k + 1) * P], ahl[:, buf, 1, k * P:(k + 1) * P]

        def x_source(t):
            return a["x_prompt"][0, t * P:(t + 1) * P, :] if t < TS else a["x_sample"][0]

        LOADS = NH + NKV + 2 + 1 + NG + 2

        conv_spans = [(0, 0, 4), (HALO + 0, 4, 4), (None, TS, 1)]
        CONV_OPS = 3 * KC * TAPS

        def conv_ops(eng):
            n = 0
            for span, (_, t0, nt) in enumerate(conv_spans):
                w = nt * P if t0 < TS else SAMPLE
                base = t0 * P if t0 < TS else U_SAMPLE
                for j in range(TAPS):
                    for c in range(KC):
                        src = uT[:, c, base + j:base + j + w]
                        if t0 < TS:
                            acc = R[:, t0:t0 + nt, C + c * P:C + (c + 1) * P]
                            src = src.rearrange("p (t n) -> p t n", n=P)
                        else:
                            acc = R[:, TS, C + c * P:C + c * P + w]
                        if j == 0:
                            if c == 0:
                                eng.wait_ge(s_uT, t0 + nt)
                                eng.wait_ge(s_zero, 2)
                                eng.wait_ge(s_stt, 4)
                            ins = nc.vector.tensor_scalar(acc, src, convw[:, c, 0:1], convw[:, c, TAPS:TAPS + 1], ALU.mult, ALU.add)
                        else:
                            eng.wait_ge(s_conv, n - KC + 1)
                            ins = nc.vector.scalar_tensor_tensor(acc, src, convw[:, c, j:j + 1], acc, ALU.mult, ALU.add)
                        ins.then_inc(s_conv, 1)
                        n += 1
                        yield

        block = ctx.enter_context(nc.Block())

        @block.sync
        def _(sp):
            def load_x(n):
                t = n % NT
                if n >= 2:
                    if n < 20:
                        sp.wait_ge(s_xt, 2 * n - 2)
                    else:
                        sp.wait_ge(s_x1, n - 19)
                sp.dma_start(xb[n % 2][0:rows_of(t), :], x_source(t)).then_inc(s_x[n % 2], 16)

            def load_chunk(j):
                if j >= 2:
                    sp.wait_ge(s_wlv, j - 1)
                    sp.wait_ge(s_wlp, j - 1)
                sp.dma_start(raw1[j % 2][:, 0:chunk_size(j)].rearrange("p (k n) -> p k n", k=mixer_chunks[j][0].shape[1]),
                             mixer_chunks[j][0]).then_inc(s_raw[j % 2], 16)

            load_x(0)
            sp.dma_start(gmix, a["g_mix"][0].partition_broadcast(P)).then_inc(s_gm, 16)
            load_chunk(0)
            load_x(1)
            load_chunk(1)
            sp.dma_start(S[0:HALO, 0:C], a["state_conv"][0, 0]).then_inc(s_st, 16)
            sp.dma_start(S[:, C:C + KVW], a["cache_k"][0, 0].rearrange("t g d -> t (g d)")).then_inc(s_st, 16)
            sp.dma_start(u2[0:TAPS, :], a["w_dw"][0]).then_inc(s_st, 16)
            sp.dma_start(u2[TAPS:TAPS + 1, :], a["b_dw"]).then_inc(s_st, 16)
            for h in range(NH):
                sp.dma_start(gqk[:, h * HD:(h + 1) * HD], a["g_q"][0].partition_broadcast(P)).then_inc(s_ld, 16)
            for h in range(NKV):
                sp.dma_start(gqk[:, QW + h * HD:QW + (h + 1) * HD], a["g_k"][0].partition_broadcast(P)).then_inc(s_ld, 16)
            sp.dma_start(goa, a["g_oa"][0].partition_broadcast(P)).then_inc(s_ld, 16)
            sp.dma_start(sink, a["sinks"][0].partition_broadcast(P)).then_inc(s_ld, 16)
            sp.dma_start(wr[:, :, 0:NG], a["w_coarse"][0].rearrange("(k p) g -> p k g", p=P)).then_inc(s_ld, 16)
            for g in range(NG):
                sp.dma_start(wr[:, :, NG + g * EPG:NG + (g + 1) * EPG],
                             a["w_fine"][0, g].rearrange("(k p) e -> p k e", p=P)).then_inc(s_ld, 16)
            sp.dma_start(rbias[:, 0:NG], a["b_coarse"][0].partition_broadcast(P)).then_inc(s_ld, 16)
            sp.dma_start(rbias[:, NG:NR], a["b_fine"][0].rearrange("g e -> (g e)").partition_broadcast(P)).then_inc(s_ld, 16)
            load_chunk(2)
            load_chunk(3)
            sp.dma_start(vb[:, 3, :], a["cache_v"][0, 0].rearrange("t g d -> t (g d)")).then_inc(s_cv, 16)
            load_chunk(4)
            load_chunk(5)
            for n in range(2, 2 * NT):
                load_x(n)
                if n == NT + 1:
                    for j in range(6, 10):
                        load_chunk(j)
                if n == NT + 2:
                    sp.wait_ge(s_uout, 2)
                    sp.dma_start(o["new_conv_prompt"][0, 0], S[P - HALO:P, 0:C]).then_inc(s_uo, 16)
                    sp.dma_start(o["new_conv_sample"][0, 0], S[SAMPLE - HALO:SAMPLE, C:2 * C]).then_inc(s_uo, 16)
            kp, vp = (o[x][0, 0].rearrange("t g d -> t (g d)") for x in ("new_k_prompt", "new_v_prompt"))
            ks, vs = (o[x][0, 0].rearrange("t g d -> t (g d)") for x in ("new_k_sample", "new_v_sample"))
            ck, cv = (a[x][0, 0].rearrange("t g d -> t (g d)") for x in ("cache_k", "cache_v"))
            sp.dma_start(ks[0:P - SAMPLE], ck[SAMPLE:P]).then_inc(s_kv, 16)
            sp.dma_start(vs[0:P - SAMPLE], cv[SAMPLE:P]).then_inc(s_kv, 16)
            sp.wait_ge(s_qkn, TS)
            sp.wait_ge(s_v, TS)
            sp.dma_start(kp, qkn[:, QW:QW + KVW]).then_inc(s_kv, 16)
            sp.dma_start(vp, vb[:, (TS - 1) % 3, :]).then_inc(s_kv, 16)
            sp.wait_ge(s_qkn, NT)
            sp.wait_ge(s_v, NT)
            sp.dma_start(ks[P - SAMPLE:P], qkn[0:SAMPLE, QW:QW + KVW]).then_inc(s_kv, 16)
            sp.dma_start(vs[P - SAMPLE:P], vb[0:SAMPLE, TS % 3, :]).then_inc(s_kv, 16)
            load_x(2 * NT)
            load_x(2 * NT + 1)
            sp.wait_ge(s_o, NT)
            sp.wait_ge(s_kv, 16 * 6)
            for dst, name in ((gcn, "g_cn"), (bcn, "b_cn"), (bpw, "b_pw"), (goc, "g_oc"), (gffn, "g_ffn")):
                sp.dma_start(dst, a[name][0].partition_broadcast(P)).then_inc(s_ld2, 16)
            for j in range(10, SPLIT_JOBS):
                load_chunk(j)
            gate_v, up_v, down_v = (a[x][0] for x in ("w_e_gate", "w_e_up", "w_e_down"))

            def expert_chunk(e, c):
                w = (gate_v, gate_v, up_v, up_v, down_v, down_v)[c]
                w = w[e] if isinstance(e, int) else w[bass.ds(e, 1)].rearrange("e a b -> (e a) b")
                w = w.rearrange("(k p) n -> p k n", p=P)
                return w[:, 4 * (c % 2):4 * (c % 2) + 4, :] if c < 4 else w[:, 2 * (c % 2):2 * (c % 2) + 2, :]

            def raw_view(c):
                return raw[c].rearrange("p (k n) -> p k n", k=4 if c < 4 else 2)

            sp.wait_ge(s_conv, CONV_OPS)
            for c in (2, 3, 4, 5):
                sp.dma_start(raw_view(c), expert_chunk(0, c)).then_inc(s_mraw[c], 16)
            for n in range(2 * NT + 2, 3 * NT):
                load_x(n)
                t = n - 2 * NT - 2
                if t == 0:
                    for c in (0, 1):
                        sp.wait_ge(s_wlv, SPLIT_JOBS - c)
                        sp.wait_ge(s_wlp, SPLIT_JOBS - c)
                        sp.dma_start(raw_view(c), expert_chunk(0, c)).then_inc(s_mraw[c], 16)
                sp.wait_ge(s_h, t + 1)
                sp.dma_start(H[t * P:(t + 1) * P], hb[t % 2]).then_inc(s_hst[t % 2], 16)
            for t in (NT - 2, NT - 1):
                sp.wait_ge(s_h, t + 1)
                sp.dma_start(H[t * P:t * P + rows_of(t)], hb[t % 2][0:rows_of(t)]).then_inc(s_hst[t % 2], 16)
            with sp.Fori(1, NE) as e:
                for c in range(6):
                    sp.wait_ge(s_mlv, 6 * e + (c - 5))
                    sp.wait_ge(s_mlp, 6 * e + (c - 5))
                    sp.dma_start(raw_view(c), expert_chunk(e, c)).then_inc(s_mraw[c], 16)
            w_gate = a["w_ple_gate"][0].rearrange("(k p) n -> p k n", p=P)
            for c in range(4):
                sp.wait_ge(s_mlv, 6 * NE + c - 5)
                sp.wait_ge(s_mlp, 6 * NE + c - 5)
                sp.dma_start(raw[c].rearrange("p (k n) -> p k n", k=2), w_gate[:, 2 * c:2 * c + 2, :]).then_inc(s_mraw[c], 16)
            sp.dma_start(wproj.rearrange("p (k n) -> p k n", k=2), a["w_ple_proj"][0].rearrange("(k p) n -> p k n", p=P)).then_inc(s_gp, 16)
            sp.wait_ge(s_tab, 1)
            n_ovf = sp.value_load(novf[0:1, 0:1].bitcast(I32), min_val=0, max_val=NOVF)
            with sp.Fori(0, NOVF) as j:
                with sp.If(n_ovf > j):
                    e = sp.value_load(ebk[0:1, bass.ds(j, 1)].bitcast(I32), min_val=0, max_val=NE - 1)
                    for c in range(6):
                        sp.wait_ge(g_use, 6 * j + c + 1)
                        sp.dma_start(graw.rearrange("p (k n) -> p k n", k=4 if c < 4 else 2), expert_chunk(e, c)).then_inc(g_raw, 16)
            sp.wait_ge(s_moe, 1)
            sp.dma_start(gple, a["g_ple"][0].partition_broadcast(P)).then_inc(s_gp, 16)
            sp.wait_ge(s_mlv, 6 * NE + 4)
            sp.wait_ge(s_mlp, 6 * NE + 4)
            for t in range(NT + 2):
                if t < NT:
                    b, r = t % 2, rows_of(t)
                    if t >= 2:
                        sp.wait_ge(s_x2, t - 1)
                        sp.wait_ge(s_3pt, t - 1)
                    for k in range(2):
                        sp.dma_start(yb[b][k][0:r], Y[k * TOKENS + t * P:k * TOKENS + t * P + r]).then_inc(s_y[b], 16)
                    src = a["p_prompt"][0, 0, t * P:(t + 1) * P] if t < TS else a["p_sample"][0, 0]
                    sp.dma_start(pin[b][0:r], src).then_inc(s_p[b], 16)
                if t >= 2:
                    q = t - 2
                    r = rows_of(q)
                    sp.wait_ge(s_3f, q + 1)
                    dst = o["y_prompt"][0, q * P:(q + 1) * P] if q < TS else o["y_sample"][0]
                    sp.dma_start(dst, fin[q % 2][0:r]).then_inc(s_out[q % 2], 16)
            sp.wait_ge(s_out[0], 16 * 5)
            sp.wait_ge(s_out[1], 16 * 4)

        @block.gpsimd
        def _(pool):
            last_pow = []

            def rstd(dst, src, scale, signal, count):
                n = dst.shape[1]
                if last_pow:
                    pool.wait_ge(*last_pow)
                last_pow[:] = (signal, count)
                link(pool, "pool", nc.gpsimd.tensor_scalar(ms[:, 0:n], src, scale, EPS, ALU.mult, ALU.add))
                nc.gpsimd.tensor_tensor(dst, ms[:, 0:n], neghalf[:, 0:n], ALU.pow).then_inc(signal, 1)

            link(pool, "pool", nc.gpsimd.memset(ident, 0.0))
            nc.gpsimd.affine_select(out=ident, in_=ident, compare_op=ALU.not_equal, fill=1.0, base=0,
                                    pattern=[[-1, P]], channel_multiplier=1).then_inc(s_id, 1)
            link(pool, "pool", nc.gpsimd.memset(neghalf, -0.5))
            nc.gpsimd.memset(uT[:, :, 0:HALO], 0.0).then_inc(s_zero, 1)
            nc.gpsimd.memset(R[:, TS, C:2 * C], 0.0).then_inc(s_zero, 1)
            nc.gpsimd.iota(bias[:, 0, :], [[-1, 2 * P]], base=P, channel_multiplier=1,
                           allow_small_or_imprecise_dtypes=True).then_inc(s_const, 1)

            def pool_chunk(j):
                mixer_lo(pool, nc.gpsimd, s_wlp, j, lo_cut(j), chunk_size(j))

            for t in range(NT):
                pool.wait_ge(s_ss, t + 1)
                rstd(rsx[:, t:t + 1], ssx[:, t:t + 1], 1.0 / D, s_rs, t + 1)
                if t == 0:
                    for j in range(4):
                        pool_chunk(j)
            for j in range(4, 9):
                pool_chunk(j)
            for t in range(NT + 1):
                if t < NT:
                    pool.wait_ge(s_ssq, t + 1)
                    rstd(r10, ss10, 1.0 / HD, s_r10, t + 1)
                if t >= 1:
                    pool.wait_ge(s_osq, t)
                    pool.wait_ge(s_o, t - 1)
                    rstd(r1, ss1, 1.0 / C, s_ors, t)
            for j in range(J_OUT, SPLIT_JOBS - 1):
                pool_chunk(j)
            pool.wait_ge(s_ld2, 16 * 5)
            for t in range(NT + 1):
                if t < NT:
                    pool.wait_ge(s_bn, t + 1)
                    rstd(r10[:, 0:1], bnag[:, 1:2], 1.0, s_crs, t + 1)
                    pool.wait_ge(s_cn, t + 1)
                    link(pool, "pool", nc.gpsimd.tensor_tensor(c1[t % 2], c1[t % 2], gcn, ALU.mult))
                    nc.gpsimd.tensor_tensor(c1[t % 2], c1[t % 2], bcn, ALU.add).then_inc(s_cg, 1)
                if t >= 1:
                    pool.wait_ge(s_c3s, t)
                    pool.wait_ge(s_c4, t - 1)
                    rstd(r1, ss1, 1.0 / C, s_c3r, t)
            pool_chunk(SPLIT_JOBS - 1)
            for t in range(NT):
                pool.wait_ge(s_hs, t + 1)
                pool.wait_ge(s_h, t)
                rstd(r1, ss1, 1.0 / D, s_hr, t + 1)
            pool.wait_ge(s_h, NT)
            pool.wait_ge(s_hst[0], 16 * 5)
            pool.wait_ge(s_hst[1], 16 * 4)
            nc.gpsimd.iota(iota, [[1, P]], base=0, channel_multiplier=0, allow_small_or_imprecise_dtypes=True).then_inc(s_const, 1)
            nc.gpsimd.iota(rev8, [[-1, 8]], base=8, channel_multiplier=0, allow_small_or_imprecise_dtypes=True).then_inc(s_const, 1)
            nc.gpsimd.iota(thr8, [[P, 8]], base=P, channel_multiplier=0, allow_small_or_imprecise_dtypes=True).then_inc(s_const, 1)
            nc.gpsimd.iota(idk[0], [[P, NT]], base=1, channel_multiplier=1, allow_small_or_imprecise_dtypes=True).then_inc(s_const, 1)
            nc.gpsimd.memset(ones, 1.0).then_inc(s_const, 1)
            link(pool, "pool", nc.gpsimd.memset(tri, 1.0))
            nc.gpsimd.affine_select(out=tri, in_=tri, compare_op=ALU.is_gt, fill=0.0, base=0,
                                    pattern=[[1, P]], channel_multiplier=-1).then_inc(s_const, 1)
            pool.wait_ge(s_tab, 1)

            def col(table, v):
                return table[:, v:v + 1] if isinstance(v, int) else table[:, bass.ds(v, 1)]

            def passed():
                pool.sem_inc(s_go, 1)

            def gather(b, signal):
                nc.gpsimd.indirect_dma_start(out=xs[b], out_offset=None, in_=H,
                                             in_offset=bass.IndirectOffsetOnAxis(ap=idxg_cur[b].bitcast(I32), axis=0)).then_inc(signal, 16)

            def scatter(b, signal):
                nc.gpsimd.indirect_dma_start(out=Y, out_offset=bass.IndirectOffsetOnAxis(ap=idxs_cur[b].bitcast(I32), axis=0),
                                             in_=y, in_offset=None, bounds_check=2 * TOKENS - 1,
                                             oob_is_err=False).then_inc(signal, 16)

            def expert_lo(J, slot, c):
                pool.wait_ge(s_mhi, J + 1)
                lo_part(nc.gpsimd, whl[:, 1, slot * CH + LOV:(slot + 1) * CH], whl[:, 0, slot * CH + LOV:(slot + 1) * CH],
                        raw[c][:, LOV:CH]).then_inc(s_mlp, 1)

            for e in range(2):
                link(pool, "pool", nc.gpsimd.tensor_copy(idxg_cur[e].bitcast(I32), col(idx_gather, e).bitcast(I32)))
                gather(e, s_g[e])
            for c in range(4):
                expert_lo(c, c, c)
            nc.gpsimd.memset(y, 0.0).then_inc(s_idx0, 1)
            nc.gpsimd.memset(w_cur[0], 4096.0).then_inc(s_idx0, 1)
            pool.wait_ge(s_idx0, 2)
            nc.gpsimd.tensor_copy(idxs_cur[0].bitcast(I32), w_cur[0]).then_inc(s_idx0, 1)
            pool.wait_ge(s_idx0, 3)
            scatter(0, s_sc_d)
            pool.wait_ge(s_sc_d, 16)
            with pool.Fori(0, NE, 2) as e0:
                for b in range(2):
                    e = e0 + b
                    pool.wait_ge(s_xst, e + 1)
                    pool.wait_ge(s_g[b], 8 * e0 + 16)
                    passed()
                    nc.gpsimd.tensor_copy(idxg_cur[b].bitcast(I32), col(idx_gather, e + 2).bitcast(I32)).then_inc(s_idx, 1)
                    nc.gpsimd.tensor_copy(idxs_cur[b].bitcast(I32), col(idx_scatter, e).bitcast(I32)).then_inc(s_idx, 1)
                    nc.gpsimd.tensor_copy(w_cur[b], col(wtab, e)).then_inc(s_idx, 1)
                    pool.wait_ge(s_idx, 3 * e + 3)
                    passed()
                    gather(b, s_g[b])
                    for c in range(4, 10):
                        expert_lo(6 * e + c, (6 * b + c) % 4, c % 6)
                    pool.wait_ge(s_y0, e + 2)
                    pool.wait_ge(s_y1, e + 2)
                    passed()
                    scatter(b, s_sc_d)
            pool.wait_ge(s_g[0], 16 * (NE // 2 + 1))
            pool.wait_ge(s_g[1], 16 * (NE // 2 + 1))
            pool.wait_ge(s_sc_d, 16 * (NE + 1))
            pool.wait_ge(s_xst, NE + 1)
            n_ovf = pool.value_load(novf[0:1, 0:1].bitcast(I32), min_val=0, max_val=NOVF)
            with pool.Fori(0, NOVF) as j:
                with pool.If(n_ovf > j):
                    nc.gpsimd.tensor_copy(idxg_cur[0].bitcast(I32), col(idx_gather, j + NE).bitcast(I32)).then_inc(g_idx, 1)
                    nc.gpsimd.tensor_copy(idxs_cur[0].bitcast(I32), col(idx_scatter, j + NE).bitcast(I32)).then_inc(g_idx, 1)
                    nc.gpsimd.tensor_copy(w_cur[0], col(wtab, j + NE)).then_inc(g_idx, 1)
                    pool.wait_ge(g_idx, 3 * j + 3)
                    passed()
                    gather(0, g_gath)
                    pool.wait_ge(g_gath, 16 * j + 16)
                    pool.wait_ge(g_dve, 3 * j + 3)
                    passed()
                    scatter(0, g_scat)
                    pool.wait_ge(g_scat, 16 * j + 16)
                    passed()
            pool.sem_inc(s_moe, 1)
            for t in range(NT):
                pool.wait_ge(s_3s, t + 1)
                pool.wait_ge(s_3n, t)
                rstd(r1, ss1, 1.0 / D, s_3r, t + 1)

        @block.scalar
        def _(act):
            def square_sum(src, junk, out, signal):
                nc.scalar.activation(junk, src, ACT.Square, accum_out=out).then_inc(signal, 1)

            def junk_of(v, n):
                return v.bitcast(BF16)[:, 0:n]

            def x_square(t):
                act.wait_ge(s_x[t % 2], 16 * (t // 2 + 1))
                square_sum(xb[t % 2], junk_of(qT, D), ssx[:, t:t + 1], s_ss)

            def x_hi(n, half, b):
                act.wait_ge(s_xt, 2 * n + half + 1)
                nc.scalar.activation(ahl[:, n % 2, 0, half * C:(half + 1) * C], bank(b), ACT.Copy).then_inc(s_xh, 1)

            x_square(0)
            mixer_hi(act, 0)
            mixer_hi(act, 1)
            act.wait_ge(s_stt, 1)
            nc.scalar.activation(uT[:, :, U_SAMPLE:U_SAMPLE + HALO], ps[:, 7, 0:KC * 32].rearrange("p (c n) -> p c n", c=KC)[:, :, 0:HALO],
                                 ACT.Copy).then_inc(s_stt, 1)
            nc.scalar.activation(kcache[0:HD, :], ps[0:HD, 7, P:P + NKV * P], ACT.Copy).then_inc(s_stt, 1)
            nc.scalar.activation(convw.rearrange("p c j -> p (c j)"), ps[:, 7, 3 * P:4 * P], ACT.Copy).then_inc(s_stt, 1)
            x_hi(0, 0, 0)
            x_hi(0, 1, 1)
            x_square(1)
            mixer_hi(act, 2)
            mixer_hi(act, 3)
            for t in range(NT):
                if t + 2 < NT:
                    x_square(t + 2)
                if t + 1 < NT:
                    x_hi(t + 1, 0, 0)
                    x_hi(t + 1, 1, 1)
                if t == NT - 1:
                    for h in range(2):
                        x_hi(NT, h, 0)
                zb = 2 + 2 * (t % 2)
                act.wait_ge(s_z, t + 1)
                if t >= 1:
                    act.wait_ge(s_u, t)
                nc.scalar.activation(pT[:, 0:C], bank(zb + 1), ACT.Tanh, scale=0.5).then_inc(s_th, 1)
                act.wait_ge(s_ut, t + 1)
                at = HALO + t * P if t < TS else U_SAMPLE + HALO
                nc.scalar.activation(uT[:, :, at:at + rows_of(t)],
                                     bank(6).rearrange("p (c n) -> p c n", c=KC)[:, :, 0:rows_of(t)],
                                     ACT.Copy, scale=0.5).then_inc(s_uT, 1)
                if t >= TS - 1:
                    side = t - (TS - 1)
                    act.wait_ge(s_u, t + 1)
                    nc.scalar.activation(S[:, side * C:(side + 1) * C], u2, ACT.Copy, scale=0.5).then_inc(s_uout, 1)

            for j in range(J_QKV, J_OUT):
                mixer_hi(act, j)

            def square_qk(t):
                act.wait_ge(s_z, NT + t + 1)
                if t >= 1:
                    act.wait_ge(s_qkt, t)
                if t == TS:
                    act.wait_ge(s_kv, 16 * 4)
                nc.scalar.activation(qkn[:, 0:QW + KVW], banks2(2)[:, 0:QW + KVW], ACT.Square).then_inc(s_sq, 1)
                nc.scalar.activation(vb[:, t % 3, :], banks2(2)[:, QW + KVW:GLU0], ACT.Copy).then_inc(s_v, 1)

            def exps(t, hf):
                act.wait_ge(s_nm, 2 * t + hf + 1)
                lo = P if t == 0 else 0
                nc.scalar.activation(esink[:, 4 * hf:4 * hf + 4], msink[:, 4 * hf:4 * hf + 4], ACT.Exp).then_inc(s_ex, 1)
                for i in range(4):
                    h = 4 * hf + i
                    s = S.rearrange("p (h k) -> p h k", h=4)[:, i, lo:2 * P]
                    nc.scalar.activation(s, s, ACT.Exp, bias=negm[:, h:h + 1], accum_out=den[:, h:h + 1]).then_inc(s_ex, 1)

            def pt_copy(t, hf):
                act.wait_ge(s_pt, 2 * t + hf + 1)
                lo = P if t == 0 else 0
                act_out = pT.rearrange("p (h k) -> p h k", h=4)[:, :, lo:2 * P]
                nc.scalar.activation(act_out, banks2(4).rearrange("p (h k) -> p h k", h=4)[:, :, lo:2 * P], ACT.Copy).then_inc(s_pT, 1)

            square_qk(0)
            for t in range(NT + 1):
                if t >= 1:
                    exps(t - 1, 1)
                if t + 1 < NT:
                    x_hi(NT + t + 1, 0, 0)
                if t < NT:
                    act.wait_ge(s_qkt, t + 1)
                    nc.scalar.activation(qT[0:HD, :], banks2(4)[0:HD, :], ACT.Copy).then_inc(s_qT, 1)
                    src = ps[0:HD, 6, 0:NKV * P].rearrange("p (g k) -> p g k", g=NKV)
                    nc.scalar.activation(kTb[0:HD, t % 2, :, P:2 * P], src, ACT.Copy).then_inc(s_kT, 1)
                    if t < TS - 1:
                        nc.scalar.activation(kTb[0:HD, (t + 1) % 2, :, 0:P], src, ACT.Copy).then_inc(s_kT, 1)
                    if t == TS - 1:
                        nc.scalar.activation(kTb[0:HD, (t + 1) % 2, :, 0:P], kcache[0:HD, :].rearrange("p (g k) -> p g k", g=NKV),
                                             ACT.Copy).then_inc(s_kT, 1)
                if t + 1 < NT:
                    x_hi(NT + t + 1, 1, 0)
                if t >= 1:
                    pt_copy(t - 1, 1)
                    act.wait_ge(s_oe, t)
                    act.wait_ge(s_ors, t - 1)
                    square_sum(R[:, t - 1, 0:QW], junk_of(u2, QW), ss1, s_osq)
                if t < NT:
                    exps(t, 0)
                if t + 1 < NT:
                    square_qk(t + 1)
                if t < NT:
                    pt_copy(t, 0)

            for j in range(J_OUT, SPLIT_JOBS - 1):
                mixer_hi(act, j)
            for t in range(NT + 1):
                if t < NT:
                    act.wait_ge(s_cg, t + 1)
                    if t >= 2:
                        act.wait_ge(s_c2t, t - 1)
                    nc.scalar.activation(c2[t % 2], c1[t % 2], ACT.Tanh, scale=0.5).then_inc(s_cth, 1)
                if t >= 1:
                    q = t - 1
                    act.wait_ge(s_c2t, q + 1)
                    nc.scalar.activation(ahl[:, q % 2, 0, 0:C], bank(2 + q % 2), ACT.Copy, scale=0.5).then_inc(s_ch, 1)
                    act.wait_ge(s_c3, q + 1)
                    act.wait_ge(s_c3r, q)
                    square_sum(R[:, q, C:2 * C], junk_of(hT, C), ss1, s_c3s)
            mixer_hi(act, SPLIT_JOBS - 1)
            for h in range(2):
                x_hi(2 * NT, h, h)
            for t in range(NT + 1):
                if t + 1 < NT:
                    for h in range(2):
                        x_hi(2 * NT + t + 1, h, h)
                if t < NT:
                    act.wait_ge(s_x1, t + 1)
                    if t >= 1:
                        act.wait_ge(s_hr, t)
                    square_sum(R[:, t, :], junk_of(gcn, D), ss1, s_hs)
                if t >= 1:
                    for h in range(2):
                        act.wait_ge(s_ht, 2 * (t - 1) + h + 1)
                        if t >= 2 and h == 0:
                            act.wait_ge(s_rl, t - 1)
                        nc.scalar.activation(hT[:, h * C:(h + 1) * C], bank(6), ACT.Copy).then_inc(s_hT, 1)
            act.wait_ge(s_rta, 1)
            nc.scalar.activation(eqc, dc, ACT.Exp).then_inc(s_rta, 1)
            act.wait_ge(s_rta, 3)
            nc.scalar.activation(e2, mt, ACT.Exp).then_inc(s_rta, 1)

            def expert_hi(J, slot, c, arrived, used):
                act.wait_ge(s_mraw[c], arrived)
                if used is not None:
                    act.wait_ge(s_use, used)
                nc.scalar.activation(whl[:, 0, slot * CH:(slot + 1) * CH], raw[c], ACT.Copy).then_inc(s_mhi, 1)

            def slots_hi(b, count):
                act.wait_ge(s_xst, count)
                nc.scalar.activation(ahl[:, b, 0, :], banks2(0), ACT.Copy).then_inc(s_xsh, 1)

            act.wait_ge(s_w, NT)
            for c in range(4):
                expert_hi(c, c, c, 16, None)
            slots_hi(0, 1)
            for signal in (s_y0, s_mth):
                act.sem_inc(signal, 1)
            with act.Fori(0, NE, 2) as e0:
                for b in range(2):
                    e = e0 + b
                    for c in (4, 5):
                        expert_hi(None, (6 * b + c) % 4, c, 16 * e + 16, 6 * e + (c - 3))
                    act.wait_ge(s_use, 6 * e + 2)
                    act.wait_ge(s_mht, e + 1)
                    nc.scalar.activation(th, bank(2), ACT.Tanh, scale=0.5).then_inc(s_mth, 1)
                    expert_hi(None, (6 * b + 6) % 4, 0, 16 * e + 32, 6 * e + 3)
                    slots_hi(1 - b, e + 2)
                    act.wait_ge(s_mht, e + 2)
                    nc.scalar.activation(hhl[:, 0, :], bank(4), ACT.Copy).then_inc(s_hh, 1)
                    for c in (1, 2, 3):
                        expert_hi(None, (6 * b + 6 + c) % 4, c, 16 * e + 32, 6 * e + 3 + c)
                    act.wait_ge(s_use, 6 * e + 6)
                    act.wait_ge(s_sc_d, 16 * e + 16)
                    act.wait_ge(s_idx, 3 * e + 3)
                    nc.scalar.activation(y[:, 0:C], bank(5), ACT.Copy, scale=w_cur[b]).then_inc(s_y0, 1)
            act.wait_ge(s_tab, 1)
            n_ovf = act.value_load(novf[0:1, 0:1].bitcast(I32), min_val=0, max_val=NOVF)
            with act.Fori(0, NOVF) as j:
                with act.If(n_ovf > j):
                    act.wait_ge(g_pe, 2 * j + 1)
                    nc.scalar.activation(xs[1], banks2(0), ACT.Copy).then_inc(g_act, 1)
                    act.wait_ge(g_use, 6 * j + 3)
                    nc.scalar.activation(th, bank(2), ACT.Tanh, scale=0.5).then_inc(g_act, 1)
                    act.wait_ge(g_pe, 2 * j + 2)
                    nc.scalar.activation(xs[0][:, 0:DE], bank(4), ACT.Copy).then_inc(g_act, 1)
            act.wait_ge(s_moe, 1)

            def ple_tanh(t):
                act.wait_ge(s_3g, t + 1)
                act.wait_ge(s_3f, t)
                nc.scalar.activation(tg, banks2(2), ACT.Tanh, scale=0.5).then_inc(s_3th, 1)

            for t in range(NT):
                act.wait_ge(s_x2, t + 1)
                act.wait_ge(s_3r, t)
                square_sum(R[:, t, :], junk_of(xs[1], D), ss1, s_3s)
                for h in range(2):
                    act.wait_ge(s_3t, 2 * t + h + 1)
                    nc.scalar.activation(ahl[:, t % 2, 0, h * C:(h + 1) * C], bank(h), ACT.Copy).then_inc(s_3h, 1)
                if t >= 1:
                    ple_tanh(t - 1)
                    act.wait_ge(s_3p, t)
                act.wait_ge(s_3pt, t + 1)
                nc.scalar.activation(pT3, bank(6, PLE), ACT.Copy).then_inc(s_3pT, 1)
            ple_tanh(NT - 1)

        @block.vector
        def _(dve):
            def chain(ins):
                link(dve, "dve", ins)

            conv = conv_ops(dve)
            done = [0]

            def convs(n):
                for _ in range(n):
                    if done[0] < CONV_OPS:
                        next(conv)
                        done[0] += 1

            def dve_chunk(j):
                mixer_lo(dve, nc.vector, s_wlv, j, 0, lo_cut(j))

            def x_norm(n):
                dve.wait_ge(s_x[n % 2], 16 * (n // 2 + 1))
                if n < NT:
                    dve.wait_ge(s_rs, n + 1)
                if n == 0:
                    dve.wait_ge(s_gm, 16)
                t = n % NT
                nc.vector.scalar_tensor_tensor(xb[n % 2], xb[n % 2], rsx[:, t:t + 1], gmix, ALU.mult, ALU.mult).then_inc(s_xn, 1)

            def x_lo(n, half, b):
                dve.wait_ge(s_xh, 2 * n + half + 1)
                at = slice(half * C, (half + 1) * C)
                lo_part(nc.vector, ahl[:, n % 2, 1, at], ahl[:, n % 2, 0, at], bank(b)).then_inc(s_xl, 1)

            def ev(t):
                zb = 2 + 2 * (t % 2)
                dve.wait_ge(s_th, t + 1)
                if t >= 1:
                    dve.wait_ge(s_ut, t)
                if t == TS:
                    dve.wait_ge(s_uout, 1)
                nc.vector.scalar_tensor_tensor(u2, pT[:, 0:C], 1.0, bank(zb), ALU.add, ALU.mult).then_inc(s_u, 1)

            x_norm(0)
            dve.wait_ge(s_const, 1)
            chain(nc.vector.scalar_tensor_tensor(bias[:, 0, :], bias[:, 0, :], -1.0, bias[:, 0, :], ALU.mult, ALU.min))
            for h in range(NH - 1, -1, -1):
                chain(nc.vector.tensor_scalar(bias[:, h, :], bias[:, 0, :], 2.0 ** (-8.0 * (h + 1) / NH), None, ALU.mult))
            chain(nc.vector.memset(bias[0:64, :, 192:256], NEG))
            chain(nc.vector.memset(bias[64:128, :, 0:64], NEG))
            dve_chunk(0)
            dve_chunk(1)
            x_lo(0, 0, 0)
            x_lo(0, 1, 1)
            x_norm(1)
            dve_chunk(2)
            dve_chunk(3)
            for t in range(NT):
                n = t + 1
                if t + 1 < NT:
                    x_lo(n, 0, 0)
                    x_lo(n, 1, 1)
                else:
                    x_lo(n, 0, 0)
                    x_lo(n, 1, 0)
                x_norm(t + 2)
                ev(t)
                if t >= 4:
                    convs(12)
            for j in range(J_QKV, J_OUT):
                dve_chunk(j)

            def qk_norm(t):
                dve.wait_ge(s_sq, t + 1)
                nc.vector.tensor_reduce(ss10, qkn[:, 0:QW + KVW].rearrange("p (h d) -> p h d", d=HD), AX.X, ALU.add).then_inc(s_ssq, 1)
                convs(2)
                dve.wait_ge(s_r10, t + 1)
                dve.wait_ge(s_v, t + 1)
                nc.vector.tensor_tensor(qkn[:, 0:QW + KVW].rearrange("p (h d) -> p h d", d=HD),
                                        banks2(2)[:, 0:QW + KVW].rearrange("p (h d) -> p h d", d=HD),
                                        r10.unsqueeze(2).broadcast_to([P, NH + NKV, HD]), ALU.mult).then_inc(s_zev, 1)
                dve.wait_ge(s_zev, t + 1)
                nc.vector.tensor_tensor(qkn[:, 0:QW + KVW], qkn[:, 0:QW + KVW], gqk, ALU.mult).then_inc(s_qkn, 1)

            def biased(t, hf):
                lo = P if t == 0 else 0
                if t == 0 and hf == 0:
                    dve.wait_ge(s_uo, 16 * 2)
                dve.wait_ge(s_sc, 2 * t + hf + 1)
                if 2 * t + hf > 0:
                    dve.wait_ge(s_pt, 2 * t + hf)
                hs = slice(4 * hf, 4 * hf + 4)
                s = S.rearrange("p (h k) -> p h k", h=4)[:, :, lo:2 * P]
                nc.vector.scalar_tensor_tensor(s, banks2(6).rearrange("p (h k) -> p h k", h=4)[:, :, lo:2 * P],
                                               HD ** -0.5, bias[:, hs, lo:2 * P], ALU.mult, ALU.add).then_inc(s_sb, 1)
                dve.wait_ge(s_sb, 2 * t + hf + 1)
                chain(nc.vector.tensor_reduce(mx[:, hs], s, AX.X, ALU.max))
                chain(nc.vector.tensor_tensor(mx[:, hs], mx[:, hs], sink[:, hs], ALU.max))
                chain(nc.vector.tensor_tensor(msink[:, hs], sink[:, hs], mx[:, hs], ALU.subtract))
                nc.vector.tensor_scalar(negm[:, hs], mx[:, hs], -1.0, None, ALU.mult).then_inc(s_nm, 1)

            def attention_out(t):
                dve.wait_ge(s_ex, 10 * t + 10)
                chain(nc.vector.tensor_tensor(den, den, esink, ALU.add))
                chain(nc.vector.reciprocal(rden, den))
                dve.wait_ge(s_pv, 2 * t + 2)
                nc.vector.tensor_tensor(R[:, t, 0:QW].rearrange("p (h d) -> p h d", d=HD),
                                        bank(1).rearrange("p (h d) -> p h d", d=HD),
                                        rden.unsqueeze(2).broadcast_to([P, NH, HD]), ALU.mult).then_inc(s_oe, 1)

            def attention_norm(t):
                dve.wait_ge(s_ors, t + 1)
                dve.wait_ge(s_oe, t + 1)
                nc.vector.scalar_tensor_tensor(R[:, t, 0:QW], R[:, t, 0:QW], r1, goa, ALU.mult, ALU.mult).then_inc(s_o, 1)

            dve.wait_ge(s_ld, 16 * LOADS)
            qk_norm(0)
            for t in range(NT + 1):
                if t >= 1:
                    biased(t - 1, 1)
                    convs(3)
                if t + 1 < NT:
                    x_lo(NT + t + 1, 0, 0)
                    x_lo(NT + t + 1, 1, 0)
                if t + 2 < NT:
                    x_norm(NT + t + 2)
                if t >= 1:
                    attention_out(t - 1)
                    convs(3)
                if t < NT:
                    biased(t, 0)
                    convs(4)
                if t >= 1:
                    attention_norm(t - 1)
                if t + 1 < NT:
                    qk_norm(t + 1)
            convs(CONV_OPS)
            for j in range(J_OUT, SPLIT_JOBS - 1):
                dve_chunk(j)
            dve.wait_ge(s_ld2, 16 * 5)
            for t in range(NT + 2):
                if t < NT:
                    dve.wait_ge(s_ct, t + 1)
                    chain(nc.vector.bn_stats(bnst, bank(t % 2)))
                    nc.vector.bn_aggr(bnag, bnst).then_inc(s_bn, 1)
                    dve.wait_ge(s_crs, t + 1)
                    dve.wait_ge(s_bn, t + 1)
                    if t >= 2:
                        dve.wait_ge(s_c2, t - 1)
                    nc.vector.tensor_scalar(c1[t % 2], bank(t % 2), bnag[:, 0:1], r10[:, 0:1], ALU.subtract, ALU.mult).then_inc(s_cn, 1)
                if 1 <= t <= NT:
                    q = t - 1
                    dve.wait_ge(s_cth, q + 1)
                    nc.vector.scalar_tensor_tensor(c2[q % 2], c2[q % 2], 1.0, c1[q % 2], ALU.add, ALU.mult).then_inc(s_c2, 1)
                    dve.wait_ge(s_ch, q + 1)
                    nc.vector.scalar_tensor_tensor(ahl[:, q % 2, 1, 0:C], bank(2 + q % 2), 0.5, ahl[:, q % 2, 0, 0:C].bitcast(F32),
                                                   ALU.mult, ALU.subtract).then_inc(s_cl, 1)
                    dve.wait_ge(s_pw, q + 1)
                    nc.vector.tensor_tensor(R[:, q, C:2 * C], bank(4 + q % 2), bpw, ALU.add).then_inc(s_c3, 1)
                if t >= 2:
                    q = t - 2
                    dve.wait_ge(s_c3r, q + 1)
                    nc.vector.scalar_tensor_tensor(R[:, q, C:2 * C], R[:, q, C:2 * C], r1, goc, ALU.mult, ALU.mult).then_inc(s_c4, 1)
            dve_chunk(SPLIT_JOBS - 1)
            for h in range(2):
                x_lo(2 * NT, h, h)
            for t in range(NT + 1):
                if t + 1 < NT:
                    for h in range(2):
                        x_lo(2 * NT + t + 1, h, h)
                if t < NT:
                    dve.wait_ge(s_w, t + 1)
                    dve.wait_ge(s_x[t % 2], 16 * ((2 * NT + t) // 2 + 1))
                    nc.vector.tensor_tensor(R[:, t, :], banks2(2 + 2 * (t % 2)), xb[t % 2], ALU.add).then_inc(s_x1, 1)
                    dve.wait_ge(s_hr, t + 1)
                    if t >= 2:
                        dve.wait_ge(s_hst[t % 2], 16 * (t // 2))
                        dve.wait_ge(s_ht, 2 * (t - 1))
                    dve.wait_ge(s_x1, t + 1)
                    nc.vector.scalar_tensor_tensor(hb[t % 2], R[:, t, :], r1, gffn, ALU.mult, ALU.mult).then_inc(s_h, 1)
                if t >= 1:
                    dve.wait_ge(s_rl, t)
                    nc.vector.tensor_tensor(lg[:, t - 1, :], bank(7, NR), rbias, ALU.add).then_inc(s_lg, 1)

            def r3(v, n):
                return v.rearrange("p (t n) -> p t n", n=n)

            def over(v, n):
                return v.unsqueeze(2).broadcast_to([P, v.shape[1], n])

            def rowof(v, t):
                return v.unsqueeze(1).broadcast_to([P, t, v.shape[1]])

            tt = nc.vector.tensor_tensor
            red = nc.vector.tensor_reduce
            dve.wait_ge(s_lg, NT)
            dve.wait_ge(s_const, 7)
            dve.wait_ge(s_hst[0], 16 * 5)
            dve.wait_ge(s_hst[1], 16 * 4)
            lc, lf = lg[:, :, 0:NG], lg[:, :, NG:NR]
            chain(red(gmx, lc, AX.X, ALU.max))
            chain(tt(r3(dc, NG), lc, over(gmx, NG), ALU.subtract))
            dve.sem_inc(s_rta, 1)
            chain(nc.vector.tensor_scalar(og, dc, 0.0, None, ALU.is_ge))
            chain(tt(r3(og, NG), r3(og, NG), rowof(rev8[:, 4:8], NT), ALU.mult))
            chain(red(mt, r3(og, NG), AX.X, ALU.max))
            chain(tt(r3(og, NG), r3(og, NG), over(mt, NG), ALU.is_equal))
            for g in range(NG):
                pick = over(r3(og, NG)[:, :, g], EPG)
                chain(tt(r3(prod, NE)[:, :, g * EPG:(g + 1) * EPG], lf[:, :, g * EPG:(g + 1) * EPG], pick, ALU.mult))
            chain(red(r3(lsel, EPG), prod.rearrange("p (t g e) -> p t e g", t=NT, g=NG), AX.X, ALU.add))

            def best(m, one):
                chain(red(m, r3(lsel, EPG), AX.X, ALU.max))
                chain(tt(r3(eqf, EPG), r3(lsel, EPG), over(m, EPG), ALU.is_equal))
                chain(tt(r3(eqf, EPG), r3(eqf, EPG), rowof(rev8, NT), ALU.mult))
                chain(red(mt, r3(eqf, EPG), AX.X, ALU.max))
                chain(tt(r3(one, EPG), r3(eqf, EPG), over(mt, EPG), ALU.is_equal))

            best(m1, o1)
            chain(nc.vector.scalar_tensor_tensor(lsel, o1, -3e38, lsel, ALU.mult, ALU.add))
            best(m2, o2)
            chain(tt(mt, m2, m1, ALU.subtract))
            dve.wait_ge(s_rta, 2)
            dve.sem_inc(s_rta, 1)
            chain(red(se, r3(eqc, NG), AX.X, ALU.add))
            for g in range(NG):
                pick = over(r3(og, NG)[:, :, g], EPG)
                chain(tt(r3(A1, NE)[:, :, g * EPG:(g + 1) * EPG], r3(o1, EPG), pick, ALU.mult))
                chain(tt(r3(A2, NE)[:, :, g * EPG:(g + 1) * EPG], r3(o2, EPG), pick, ALU.mult))
            chain(nc.vector.memset(A1[SAMPLE:P, TS * NE:NT * NE], 0.0))
            chain(nc.vector.memset(A2[SAMPLE:P, TS * NE:NT * NE], 0.0))
            chain(nc.vector.memset(A12[:, NT * NE:(NT + 1) * NE], 0.0))
            nc.vector.tensor_tensor(A12[:, 0:NT * NE], A1, A2, ALU.add).then_inc(s_rt, 1)
            dve.wait_ge(s_rta, 4)
            chain(nc.vector.scalar_tensor_tensor(rw, e2, 1.0, se, ALU.add, ALU.mult))
            chain(nc.vector.reciprocal(rw, rw))
            chain(nc.vector.tensor_scalar(wk[0], rw, 0.5, None, ALU.mult))
            chain(tt(wk[1], wk[0], e2, ALU.mult))
            chain(nc.vector.memset(idmask, 1.0))
            chain(nc.vector.memset(idmask[SAMPLE:P, TS:NT], 0.0))
            for k in range(2):
                chain(tt(wk[k], wk[k], idmask, ALU.mult))
            chain(tt(idk[0], idk[0], idmask, ALU.mult))
            chain(nc.vector.scalar_tensor_tensor(idk[1], idmask, float(TOKENS), idk[0], ALU.mult, ALU.add))
            dve.wait_ge(s_rtp, 1)
            chain(nc.vector.tensor_copy(pos, bank(0, (NT + 1) * NE)))
            cnt = pos[:, NT * NE:(NT + 1) * NE]
            chain(tt(r3(ovf8, 8), over(cnt, 8), rowof(thr8, NE), ALU.is_gt))
            chain(red(ovf, r3(ovf8, 8), AX.X, ALU.add))
            chain(tt(r3(lt, NE), over(iota[:, 0:NE], NE), rowof(iota[:, 0:NE], NE), ALU.is_gt))
            chain(tt(r3(lt, NE), r3(lt, NE), rowof(ovf, NE), ALU.mult))
            chain(red(start, r3(lt, NE), AX.X, ALU.add))
            chain(tt(end, start, ovf, ALU.add))
            for k, A in enumerate((A1, A2)):
                for dst, row in ((pk[k], pos[:, 0:NT * NE]), (ek[k], None), (stk[k], None)):
                    other = r3(row, NE) if row is not None else rowof(iota[:, 0:NE] if dst is ek[k] else start, NT)
                    chain(tt(r3(prod, NE), r3(A, NE), other, ALU.mult))
                    chain(red(dst, r3(prod, NE), AX.X, ALU.add))
                chain(tt(r3(cmp9, 8), over(pk[k], 8), rowof(thr8, NT), ALU.is_ge))
                chain(red(bk[k], r3(cmp9, 8), AX.X, ALU.add))
                chain(nc.vector.scalar_tensor_tensor(sk[k], bk[k], -float(P), pk[k], ALU.mult, ALU.add))
                chain(tt(stk[k], stk[k], bk[k], ALU.add))
                chain(tt(stk[k], stk[k], ek[k], ALU.subtract))
                chain(nc.vector.tensor_scalar(bk[k], bk[k], 0.0, None, ALU.is_gt))
                chain(nc.vector.scalar_tensor_tensor(vk[k], stk[k], float(NE - 1), bk[k], ALU.add, ALU.mult))
                chain(tt(vk[k], vk[k], ek[k], ALU.add))
                if k == 1:
                    dve.wait_ge(s_rtp, 2)
                chain(tt(r3(Ph, P), rowof(iota, NT), over(sk[k], P), ALU.is_equal))
                chain(tt(r3(oh, NBLK), rowof(iota[:, 0:NBLK], NT), over(vk[k], NBLK), ALU.is_equal))
                Vv = V.rearrange("p (t c v) -> p t c v", t=NT, c=2)
                chain(tt(Vv[:, :, 0, :], r3(oh, NBLK), over(idk[k], NBLK), ALU.mult))
                nc.vector.tensor_tensor(Vv[:, :, 1, :], r3(oh, NBLK), over(wk[k], NBLK), ALU.mult).then_inc(s_rt, 1)
            j16 = over(iota[:, 0:NOVF], NE)
            chain(tt(r3(eb, NE), rowof(start, NOVF), j16, ALU.is_le))
            chain(tt(r3(lt[:, 0:NOVF * NE], NE), rowof(end, NOVF), j16, ALU.is_gt))
            chain(tt(eb, eb, lt[:, 0:NOVF * NE], ALU.mult))
            chain(tt(r3(eb, NE), r3(eb, NE), rowof(iota[:, 0:NE], NOVF), ALU.mult))
            chain(red(tmp48[:, 0:NOVF], r3(eb, NE), AX.X, ALU.add))
            chain(nc.vector.tensor_copy(ebk.bitcast(I32), tmp48[:, 0:NOVF]))
            chain(nc.vector.tensor_copy(novf.bitcast(I32), end[:, NE - 1:NE]))
            dve.wait_ge(s_rtp, 3)
            chain(nc.vector.tensor_copy(tab, bank(2, 2 * NBLK)))
            ids, wts = tab[:, 0:NBLK], tab[:, NBLK:2 * NBLK]
            chain(nc.vector.tensor_copy(wtab, wts))
            chain(nc.vector.tensor_scalar(tmp48, ids, 0.0, 4096.0, ALU.is_equal, ALU.mult))
            chain(nc.vector.scalar_tensor_tensor(tmp48, ids, -1.0, tmp48, ALU.add, ALU.add))
            chain(nc.vector.tensor_copy(idx_scatter.bitcast(I32), tmp48))
            chain(nc.vector.tensor_scalar(tmp48, ids, float(TOKENS), -float(TOKENS), ALU.is_gt, ALU.mult))
            chain(nc.vector.scalar_tensor_tensor(tmp48, ids, -1.0, tmp48, ALU.add, ALU.add))
            chain(nc.vector.tensor_scalar(tmp48, tmp48, 0.0, None, ALU.max))
            nc.vector.tensor_copy(idx_gather.bitcast(I32), tmp48).then_inc(s_tab, 1)

            def expert_lo(J, slot, c):
                dve.wait_ge(s_mhi, J + 1)
                lo_part(nc.vector, whl[:, 1, slot * CH:slot * CH + LOV], whl[:, 0, slot * CH:slot * CH + LOV],
                        raw[c][:, 0:LOV]).then_inc(s_mlv, 1)

            def slots_lo(b, count):
                dve.wait_ge(s_xsh, count)
                lo_part(nc.vector, ahl[:, b, 1, :], ahl[:, b, 0, :], banks2(0)).then_inc(s_xsl, 1)

            for c in range(4):
                expert_lo(c, c, c)
            slots_lo(0, 1)
            for signal in (s_mg, s_mh, s_hl, s_y1):
                dve.sem_inc(signal, 1)
            with dve.Fori(0, NE, 2) as e0:
                for b in range(2):
                    e = e0 + b
                    for c in (4, 5):
                        expert_lo(6 * e + c, (6 * b + c) % 4, c)
                    dve.wait_ge(s_mth, e + 2)
                    nc.vector.scalar_tensor_tensor(th, th, 1.0, bank(2), ALU.add, ALU.mult).then_inc(s_mg, 1)
                    expert_lo(6 * e + 6, (6 * b + 6) % 4, 0)
                    dve.wait_ge(s_use, 6 * e + 4)
                    dve.wait_ge(s_mg, e + 2)
                    nc.vector.tensor_tensor(th, th, bank(3), ALU.mult).then_inc(s_mh, 1)
                    slots_lo(1 - b, e + 2)
                    dve.wait_ge(s_hh, e + 1)
                    lo_part(nc.vector, hhl[:, 1, :], hhl[:, 0, :], bank(4)).then_inc(s_hl, 1)
                    for c in (1, 2, 3):
                        expert_lo(6 * e + 6 + c, (6 * b + 6 + c) % 4, c)
                    dve.wait_ge(s_use, 6 * e + 6)
                    dve.wait_ge(s_sc_d, 16 * e + 16)
                    dve.wait_ge(s_idx, 3 * e + 3)
                    nc.vector.tensor_scalar(y[:, C:2 * C], bank(6), w_cur[b], None, ALU.mult).then_inc(s_y1, 1)
            n_ovf = dve.value_load(novf[0:1, 0:1].bitcast(I32), min_val=0, max_val=NOVF)
            with dve.Fori(0, NOVF) as j:
                with dve.If(n_ovf > j):
                    dve.wait_ge(g_act, 3 * j + 2)
                    dve.wait_ge(g_use, 6 * j + 3)
                    nc.vector.scalar_tensor_tensor(th, th, 1.0, bank(2), ALU.add, ALU.mult).then_inc(g_dve, 1)
                    dve.wait_ge(g_dve, 3 * j + 1)
                    dve.wait_ge(g_use, 6 * j + 5)
                    nc.vector.tensor_tensor(th, th, bank(3), ALU.mult).then_inc(g_dve, 1)
                    dve.wait_ge(g_use, 6 * j + 7)
                    dve.wait_ge(g_idx, 3 * j + 3)
                    nc.vector.tensor_scalar(y, banks2(5), w_cur[0], None, ALU.mult).then_inc(g_dve, 1)
            dve.wait_ge(s_gp, 16 * 2)
            for t in range(NT + 1):
                b = t % 2
                if t < NT:
                    dve.wait_ge(s_y[b], 32 * (t // 2 + 1))
                    chain(tt(R[:, t, :], R[:, t, :], yb[b][0], ALU.add))
                    nc.vector.tensor_tensor(R[:, t, :], R[:, t, :], yb[b][1], ALU.add).then_inc(s_x2, 1)
                    dve.wait_ge(s_3r, t + 1)
                    dve.wait_ge(s_x2, t + 1)
                    if t >= 2:
                        dve.wait_ge(s_3t, 2 * (t - 1))
                    nc.vector.scalar_tensor_tensor(xn3[b], R[:, t, :], r1, gple, ALU.mult, ALU.mult).then_inc(s_3n, 1)
                    for h in range(2):
                        dve.wait_ge(s_3h, 2 * t + h + 1)
                        at = slice(h * C, (h + 1) * C)
                        lo_part(nc.vector, ahl[:, b, 1, at], ahl[:, b, 0, at], bank(h)).then_inc(s_3l, 1)
                if t >= 1:
                    q = t - 1
                    dve.wait_ge(s_3th, q + 1)
                    dve.wait_ge(s_3p, q + 1)
                    nc.vector.scalar_tensor_tensor(tg, tg, 1.0, banks2(4), ALU.add, ALU.mult).then_inc(s_3m, 1)
                    dve.wait_ge(s_3m, q + 1)
                    if q >= 2:
                        dve.wait_ge(s_out[q % 2], 16 * (q // 2))
                    nc.vector.scalar_tensor_tensor(fin[q % 2], tg, 0.5, R[:, q, :], ALU.mult, ALU.add).then_inc(s_3f, 1)

        @block.tensor
        def _(pe):
            def transposes(n, half, src, b, free=None):
                for i in range(4):
                    k = 4 * half + i
                    last = nc.tensor.transpose(ps[:, b, i * P:(i + 1) * P], src[:, k * P:(k + 1) * P], ident)
                return last

            def x_transpose(n, half, b, src, ready):
                pe.wait_ge(*ready)
                pe.wait_ge(s_xl, 2 * n + half if n >= NT else max(0, 2 * n + half - 1))
                transposes(n, half, src, b).then_inc(s_xt, 1)

            pe.wait_ge(s_id, 1)
            pe.wait_ge(s_st, 16 * 4)
            for c in range(KC):
                nc.tensor.transpose(ps[:, 7, c * 32:c * 32 + HALO], S[0:HALO, c * P:(c + 1) * P], ident[0:HALO, 0:HALO])
                nc.tensor.transpose(ps[:, 7, 3 * P + c * 32:3 * P + (c + 1) * 32], u2[0:32, c * P:(c + 1) * P], ident[0:32, 0:32])
            for g in range(NKV):
                last = nc.tensor.transpose(ps[0:HD, 7, (1 + g) * P:(2 + g) * P], S[:, C + g * HD:C + (g + 1) * HD], ident)
            last.then_inc(s_stt, 1)
            for h in range(2):
                x_transpose(0, h, h, xb[0], (s_xn, 1))
            for t in range(NT):
                if t + 1 < NT:
                    for h in range(2):
                        x_transpose(t + 1, h, h, xb[(t + 1) % 2], (s_xn, t + 2))
                else:
                    for h in range(2):
                        x_transpose(NT, h, 0, xb[NT % 2], (s_xn, NT + 1))
                zb = 2 + 2 * (t % 2)
                if t >= 2:
                    pe.wait_ge(s_u, t - 1)
                for k in range(KD):
                    if t == 0 and k % 2 == 0:
                        weights_ready(pe, k // 2)
                    if k % 4 == 0:
                        pe.wait_ge(s_xl, 2 * t + k // 4 + 1)
                    hi, lo = act_tile(t % 2, k)
                    for n in range(2):
                        last = split_product(bank(zb + n), hi, lo, slice(k * D + n * C, k * D + (n + 1) * C), k == 0, k == KD - 1)
                last.then_inc(s_z, 1)
                pe.wait_ge(s_u, t + 1)
                if t >= 1:
                    pe.wait_ge(s_uT, t)
                transposes(t, 0, u2, 6).then_inc(s_ut, 1)

            def qkv(t, half):
                n = NT + t
                if half == 0:
                    if t == 0:
                        pe.wait_ge(s_u, NT)
                    else:
                        pe.wait_ge(s_zev, t)
                        pe.wait_ge(s_v, t)
                pe.wait_ge(s_xl, 2 * n + half + 1)
                for k in range(4 * half, 4 * half + 4):
                    if t == 0 and k % 2 == 0:
                        weights_ready(pe, J_QKV + k // 2)
                    hi, lo = act_tile(n % 2, k)
                    for c0, c1_ in ((0, QW), (QW, GLU0)):
                        last = split_product(banks2(2)[:, c0:c1_], hi, lo, slice(k * GLU0 + c0, k * GLU0 + c1_), k == 0, k == KD - 1)
                if half == 1:
                    last.then_inc(s_z, 1)

            def score(t, hf):
                pe.wait_ge(s_kT, 2 * t + 2 if t < TS else 2 * t + 1)
                pe.wait_ge(s_qT, t + 1)
                if 2 * t + hf > 0:
                    pe.wait_ge(s_sb, 2 * t + hf)
                lo = P if t == 0 else 0
                for i in range(4):
                    h = 4 * hf + i
                    last = nc.tensor.matmul(banks2(6)[:, i * 2 * P + lo:(i + 1) * 2 * P], qT[0:HD, h * P:(h + 1) * P],
                                            kTb[0:HD, t % 2, hf, lo:2 * P], start=True, stop=True)
                last.then_inc(s_sc, 1)

            def prob_transpose(t, hf):
                pe.wait_ge(s_ex, 10 * t + 5 * hf + 5)
                pe.wait_ge(s_qT, min(t + hf + 1, NT))
                if 2 * t + hf > 0:
                    pe.wait_ge(s_pT, 2 * t + hf)
                for i in range(4):
                    for s in range(1 if t == 0 else 0, 2):
                        at = (2 * i + s) * P
                        last = nc.tensor.transpose(banks2(4)[:, at:at + P], S[:, at:at + P], ident)
                last.then_inc(s_pt, 1)

            def attend(t, hf):
                pe.wait_ge(s_pT, 2 * t + hf + 1)
                pe.wait_ge(s_v, t + 1)
                if t == TS:
                    pe.wait_ge(s_cv, 16)
                if hf == 0 and t >= 1:
                    pe.wait_ge(s_oe, t)
                before = 3 if t == TS else (t - 1) % 3
                for i in range(4):
                    h = 4 * hf + i
                    for s in range(1 if t == 0 else 0, 2):
                        slot = t % 3 if s else before
                        last = nc.tensor.matmul(bank(1)[:, h * HD:(h + 1) * HD], pT[:, (2 * i + s) * P:(2 * i + s + 1) * P],
                                                vb[:, slot, hf * HD:(hf + 1) * HD],
                                                start=(s == 0 or t == 0), stop=(s == 1))
                last.then_inc(s_pv, 1)

            qkv(0, 0)
            qkv(0, 1)
            for t in range(NT + 1):
                if t + 1 < NT:
                    x_transpose(NT + t + 1, 0, 0, xb[(NT + t + 1) % 2], (s_xn, NT + t + 2))
                if t < NT:
                    pe.wait_ge(s_qkn, t + 1)
                    if t >= 1:
                        pe.wait_ge(s_pT, 2 * t - 1)
                        pe.wait_ge(s_sb, 2 * t)
                    for h in range(NH):
                        nc.tensor.transpose(banks2(4)[0:HD, h * P:(h + 1) * P], qkn[:, h * HD:(h + 1) * HD], ident)
                    for g in range(NKV):
                        last = nc.tensor.transpose(ps[0:HD, 6, g * P:(g + 1) * P], qkn[:, QW + g * HD:QW + (g + 1) * HD], ident)
                    last.then_inc(s_qkt, 1)
                if t + 1 < NT:
                    x_transpose(NT + t + 1, 1, 0, xb[(NT + t + 1) % 2], (s_xn, NT + t + 2))
                    qkv(t + 1, 0)
                if t >= 1:
                    prob_transpose(t - 1, 1)
                    attend(t - 1, 1)
                if t < NT:
                    score(t, 0)
                if t + 1 < NT:
                    qkv(t + 1, 1)
                if t < NT:
                    score(t, 1)
                    prob_transpose(t, 0)
                    attend(t, 0)

            pe.wait_ge(s_oe, NT)
            weights_ready(pe, J_PW)
            for t in range(NT + 2):
                if t < NT:
                    if t == 0:
                        pe.wait_ge(s_conv, CONV_OPS)
                    if t >= 2:
                        pe.wait_ge(s_cn, t - 1)
                    for c in range(KC):
                        last = nc.tensor.transpose(bank(t % 2)[:, c * P:(c + 1) * P], R[:, t, C + c * P:C + (c + 1) * P], ident)
                    last.then_inc(s_ct, 1)
                if 1 <= t <= NT:
                    q = t - 1
                    pe.wait_ge(s_c2, q + 1)
                    if q >= 2:
                        pe.wait_ge(s_cl, q - 1)
                    transposes(q, 0, c2[q % 2], 2 + q % 2).then_inc(s_c2t, 1)
                    pe.wait_ge(s_cl, q + 1)
                    if q >= 2:
                        pe.wait_ge(s_c3, q - 1)
                    for k in range(KC):
                        hi, lo = act_tile(q % 2, k)
                        last = split_product(bank(4 + q % 2), hi, lo, slice(PW0 + k * C, PW0 + (k + 1) * C), k == 0, k == KC - 1)
                    last.then_inc(s_pw, 1)

            pe.wait_ge(s_cn, NT)
            pe.wait_ge(s_c3, NT)
            pe.wait_ge(s_o, NT)
            for h in range(2):
                pe.wait_ge(s_c4, 1)
                transposes(0, h, R[:, 0, :], h).then_inc(s_xt, 1)
            for t in range(NT + 1):
                n = 2 * NT + t + 1
                if t + 1 < NT:
                    pe.wait_ge(s_c4, t + 2)
                    for h in range(2):
                        pe.wait_ge(s_xl, 2 * n - 1 + h)
                        transposes(0, h, R[:, t + 1, :], h).then_inc(s_xt, 1)
                if t < NT:
                    zb = 2 + 2 * (t % 2)
                    if t >= 2:
                        pe.wait_ge(s_x1, t - 1)
                    for k in range(KD):
                        if t == 0 and k % 2 == 0:
                            weights_ready(pe, J_OUT + k // 2)
                        if k % 4 == 0:
                            pe.wait_ge(s_xl, 2 * (n - 1) + k // 4 + 1)
                        hi, lo = act_tile((n - 1) % 2, k)
                        for i in range(2):
                            last = split_product(bank(zb + i), hi, lo, slice(k * D + i * C, k * D + (i + 1) * C), k == 0, k == KD - 1)
                    last.then_inc(s_w, 1)
                if t >= 1:
                    q = t - 1
                    pe.wait_ge(s_h, q + 1)
                    for h in range(2):
                        if 2 * q + h > 0:
                            pe.wait_ge(s_hT, 2 * q + h)
                        transposes(0, h, hb[q % 2], 6).then_inc(s_ht, 1)
                    pe.wait_ge(s_hT, 2 * q + 2)
                    if q >= 1:
                        pe.wait_ge(s_lg, q)
                    for k in range(KD):
                        last = nc.tensor.matmul(bank(7, NR), hT[:, k * P:(k + 1) * P], wr[:, k, :], start=(k == 0), stop=(k == KD - 1))
                    last.then_inc(s_rl, 1)

            pe.wait_ge(s_ld, 16 * LOADS)
            pe.wait_ge(s_rt, 1)
            pe.wait_ge(s_const, 7)
            nc.tensor.matmul(bank(0, NE), tri, A12[:, 0:NE], start=True, stop=True)
            nc.tensor.matmul(ps[:, 0, NE:(NT + 1) * NE], tri, A12[:, NE:(NT + 1) * NE], start=True, stop=False)
            for t in range(NT - 1, -1, -1):
                later = A12[:, t * NE:(t + 1) * NE].unsqueeze(1).broadcast_to([P, NT - t, NE])
                last = nc.tensor.matmul(ps[:, 0, (t + 1) * NE:(NT + 1) * NE].rearrange("p (t n) -> p t n", n=NE), ones, later,
                                        start=False, stop=(t == 0), skip_group_check=(t > 0))
            last.then_inc(s_rtp, 1)
            for k in range(2):
                pe.wait_ge(s_rt, 2 + k)
                for t in range(NT):
                    last = nc.tensor.matmul(bank(2, 2 * NBLK), Ph[:, t * P:(t + 1) * P], V[:, t * 2 * NBLK:(t + 1) * 2 * NBLK],
                                            start=(k == 0 and t == 0), stop=(k == 1 and t == NT - 1))
                last.then_inc(s_rtp, 1)

            def slot_transpose(b, gathered, evacuated):
                pe.wait_ge(s_g[b], gathered)
                if evacuated is not None:
                    pe.wait_ge(s_xsl, evacuated)
                transposes(0, 0, xs[b], 0)
                transposes(0, 1, xs[b], 1).then_inc(s_xst, 1)

            def expert_product(J, slot, blocks):
                pe.wait_ge(s_mlv, J + 1)
                pe.wait_ge(s_mlp, J + 1)
                for i, (b, hi, lo, first, last) in enumerate(blocks):
                    ins = split_product(bank(b), hi, lo, slice(slot * CH + i * C, slot * CH + (i + 1) * C), first, last)
                return ins

            pe.wait_ge(s_tab, 1)
            slot_transpose(0, 16, None)
            pe.sem_inc(s_mht, 1)
            with pe.Fori(0, NE, 2) as e0:
                for b in range(2):
                    e = e0 + b
                    slot = lambda c: (6 * b + c) % 4
                    pe.wait_ge(s_xsl, e + 1)
                    pe.wait_ge(s_mg, e + 1)
                    for c in (0, 1):
                        expert_product(6 * e + c, slot(c), [(2, *act_tile(b, 4 * c + i), c + i == 0, c == 1 and i == 3) for i in range(4)]
                                       ).then_inc(s_use, 1)
                    pe.wait_ge(s_mh, e + 1)
                    for c in (2, 3):
                        expert_product(6 * e + c, slot(c), [(3, *act_tile(b, 4 * (c - 2) + i), c + i == 2, c == 3 and i == 3) for i in range(4)]
                                       ).then_inc(s_use, 1)
                    slot_transpose(1 - b, 8 * e0 + 16 * (1 + b), e + 1)
                    pe.wait_ge(s_mh, e + 2)
                    pe.wait_ge(s_hl, e + 1)
                    transposes(0, 0, th, 4).then_inc(s_mht, 1)
                    pe.wait_ge(s_hl, e + 2)
                    pe.wait_ge(s_y0, e + 1)
                    pe.wait_ge(s_y1, e + 1)
                    for c in (4, 5):
                        blocks = []
                        for i in range(4):
                            k = 2 * (c - 4) + i // 2
                            at = slice(k * P, (k + 1) * P)
                            blocks.append((5 + i % 2, hhl[:, 0, at], hhl[:, 1, at], k == 0, k == KE - 1))
                        expert_product(6 * e + c, slot(c), blocks).then_inc(s_use, 1)
            n_ovf = pe.value_load(novf[0:1, 0:1].bitcast(I32), min_val=0, max_val=NOVF)
            pe.sem_inc(g_use, 1)
            with pe.Fori(0, NOVF) as j:
                with pe.If(n_ovf > j):
                    pe.wait_ge(g_gath, 16 * j + 16)
                    transposes(0, 0, xs[0], 0)
                    transposes(0, 1, xs[0], 1).then_inc(g_pe, 1)
                    pe.wait_ge(g_act, 3 * j + 1)
                    for c in range(4):
                        pe.wait_ge(g_raw, 96 * j + 16 * (c + 1))
                        for i in range(4):
                            k = 4 * (c % 2) + i
                            last = nc.tensor.matmul(bank(2 + c // 2), xs[1][:, k * P:(k + 1) * P], graw[:, i * C:(i + 1) * C],
                                                    start=(k == 0), stop=(k == KD - 1))
                        last.then_inc(g_use, 1)
                    pe.wait_ge(g_dve, 3 * j + 2)
                    transposes(0, 0, th, 4).then_inc(g_pe, 1)
                    pe.wait_ge(g_act, 3 * j + 3)
                    for c in range(2):
                        pe.wait_ge(g_raw, 96 * j + 16 * (c + 5))
                        for i in range(4):
                            k = 2 * c + i // 2
                            last = nc.tensor.matmul(bank(5 + i % 2), xs[0][:, k * P:(k + 1) * P], graw[:, i * C:(i + 1) * C],
                                                    start=(k == 0), stop=(k == KE - 1))
                        last.then_inc(g_use, 1)

            def x2_transpose(t):
                pe.wait_ge(s_3n, t + 1)
                for h in range(2):
                    if t >= 1:
                        pe.wait_ge(s_3l, 2 * t + h - 1)
                    transposes(0, h, xn3[t % 2], h).then_inc(s_3t, 1)
                pe.wait_ge(s_p[t % 2], 16 * (t // 2 + 1))
                pe.wait_ge(s_3pT, t)
                for k in range(PLE // P):
                    last = nc.tensor.transpose(ps[:, 6, k * P:(k + 1) * P], pin[t % 2][:, k * P:(k + 1) * P], ident)
                last.then_inc(s_3pt, 1)

            pe.wait_ge(s_moe, 1)
            pe.wait_ge(s_gp, 16 * 2)
            x2_transpose(0)
            for t in range(NT):
                if t + 1 < NT:
                    x2_transpose(t + 1)
                pe.wait_ge(s_3th, t)
                for k in range(KD):
                    if t == 0 and k % 2 == 0:
                        pe.wait_ge(s_mlv, 6 * NE + k // 2 + 1)
                        pe.wait_ge(s_mlp, 6 * NE + k // 2 + 1)
                    if k % 4 == 0:
                        pe.wait_ge(s_3l, 2 * t + k // 4 + 1)
                    hi, lo = act_tile(t % 2, k)
                    for i in range(2):
                        last = split_product(bank(2 + i), hi, lo, slice(k * D + i * C, k * D + (i + 1) * C), k == 0, k == KD - 1)
                last.then_inc(s_3g, 1)
                pe.wait_ge(s_3pT, t + 1)
                pe.wait_ge(s_3m, t)
                for k in range(PLE // P):
                    for i in range(2):
                        last = nc.tensor.matmul(bank(4 + i), pT3[:, k * P:(k + 1) * P], wproj[:, k * D + i * C:k * D + (i + 1) * C],
                                                start=(k == 0), stop=(k == PLE // P - 1))
                last.then_inc(s_3p, 1)


_INS = ['x_prompt', 'x_sample', 'p_prompt', 'p_sample', 'cache_k', 'cache_v', 'state_conv', 'g_mix', 'w_in', 'g_q', 'g_k',
        'sinks', 'w_dw', 'b_dw', 'g_cn', 'b_cn', 'w_pw', 'b_pw', 'g_oa', 'g_oc', 'w_out', 'g_ffn', 'w_coarse', 'b_coarse',
        'w_fine', 'b_fine', 'w_e_gate', 'w_e_up', 'w_e_down', 'g_ple', 'w_ple_gate', 'w_ple_proj']
_OUTS = [('y_prompt', (1, SEQ, D)), ('y_sample', (1, SAMPLE, D)),
         ('new_k_prompt', (1, 1, P, NKV, HD)), ('new_v_prompt', (1, 1, P, NKV, HD)), ('new_conv_prompt', (1, 1, HALO, C)),
         ('new_k_sample', (1, 1, P, NKV, HD)), ('new_v_sample', (1, 1, P, NKV, HD)), ('new_conv_sample', (1, 1, HALO, C))]


def kernel(**inputs):
    import numpy as _np
    import concourse.bacc as _bacc
    from concourse import mybir as _mybir
    from concourse.bass_utils import run_bass_kernel_spmd as _run

    nc = _bacc.Bacc("TRN2", target_bir_lowering=False, num_devices=1)
    arrays, ins, outs = {}, {}, {}
    for name in _INS:
        arr = _np.ascontiguousarray(inputs[name])
        arrays[f"in_{name}"] = arr
        ins[name] = nc.dram_tensor(f"in_{name}", arr.shape, _mybir.dt.from_np(arr.dtype), kind="ExternalInput").ap()
    for name, shape in _OUTS:
        outs[name] = nc.dram_tensor(f"out_{name}", shape, F32, kind="ExternalOutput").ap()
    build_step(nc, ins, outs)
    r = _run(nc, [arrays], core_ids=[0])
    return tuple(r.results[0][f"out_{name}"] for name, _ in _OUTS)
```

```python
from contextlib import ExitStack

import concourse.bass as bass
from concourse import mybir

ALU = mybir.AluOpType
ACT = mybir.ActivationFunctionType
AX = mybir.AxisListType
F32 = mybir.dt.float32
F32R = mybir.dt.float32r
BF16 = mybir.dt.bfloat16
I32 = mybir.dt.int32

P = 128
D = 1024
SEQ, SAMPLE = 1024, 64
TOKENS = SEQ + SAMPLE
NT = SEQ // P + 1
TS = NT - 1
KD = D // P
HD = 64
NH, NKV = 8, 2
QW, KVW = NH * HD, NKV * HD
C = 512
KC = C // P
TAPS = 31
HALO = TAPS - 1
DE = 512
KE = DE // P
NG, EPG = 4, 8
NE = NG * EPG
NR = NG + NE
NOVF = (2 * TOKENS) // (P + 1)
NBLK = NE + NOVF
PLE = 256
EPS = 1e-6
NEG = -1e30
CH = 2048
LOV = 1280
CROWS = TAPS + 3
SPANS = ((0, 4), (4, 4), (8, 1))
UW = HALO + SEQ + HALO + SAMPLE
U_SAMPLE = HALO + SEQ
SPLIT_JOBS = 13


def rows_of(t):
    return P if t < TS else SAMPLE


def build_step(nc, a, o):
    ctx = ExitStack()
    with ctx:
        def sem(name):
            return ctx.enter_context(nc.semaphore(name))

        CONST, B_SIZE = 1524, 8576
        RAW_MOE = 6 * CH
        mem = ctx.enter_context(nc.sbuf_tensor("mem", [P, CONST + NT * D + RAW_MOE + B_SIZE], F32))
        whl = ctx.enter_context(nc.sbuf_tensor("whl", [P, 2, 4 * CH], F32R))
        ahl = ctx.enter_context(nc.sbuf_tensor("ahl", [P, 2, 2, D], F32R))
        hhl = ctx.enter_context(nc.sbuf_tensor("hhl", [P, 2, DE], F32R))
        ps = ctx.enter_context(nc.psum_tensor("ps", [P, 8, 512], F32))

        top = [0]

        def take(n):
            v = mem[:, top[0]:top[0] + n]
            top[0] += n
            return v

        def bank(b, n=512):
            return ps[:, b, 0:n]

        def banks2(b):
            return ps[:, b:b + 2, :].rearrange("p b n -> p (b n)")

        ident = take(P)
        convw = take(KC * CROWS).rearrange("p (c j) -> p c j", c=KC)
        lnh = take(KC * 2).rearrange("p (c j) -> p c j", c=KC)
        kcache = take(NKV * P)
        wr = take(KD * NR).rearrange("p (k r) -> p k r", k=KD)
        rbias = take(NR)
        lg = take(NT * NR).rearrange("p (t r) -> p t r", t=NT)
        idx_gather = take(NBLK)
        idx_scatter = take(NBLK)
        wtab = take(NBLK)
        ebk = take(NOVF)
        novf = take(1)
        idxg_cur = [take(1) for _ in range(2)]
        idxs_cur = [take(1) for _ in range(2)]
        w_cur = [take(1) for _ in range(2)]
        neghalf = take(12)
        ssx, rsx = take(NT), take(NT)
        ms = take(12)
        ss10, r10 = take(10), take(10)
        sink = take(NH)
        negm, msink = take(NH), take(NH)
        esink = [take(NH), take(NH)]
        mx = take(NH)
        den, rden = [take(NH), take(NH)], take(NH)
        ss1, r1 = take(1), take(1)
        assert top[0] <= CONST, top[0]
        top[0] = CONST
        R = take(NT * D).rearrange("p (t n) -> p t n", t=NT)
        A0 = top[0]
        raw1 = [take(CH) for _ in range(2)]
        uT = take(KC * UW).rearrange("p (c n) -> p c n", c=KC)
        S = take(4 * 2 * P)
        qT = take(NH * P)
        pT = take(D)
        u2 = take(C)
        assert top[0] <= A0 + RAW_MOE, top[0] - A0
        raw = [mem[:, A0 + CH * i:A0 + CH * (i + 1)] for i in range(6)]
        B0 = top[0] = A0 + RAW_MOE
        xb = [take(D) for _ in range(2)]
        gmix = take(D)
        gqk = take(QW + KVW)
        bias = take(NH * 2 * P).rearrange("p (h k) -> p h k", h=NH)
        kTb = take(2 * NKV * 2 * P).rearrange("p (b g k) -> p b g k", b=2, g=NKV)
        vb = take(4 * KVW).rearrange("p (s n) -> p s n", s=4)
        qkn = take(QW + 2 * KVW)
        goa = take(C)
        assert top[0] <= B0 + B_SIZE, top[0] - B0
        top[0] = B0 + 2 * D
        scr = take(2 * C)
        bpw, goc = take(C), take(C)
        gffn = take(D)
        hb = [take(D) for _ in range(2)]
        hT = take(D)
        junk3 = take(C // 2)
        assert top[0] <= B0 + B_SIZE
        hb2 = mem[:, B0 + 2 * D + 4 * C + D:B0 + 2 * D + 4 * C + D + 4 * C]
        c_sq = [hb2, raw[4], hT[:, 0:C]]
        c_th = [raw[5], hb2, hT[:, 0:C]]
        c_rs = [scr[:, P:P + C], hT[:, C:2 * C], scr[:, P + C:2 * P + C]]
        c_ones = scr[:, 0:P]
        ones = kcache[:, 0:P]
        top[0] = B0
        iota = take(P)
        rev8, thr8 = take(8), take(8)
        tri = take(P)
        dc, eqc, og = take(NT * NG), take(NT * NG), take(NT * NG)
        gmx, se, m1, m2, mt, e2, rw = (take(NT) for _ in range(7))
        eqf, o1, o2 = (take(NT * EPG) for _ in range(3))
        A1, A2 = take(NT * NE), take(NT * NE)
        A12 = take((NT + 1) * NE // 2).bitcast(BF16)
        tri16 = take(P // 2).bitcast(BF16)
        ones16 = take(P // 2).bitcast(BF16)
        pos = take((NT + 1) * NE)
        prod = take(NT * NE)
        lt = take(NE * NE)
        ovf8 = take(NE * 8)
        ovf, start, end, rel = take(NE), take(NE), take(NE), take(NE)
        pk, ek, stk, bk, sk, vk, wk, idk = ([take(NT), take(NT)] for _ in range(8))
        cmp9 = take(NT * 8)
        oh = take(NT * NBLK)
        V = take(NT * 2 * NBLK)
        Ph = take(NT * P)
        tmp48 = take(NBLK)
        eb = take(NOVF * NE)
        idmask = take(NT)
        tab = take(2 * NBLK)
        lsel = take(NT * EPG)
        assert top[0] - NT * EPG >= B0 + 2 * D
        assert top[0] <= B0 + B_SIZE, top[0] - B0
        top[0] = B0
        xs = [take(D) for _ in range(2)]
        th = take(DE)
        y = take(D)
        graw = take(CH)
        wproj = take(CH)
        assert top[0] <= B0 + B_SIZE
        top[0] = A0
        yb = [[take(D) for _ in range(2)] for _ in range(3)]
        xn3 = [take(D) for _ in range(2)]
        fin = [take(D) for _ in range(2)]
        assert top[0] <= A0 + RAW_MOE
        gple = xs[0]
        tg = [y, graw[:, 0:D]]
        pT3 = [graw[:, D:D + PLE], graw[:, D + PLE:D + 2 * PLE]]
        pin = [graw[:, D + 2 * PLE:D + 3 * PLE], graw[:, D + 3 * PLE:D + 4 * PLE]]

        H = nc.dram_tensor("h_rows", (TOKENS, D), F32).ap()
        Y = nc.dram_tensor("y_rows", (2 * TOKENS, D), F32).ap()

        s_id = sem("identity_made")
        s_const = sem("constants_made")
        s_ld = sem("small_inputs_in")
        s_ld2 = sem("late_gains_in")
        s_st = sem("conv_state_in")
        s_gm = sem("mixer_gain_then_ple_gain_in")
        s_uo = sem("conv_state_out")
        s_cv = sem("cache_v_in")
        s_x = [sem("x_in_0"), sem("x_in_1")]
        s_raw = [sem(f"chunk_in_{i}") for i in range(5)]
        s_whi = sem("weights_hi")
        s_wlv = sem("weights_lo_vector")
        s_wlp = sem("weights_lo_pool")
        s_ss = sem("sum_squares_x")
        s_rs = sem("rstd_x")
        s_xs = sem("x_scaled")
        s_xn = sem("x_normed")
        s_xnp = sem("x_normed_by_pool")
        s_xt = sem("x_transposed")
        s_xh = sem("x_hi")
        s_xl = sem("x_lo")
        s_z = sem("projected")
        s_th = sem("glu_tanh")
        s_u = sem("glu_out")
        s_ut = sem("glu_transposed")
        s_uT = sem("glu_in_conv_buffer")
        s_stt = sem("state_transposed")
        s_uout = sem("glu_rows_out")
        s_conv = sem("conv_ops")
        s_zero = sem("conv_pad_zero")
        s_sq = sem("qk_squared")
        s_v = sem("v_copied")
        s_ssq = sem("qk_sums")
        s_r10 = sem("qk_rstd")
        s_zev = sem("qk_scaled")
        s_qkn = sem("qk_normed")
        s_qkt = sem("qk_transposed")
        s_qT = sem("qT_ready")
        s_kT = sem("kT_ready")
        s_sc = sem("scores")
        s_sb = sem("scores_biased")
        s_nm = sem("neg_max")
        s_ex = sem("exps")
        s_pt = sem("probs_transposed")
        s_pT = sem("pT_ready")
        s_pv = sem("attended")
        s_oe = sem("attention_out")
        s_osq = sem("attention_sum_squares")
        s_ors = sem("attention_rstd")
        s_o = sem("attention_normed")
        s_convs = sem("sample_conv_done")
        s_ones = sem("ones_made")
        s_cs = sem("conv_sums")
        s_c1 = sem("conv_centred")
        s_cq = sem("conv_squared")
        s_ca = sem("conv_squares_added")
        s_cvv = sem("conv_square_sums")
        s_cve = sem("conv_variance")
        s_crs = sem("conv_rstd")
        s_cdg = sem("conv_rstd_diagonal")
        s_cbc = sem("conv_rstd_spread")
        s_cn = sem("conv_scaled")
        s_cth = sem("conv_tanh")
        s_cy = sem("conv_half_normed")
        s_c2 = sem("conv_swished")
        s_ch = sem("swish_hi")
        s_cl = sem("swish_lo")
        s_zk = sem("last_glu_products")
        s_pw = sem("pointwise")
        s_c3 = sem("pointwise_biased")
        s_c3s = sem("pointwise_sum_squares")
        s_c3r = sem("pointwise_rstd")
        s_c4 = sem("pointwise_normed")
        s_w = sem("mixed")
        s_x1 = sem("mixer_residual")
        s_hs = sem("h_sum_squares")
        s_hr = sem("h_rstd")
        s_h = sem("h_ready")
        s_hst = [sem("h_rows_out_0"), sem("h_rows_out_1")]
        s_ht = sem("h_transposed")
        s_hT = sem("hT_ready")
        s_rl = sem("router_products")
        s_lg = sem("router_logits")
        s_rt = sem("routing_step")
        s_rta = sem("routing_exps")
        s_rtp = sem("routing_products")
        s_tab = sem("slot_table_ready")
        s_mraw = [sem(f"expert_chunk_in_{c}") for c in range(6)]
        s_mhi = sem("expert_hi")
        s_mlv = sem("expert_lo_vector")
        s_mlp = sem("expert_lo_pool")
        s_use = sem("expert_chunk_used")
        s_g = [sem("gathered_0"), sem("gathered_1")]
        s_idx = sem("slot_indices")
        s_idx0 = sem("first_indices")
        s_xst = sem("slots_transposed")
        s_xsh = sem("slots_hi")
        s_xsl = sem("slots_lo")
        s_mth = sem("expert_tanh")
        s_mg = sem("expert_gated")
        s_mh = sem("expert_hidden")
        s_mht = sem("hidden_transposed")
        s_hh = sem("hidden_hi")
        s_hl = sem("hidden_lo")
        s_y0 = sem("expert_out_left")
        s_y1 = sem("expert_out_right")
        s_sc_d = sem("scattered")
        s_moe = sem("experts_done")
        s_go = sem("pool_passed")
        g_idx, g_gath, g_use = sem("ovf_indices"), sem("ovf_gathered"), sem("ovf_chunk_used")
        g_raw = [sem(f"ovf_chunk_in_{i}") for i in range(3)]
        g_pe, g_act, g_dve, g_scat = sem("ovf_pe"), sem("ovf_act"), sem("ovf_vector"), sem("ovf_scattered")
        s_y = [sem(f"y_in_{i}") for i in range(3)]
        s_p = [sem("p_in_0"), sem("p_in_1")]
        s_gp = sem("w_ple_proj_in")
        s_x2 = sem("moe_residual")
        s_3s = sem("x2_sum_squares")
        s_3r = sem("x2_rstd")
        s_3n = sem("x2_normed")
        s_3t = sem("x2_transposed")
        s_3h = sem("x2_hi")
        s_3l = sem("x2_lo")
        s_3g = sem("ple_gate_products")
        s_3th = sem("ple_tanh")
        s_3pt = sem("p_transposed")
        s_3pT = sem("pT3_ready")
        s_3p = sem("ple_proj_products")
        s_3m = sem("ple_gated")
        s_3f = sem("y_ready")
        s_out = [sem("y_out_0"), sem("y_out_1")]
        s_kv = sem("cache_rows_out")
        chains = {e: sem(f"chain_{e}") for e in ("pool", "act", "dve")}
        chain_at = dict.fromkeys(chains, 0)

        def link(eng, name, ins):
            chain_at[name] += 1
            ins.then_inc(chains[name], 1)
            eng.wait_ge(chains[name], chain_at[name])

        w_in = a["w_in"][0].rearrange("(k p) n -> p k n", p=P)
        w_pw = a["w_pw"][0].rearrange("(k p) n -> p k n", p=P)
        w_out = a["w_out"][0].rearrange("(k p) n -> p k n", p=P)
        GLU0 = QW + 2 * KVW
        PW0 = KD * GLU0
        mixer_chunks = (
            [(w_in[:, 2 * i:2 * i + 2, GLU0:], 2 * i * D) for i in range(4)]
            + [(w_in[:, 2 * i:2 * i + 2, 0:GLU0], 2 * i * GLU0) for i in range(4)]
            + [(w_pw, PW0)]
            + [(w_out[:, 2 * i:2 * i + 2, :], 2 * i * D) for i in range(4)])
        J_QKV, J_PW, J_OUT = 4, 8, 9

        def chunk_size(j):
            return 2 * GLU0 if J_QKV <= j < J_PW else CH

        def lo_cut(j):
            return 2 * C if J_QKV <= j < J_PW else LOV

        def chunk_buffer(j):
            if J_QKV <= j < J_QKV + 3:
                i = j - J_QKV
                return R[:, 3 * i:3 * i + 3, 0:C], s_raw[2 + i], 4
            i = j % 2 if j < J_QKV else (j + 1) % 2
            return raw1[i][:, 0:chunk_size(j)].rearrange("p (a n) -> p a n", n=C), s_raw[i], j // 2 + 1 if j < J_QKV else 3 + (j - 7) // 2

        def region_free(eng, j):
            if J_QKV <= j < J_OUT:
                eng.wait_ge(s_zk, ((mixer_chunks[j][1] + chunk_size(j) - 1) // CH) + 1)
            elif j >= J_OUT:
                eng.wait_ge(s_z, 2 * NT)
                if j == SPLIT_JOBS - 1:
                    eng.wait_ge(s_pw, NT)

        def mixer_hi(eng, j):
            buffer, signal, count = chunk_buffer(j)
            eng.wait_ge(signal, 16 * count)
            region_free(eng, j)
            n, at = chunk_size(j), mixer_chunks[j][1]
            nc.scalar.activation(whl[:, 0, at:at + n].rearrange("p (a n) -> p a n", n=C), buffer, ACT.Copy).then_inc(s_whi, 1)

        def lo_part(which, out, hi, full):
            return which.tensor_tensor(out, full, hi.bitcast(F32), ALU.subtract)

        def mixer_lo(eng, which, signal, j, first, last):
            eng.wait_ge(s_whi, j + 1)
            at = mixer_chunks[j][1]
            if J_QKV <= j < J_QKV + 3:
                hi, lo = (whl[:, i, at + first:at + last].rearrange("p (a n) -> p a n", n=C) for i in range(2))
                lo_part(which, lo, hi, chunk_buffer(j)[0][:, first // C:last // C]).then_inc(signal, 1)
            else:
                i = j % 2 if j < J_QKV else (j + 1) % 2
                lo_part(which, whl[:, 1, at + first:at + last], whl[:, 0, at + first:at + last],
                        raw1[i][:, first:last]).then_inc(signal, 1)

        def weights_ready(eng, j):
            eng.wait_ge(s_wlv, j + 1)
            eng.wait_ge(s_wlp, j + 1)

        def split_product(out, act_hi, act_lo, w_at, first, last):
            nc.tensor.matmul(out, act_hi, whl[:, 0, w_at], start=first, stop=False)
            nc.tensor.matmul(out, act_hi, whl[:, 1, w_at], start=False, stop=False)
            return nc.tensor.matmul(out, act_lo, whl[:, 0, w_at], start=False, stop=last)

        def act_tile(buf, k):
            return ahl[:, buf, 0, k * P:(k + 1) * P], ahl[:, buf, 1, k * P:(k + 1) * P]

        def x_source(t):
            return a["x_prompt"][0, t * P:(t + 1) * P, :] if t < TS else a["x_sample"][0]

        def extra_blocks(eng, count, block_of):
            for j in range(2):
                with eng.If(count > j):
                    block_of(j)
            with eng.If(count > 2):
                with eng.Fori(2, NOVF) as j:
                    with eng.If(count > j):
                        block_of(j)

        def first_extra(j):
            return isinstance(j, int) and j == 0

        gbuf = [graw, raw[4], raw[5]]
        LOADS = NH + NKV + 2 + 1 + NG + 2

        CONV_PARTS = ((0, 2, KC - 1), (2, 2, KC - 1), (4, 4, KC - 1))
        CONV_OPS = sum(channels for _, _, channels in CONV_PARTS) * TAPS
        CONV_FIRST = 2 * (KC - 1) * TAPS
        POOL_STEPS = 5 * TAPS
        POOL_FIRST = 2 * TAPS
        TAPS_AT = KC * HALO + NKV * P

        def conv_ops(eng):
            n = 0
            for t0, nt, channels in CONV_PARTS:
                w, base = nt * P, t0 * P
                for j in range(TAPS):
                    for c in range(channels):
                        src = uT[:, c, base + j:base + j + w].rearrange("p (t n) -> p t n", n=P)
                        acc = R[:, t0:t0 + nt, C + c * P:C + (c + 1) * P]
                        if j == 0:
                            if c == 0:
                                eng.wait_ge(s_uT, t0 + nt)
                                eng.wait_ge(s_zero, 2)
                                eng.wait_ge(s_stt, 4)
                            ins = nc.vector.tensor_scalar(acc, src, convw[:, c, 0:1], convw[:, c, TAPS:TAPS + 1], ALU.mult, ALU.add)
                        else:
                            eng.wait_ge(s_conv, n - channels + 1)
                            ins = nc.vector.scalar_tensor_tensor(acc, src, convw[:, c, j:j + 1], acc, ALU.mult, ALU.add)
                        ins.then_inc(s_conv, 1)
                        n += 1
                        yield

        def span_view(i, c):
            t0, nt = SPANS[i]
            return R[:, t0:t0 + nt, C + c * P:C + (c + 1) * P]

        def by_tile(v, i):
            nt = SPANS[i][1]
            return v[:, 0:nt * P].rearrange("p (t n) -> p t n", n=P)

        def swish_at(i, c):
            return c // 2, slice((c % 2) * C, (c % 2) * C + SPANS[i][1] * P)

        block = ctx.enter_context(nc.Block())

        @block.sync
        def _(sp):
            def load_x(n):
                t = n % NT
                if n >= 2:
                    if n < 20:
                        sp.wait_ge(s_xt, 2 * n - 2)
                    else:
                        sp.wait_ge(s_x1, n - 19)
                sp.dma_start(xb[n % 2][0:rows_of(t), :], x_source(t)).then_inc(s_x[n % 2], 16)

            def load_chunk(j):
                buffer, signal, _ = chunk_buffer(j)
                before = {2: 0, 3: 1, 7: 2, 8: 3}.get(j, j - 2 if j >= J_OUT else None)
                if before is not None:
                    sp.wait_ge(s_wlv, before + 1)
                    sp.wait_ge(s_wlp, before + 1)
                source = mixer_chunks[j][0]
                if buffer.shape[1] * C == chunk_size(j) and J_QKV <= j < J_QKV + 3:
                    for k in range(2):
                        at = k * GLU0
                        sp.dma_start(buffer[:, k, 0:C] if k == 0 else buffer[:, 2, 0:C],
                                     source[:, k, 0:C] if k == 0 else source[:, 1, GLU0 - C:GLU0]).then_inc(signal, 16)
                        sp.dma_start(buffer[:, 1, 0:GLU0 - C] if k == 0 else buffer[:, 1, GLU0 - C:C],
                                     source[:, 0, C:GLU0] if k == 0 else source[:, 1, 0:GLU0 - C]).then_inc(signal, 16)
                else:
                    i = j % 2 if j < J_QKV else (j + 1) % 2
                    sp.dma_start(raw1[i][:, 0:chunk_size(j)].rearrange("p (k n) -> p k n", k=source.shape[1]), source).then_inc(signal, 16)

            load_x(0)
            sp.dma_start(gmix, a["g_mix"][0].partition_broadcast(P)).then_inc(s_gm, 16)
            load_chunk(0)
            load_x(1)
            load_chunk(1)
            sp.dma_start(S[0:HALO, 0:C], a["state_conv"][0, 0]).then_inc(s_st, 16)
            sp.dma_start(S[:, C:C + KVW], a["cache_k"][0, 0].rearrange("t g d -> t (g d)")).then_inc(s_st, 16)
            sp.dma_start(u2[0:TAPS, :], a["w_dw"][0]).then_inc(s_st, 16)
            for row, name in enumerate(("b_dw", "g_cn", "b_cn")):
                sp.dma_start(u2[TAPS + row:TAPS + row + 1, :], a[name]).then_inc(s_st, 16)
            for h in range(NH):
                sp.dma_start(gqk[:, h * HD:(h + 1) * HD], a["g_q"][0].partition_broadcast(P)).then_inc(s_ld, 16)
            for h in range(NKV):
                sp.dma_start(gqk[:, QW + h * HD:QW + (h + 1) * HD], a["g_k"][0].partition_broadcast(P)).then_inc(s_ld, 16)
            sp.dma_start(goa, a["g_oa"][0].partition_broadcast(P)).then_inc(s_ld, 16)
            sp.dma_start(sink, a["sinks"][0].partition_broadcast(P)).then_inc(s_ld, 16)
            sp.dma_start(wr[:, :, 0:NG], a["w_coarse"][0].rearrange("(k p) g -> p k g", p=P)).then_inc(s_ld, 16)
            for g in range(NG):
                sp.dma_start(wr[:, :, NG + g * EPG:NG + (g + 1) * EPG],
                             a["w_fine"][0, g].rearrange("(k p) e -> p k e", p=P)).then_inc(s_ld, 16)
            sp.dma_start(rbias[:, 0:NG], a["b_coarse"][0].partition_broadcast(P)).then_inc(s_ld, 16)
            sp.dma_start(rbias[:, NG:NR], a["b_fine"][0].rearrange("g e -> (g e)").partition_broadcast(P)).then_inc(s_ld, 16)
            load_chunk(2)
            load_chunk(3)
            sp.dma_start(vb[:, 3, :], a["cache_v"][0, 0].rearrange("t g d -> t (g d)")).then_inc(s_cv, 16)
            for n in range(2, 2 * NT):
                load_x(n)
                if 2 <= n < 7:
                    load_chunk(n + 2)
                if n == NT + 1:
                    load_chunk(9)
                if n == NT + 2:
                    sp.wait_ge(s_uout, 2)
                    sp.dma_start(o["new_conv_prompt"][0, 0], S[P - HALO:P, 0:C]).then_inc(s_uo, 16)
                    sp.dma_start(o["new_conv_sample"][0, 0], S[SAMPLE - HALO:SAMPLE, C:2 * C]).then_inc(s_uo, 16)
            kp, vp = (o[x][0, 0].rearrange("t g d -> t (g d)") for x in ("new_k_prompt", "new_v_prompt"))
            ks, vs = (o[x][0, 0].rearrange("t g d -> t (g d)") for x in ("new_k_sample", "new_v_sample"))
            ck, cv = (a[x][0, 0].rearrange("t g d -> t (g d)") for x in ("cache_k", "cache_v"))
            sp.dma_start(ks[0:P - SAMPLE], ck[SAMPLE:P]).then_inc(s_kv, 16)
            sp.dma_start(vs[0:P - SAMPLE], cv[SAMPLE:P]).then_inc(s_kv, 16)
            sp.wait_ge(s_qkn, TS)
            sp.wait_ge(s_v, TS)
            sp.dma_start(kp, qkn[:, QW:QW + KVW]).then_inc(s_kv, 16)
            sp.dma_start(vp, vb[:, (TS - 1) % 3, :]).then_inc(s_kv, 16)
            sp.wait_ge(s_qkn, NT)
            sp.wait_ge(s_v, NT)
            sp.dma_start(ks[P - SAMPLE:P], qkn[0:SAMPLE, QW:QW + KVW]).then_inc(s_kv, 16)
            sp.dma_start(vs[P - SAMPLE:P], vb[0:SAMPLE, TS % 3, :]).then_inc(s_kv, 16)
            load_x(2 * NT)
            load_x(2 * NT + 1)
            sp.wait_ge(s_o, NT)
            sp.wait_ge(s_kv, 16 * 6)
            for dst, name in ((bpw, "b_pw"), (goc, "g_oc"), (gffn, "g_ffn")):
                sp.dma_start(dst, a[name][0].partition_broadcast(P)).then_inc(s_ld2, 16)
            for j in range(10, SPLIT_JOBS):
                load_chunk(j)
            gate_v, up_v, down_v = (a[x][0] for x in ("w_e_gate", "w_e_up", "w_e_down"))

            def expert_chunk(e, c):
                w = (gate_v, gate_v, up_v, up_v, down_v, down_v)[c]
                w = w[e] if isinstance(e, int) else w[bass.ds(e, 1)].rearrange("e a b -> (e a) b")
                w = w.rearrange("(k p) n -> p k n", p=P)
                return w[:, 4 * (c % 2):4 * (c % 2) + 4, :] if c < 4 else w[:, 2 * (c % 2):2 * (c % 2) + 2, :]

            def raw_view(c):
                return raw[c].rearrange("p (k n) -> p k n", k=4 if c < 4 else 2)

            sp.wait_ge(s_conv, CONV_OPS)
            sp.wait_ge(s_convs, 2)
            for c in (2, 3):
                sp.dma_start(raw_view(c), expert_chunk(0, c)).then_inc(s_mraw[c], 16)
            sp.wait_ge(s_ch, 3 * KC)
            for c in (4, 5):
                sp.dma_start(raw_view(c), expert_chunk(0, c)).then_inc(s_mraw[c], 16)
            for n in range(2 * NT + 2, 3 * NT):
                load_x(n)
                t = n - 2 * NT - 2
                if t == 0:
                    for c in (0, 1):
                        sp.wait_ge(s_wlv, SPLIT_JOBS - c)
                        sp.wait_ge(s_wlp, SPLIT_JOBS - c)
                        sp.dma_start(raw_view(c), expert_chunk(0, c)).then_inc(s_mraw[c], 16)
                sp.wait_ge(s_h, t + 1)
                sp.dma_start(H[t * P:(t + 1) * P], hb[t % 2]).then_inc(s_hst[t % 2], 16)
            for t in (NT - 2, NT - 1):
                sp.wait_ge(s_h, t + 1)
                sp.dma_start(H[t * P:t * P + rows_of(t)], hb[t % 2][0:rows_of(t)]).then_inc(s_hst[t % 2], 16)
            with sp.Fori(1, NE) as e:
                for c in range(6):
                    sp.wait_ge(s_mlv, 6 * e + (c - 5))
                    sp.wait_ge(s_mlp, 6 * e + (c - 5))
                    sp.dma_start(raw_view(c), expert_chunk(e, c)).then_inc(s_mraw[c], 16)
            w_gate = a["w_ple_gate"][0].rearrange("(k p) n -> p k n", p=P)
            for c in range(4):
                sp.wait_ge(s_mlv, 6 * NE + c - 5)
                sp.wait_ge(s_mlp, 6 * NE + c - 5)
                sp.dma_start(raw[c].rearrange("p (k n) -> p k n", k=2), w_gate[:, 2 * c:2 * c + 2, :]).then_inc(s_mraw[c], 16)
            sp.dma_start(wproj.rearrange("p (k n) -> p k n", k=2), a["w_ple_proj"][0].rearrange("(k p) n -> p k n", p=P)).then_inc(s_gp, 16)
            sp.wait_ge(s_mlv, 6 * NE)
            sp.wait_ge(s_mlp, 6 * NE)
            sp.wait_ge(s_tab, 1)
            def ovf_block(j):
                e = sp.value_load((ebk[0:1, j:j + 1] if isinstance(j, int) else ebk[0:1, bass.ds(j, 1)]).bitcast(I32), min_val=0, max_val=NE - 1)
                for c in range(6):
                    sp.wait_ge(g_use, 6 * j + c + 1)
                    sp.dma_start(gbuf[c % 3].rearrange("p (k n) -> p k n", k=4 if c < 4 else 2), expert_chunk(e, c)).then_inc(g_raw[c % 3], 16)

            n_ovf = sp.value_load(novf[0:1, 0:1].bitcast(I32), min_val=0, max_val=NOVF)
            extra_blocks(sp, n_ovf, ovf_block)
            sp.wait_ge(s_moe, 1)
            sp.wait_ge(s_mlv, 6 * NE + 4)
            sp.wait_ge(s_mlp, 6 * NE + 4)

            def load_p(t):
                if t >= 2:
                    sp.wait_ge(s_3pt, t - 1)
                src = a["p_prompt"][0, 0, t * P:(t + 1) * P] if t < TS else a["p_sample"][0, 0]
                sp.dma_start(pin[t % 2][0:rows_of(t)], src).then_inc(s_p[t % 2], 16)

            for t in range(NT + 3):
                if t < NT:
                    r = rows_of(t)
                    if t >= 3:
                        sp.wait_ge(s_x2, t - 2)
                    if t == 0:
                        load_p(0)
                    for k in range(2):
                        sp.dma_start(yb[t % 3][k][0:r], Y[k * TOKENS + t * P:k * TOKENS + t * P + r]).then_inc(s_y[t % 3], 16)
                    if t == 0:
                        sp.dma_start(gple, a["g_ple"][0].partition_broadcast(P)).then_inc(s_gm, 16)
                    else:
                        load_p(t)
                if t >= 3:
                    q = t - 3
                    r = rows_of(q)
                    sp.wait_ge(s_3f, q + 1)
                    dst = o["y_prompt"][0, q * P:(q + 1) * P] if q < TS else o["y_sample"][0]
                    sp.dma_start(dst, fin[q % 2][0:r]).then_inc(s_out[q % 2], 16)
            sp.wait_ge(s_out[0], 16 * 5)
            sp.wait_ge(s_out[1], 16 * 4)

        @block.gpsimd
        def _(pool):
            last_pow = []

            def rstd(dst, src, scale, signal, count):
                n = dst.shape[1]
                if last_pow:
                    pool.wait_ge(*last_pow)
                last_pow[:] = (signal, count)
                link(pool, "pool", nc.gpsimd.tensor_scalar(ms[:, 0:n], src, scale, EPS, ALU.mult, ALU.add))
                nc.gpsimd.tensor_tensor(dst, ms[:, 0:n], neghalf[:, 0:n], ALU.pow).then_inc(signal, 1)

            link(pool, "pool", nc.gpsimd.memset(ident, 0.0))
            nc.gpsimd.affine_select(out=ident, in_=ident, compare_op=ALU.not_equal, fill=1.0, base=0,
                                    pattern=[[-1, P]], channel_multiplier=1).then_inc(s_id, 1)
            link(pool, "pool", nc.gpsimd.memset(neghalf, -0.5))
            nc.gpsimd.memset(uT[:, :, 0:HALO], 0.0).then_inc(s_zero, 1)
            nc.gpsimd.memset(R[:, TS, C:2 * C], 0.0).then_inc(s_zero, 1)
            nc.gpsimd.iota(bias[:, 0, :], [[-1, 2 * P]], base=P, channel_multiplier=1,
                           allow_small_or_imprecise_dtypes=True).then_inc(s_const, 1)

            def pool_chunk(j):
                mixer_lo(pool, nc.gpsimd, s_wlp, j, lo_cut(j), chunk_size(j))

            POOL_EARLY, POOL_BEFORE, POOL_PER_TILE = 6, 36, 14
            acc = R[:, TS, C:2 * C].rearrange("p (c n) -> p c n", c=KC)[:, :, 0:SAMPLE]
            early, late = qT[:, C:C + 2 * P], u2[:, C // 2:C]

            def sample_tap(j):
                tap = late.rearrange("p (c n) -> p c n", c=KC)
                weight = convw[:, :, j:j + 1].broadcast_to([P, KC, SAMPLE])
                if j == 0:
                    pool.wait_ge(s_uT, NT)
                    pool.wait_ge(s_uout, 2)
                    pool.wait_ge(s_ut, NT)
                    link(pool, "pool", nc.gpsimd.tensor_scalar(tap, uT[:, :, U_SAMPLE:U_SAMPLE + SAMPLE], 0.0, None, ALU.mult))
                    link(pool, "pool", nc.gpsimd.tensor_tensor(acc, tap, convw[:, :, TAPS:TAPS + 1].broadcast_to([P, KC, SAMPLE]), ALU.add))
                link(pool, "pool", nc.gpsimd.tensor_tensor(tap, uT[:, :, U_SAMPLE + j:U_SAMPLE + j + SAMPLE], weight, ALU.mult))
                link(pool, "pool", nc.gpsimd.tensor_tensor(acc, acc, tap, ALU.add))

            def channel_tap(j, pair, where):
                t0 = 2 * pair
                acc2 = R[:, t0:t0 + 2, C + (KC - 1) * P:C + KC * P]
                src = uT[:, KC - 1, t0 * P + j:(t0 + 2) * P + j].rearrange("p (t n) -> p t n", n=P)
                tap2 = where.rearrange("p (t n) -> p t n", n=P)
                weight = convw[:, KC - 1, j:j + 1].unsqueeze(2).broadcast_to([P, 2, P])
                if j == 0:
                    pool.wait_ge(s_uT, t0 + 2)
                    pool.wait_ge(s_stt, 4)
                    link(pool, "pool", nc.gpsimd.tensor_scalar(acc2, src, convw[:, KC - 1, 0:1], convw[:, KC - 1, TAPS:TAPS + 1], ALU.mult, ALU.add))
                else:
                    link(pool, "pool", nc.gpsimd.tensor_tensor(tap2, src, weight, ALU.mult))
                    link(pool, "pool", nc.gpsimd.tensor_tensor(acc2, acc2, tap2, ALU.add))

            def conv_steps(first, last, where):
                for n in range(first, min(last, POOL_STEPS)):
                    if POOL_FIRST <= n < POOL_FIRST + TAPS:
                        sample_tap(n - POOL_FIRST)
                    else:
                        m = n if n < POOL_FIRST else n - TAPS
                        channel_tap(m % TAPS, m // TAPS, where)
                    if n == POOL_FIRST - 1:
                        pool.sem_inc(s_convs, 1)

            for t in range(NT):
                pool.wait_ge(s_ss, t + 1)
                rstd(rsx[:, t:t + 1], ssx[:, t:t + 1], 1.0 / D, s_rs, t + 1)
                if t == 0:
                    for j in range(4):
                        pool_chunk(j)
                if t >= 2:
                    pool.wait_ge(s_xs, t - 1)
                    nc.gpsimd.tensor_tensor(xb[t % 2], xb[t % 2], gmix, ALU.mult).then_inc(s_xnp, 1)
                if t >= 5:
                    conv_steps(POOL_EARLY * (t - 5), POOL_EARLY * (t - 4), early)
            conv_steps(4 * POOL_EARLY, POOL_BEFORE, early)
            for j in range(4, 9):
                pool_chunk(j)
            pool.wait_ge(s_ssq, 1)
            rstd(r10, ss10, 1.0 / HD, s_r10, 1)
            for t in range(NT + 1):
                if t + 1 < NT:
                    pool.wait_ge(s_ssq, t + 2)
                    rstd(r10, ss10, 1.0 / HD, s_r10, t + 2)
                if t >= 1:
                    pool.wait_ge(s_osq, t)
                    pool.wait_ge(s_o, t - 1)
                    rstd(r1, ss1, 1.0 / C, s_ors, t)
                if t == NT - 1:
                    pool.wait_ge(s_xn, NT + 2)
                    nc.gpsimd.memset(c_ones, 1.0).then_inc(s_ones, 1)
                conv_steps(POOL_BEFORE + POOL_PER_TILE * t, POOL_BEFORE + POOL_PER_TILE * (t + 1), late)
            pool.sem_inc(s_convs, 1)
            for i, (t0, nt) in enumerate(SPANS):
                pool.wait_ge(s_cve, i + 1)
                nc.gpsimd.tensor_tensor(rsx[:, t0:t0 + nt], ssx[:, t0:t0 + nt], neghalf[:, 0:nt], ALU.pow).then_inc(s_crs, 1)
            pool.wait_ge(s_oe, NT)
            nc.gpsimd.memset(ones, 1.0).then_inc(s_ones, 1)
            for i, (t0, nt) in enumerate(SPANS):
                pool_chunk(J_OUT + i)
                for t in range(t0, t0 + nt):
                    pool.wait_ge(s_c3s, t + 1)
                    rstd(rsx[:, t:t + 1], ssx[:, t:t + 1], 1.0 / C, s_c3r, t + 1)
            pool_chunk(SPLIT_JOBS - 1)
            for t in range(NT):
                pool.wait_ge(s_hs, t + 1)
                pool.wait_ge(s_h, t)
                rstd(r1, ss1, 1.0 / D, s_hr, t + 1)
            pool.wait_ge(s_h, NT)
            pool.wait_ge(s_hst[0], 16 * 5)
            pool.wait_ge(s_hst[1], 16 * 4)
            nc.gpsimd.iota(iota, [[1, P]], base=0, channel_multiplier=0, allow_small_or_imprecise_dtypes=True).then_inc(s_const, 1)
            nc.gpsimd.iota(rev8, [[-1, 8]], base=8, channel_multiplier=0, allow_small_or_imprecise_dtypes=True).then_inc(s_const, 1)
            nc.gpsimd.iota(thr8, [[P, 8]], base=P, channel_multiplier=0, allow_small_or_imprecise_dtypes=True).then_inc(s_const, 1)
            nc.gpsimd.iota(idk[0], [[P, NT]], base=1, channel_multiplier=1, allow_small_or_imprecise_dtypes=True).then_inc(s_const, 1)
            link(pool, "pool", nc.gpsimd.memset(tri, 1.0))
            nc.gpsimd.affine_select(out=tri, in_=tri, compare_op=ALU.is_gt, fill=0.0, base=0,
                                    pattern=[[1, P]], channel_multiplier=-1).then_inc(s_const, 1)
            for c in range(4):
                pool.wait_ge(s_mhi, c + 1)
                for first, last, signal in ((0, LOV, s_mlv), (LOV, CH, s_mlp)):
                    lo_part(nc.gpsimd, whl[:, 1, c * CH + first:c * CH + last], whl[:, 0, c * CH + first:c * CH + last],
                            raw[c][:, first:last]).then_inc(signal, 1)
            pool.wait_ge(s_tab, 1)
            def col(table, v):
                return table[:, v:v + 1] if isinstance(v, int) else table[:, bass.ds(v, 1)]

            def passed():
                pool.sem_inc(s_go, 1)

            def gather(b, signal):
                nc.gpsimd.indirect_dma_start(out=xs[b], out_offset=None, in_=H,
                                             in_offset=bass.IndirectOffsetOnAxis(ap=idxg_cur[b].bitcast(I32), axis=0),
                                             bounds_check=TOKENS - 1, oob_is_err=False).then_inc(signal, 16)

            def scatter(b, signal):
                nc.gpsimd.indirect_dma_start(out=Y, out_offset=bass.IndirectOffsetOnAxis(ap=idxs_cur[b].bitcast(I32), axis=0),
                                             in_=y, in_offset=None, bounds_check=2 * TOKENS - 1,
                                             oob_is_err=False).then_inc(signal, 16)

            def expert_lo(J, slot, c):
                pool.wait_ge(s_mhi, J + 1)
                lo_part(nc.gpsimd, whl[:, 1, slot * CH + LOV:(slot + 1) * CH], whl[:, 0, slot * CH + LOV:(slot + 1) * CH],
                        raw[c][:, LOV:CH]).then_inc(s_mlp, 1)

            for e in range(2):
                link(pool, "pool", nc.gpsimd.tensor_copy(idxg_cur[e].bitcast(I32), col(idx_gather, e).bitcast(I32)))
                gather(e, s_g[e])
            nc.gpsimd.memset(y, 0.0).then_inc(s_idx0, 1)
            nc.gpsimd.memset(w_cur[0], 4096.0).then_inc(s_idx0, 1)
            pool.wait_ge(s_idx0, 2)
            nc.gpsimd.tensor_copy(idxs_cur[0].bitcast(I32), w_cur[0]).then_inc(s_idx0, 1)
            pool.wait_ge(s_idx0, 3)
            scatter(0, s_sc_d)
            pool.wait_ge(s_sc_d, 16)
            with pool.Fori(0, NE, 2) as e0:
                for b in range(2):
                    e = e0 + b
                    pool.wait_ge(s_xst, e + 1)
                    pool.wait_ge(s_g[b], 8 * e0 + 16)
                    passed()
                    nc.gpsimd.tensor_copy(idxg_cur[b].bitcast(I32), col(idx_gather, e + 2).bitcast(I32)).then_inc(s_idx, 1)
                    nc.gpsimd.tensor_copy(idxs_cur[b].bitcast(I32), col(idx_scatter, e).bitcast(I32)).then_inc(s_idx, 1)
                    nc.gpsimd.tensor_copy(w_cur[b], col(wtab, e)).then_inc(s_idx, 1)
                    pool.wait_ge(s_idx, 3 * e + 3)
                    passed()
                    gather(b, s_g[b])
                    for c in range(4, 10):
                        expert_lo(6 * e + c, (6 * b + c) % 4, c % 6)
                    pool.wait_ge(s_y0, e + 2)
                    pool.wait_ge(s_y1, e + 2)
                    passed()
                    scatter(b, s_sc_d)
            pool.wait_ge(s_g[0], 16 * (NE // 2 + 1))
            pool.wait_ge(s_g[1], 16 * (NE // 2 + 1))
            pool.wait_ge(s_sc_d, 16 * (NE + 1))
            pool.wait_ge(s_xst, NE + 1)
            def ovf_block(j):
                nc.gpsimd.tensor_copy(idxg_cur[0].bitcast(I32), col(idx_gather, j + NE).bitcast(I32)).then_inc(g_idx, 1)
                nc.gpsimd.tensor_copy(idxs_cur[0].bitcast(I32), col(idx_scatter, j + NE).bitcast(I32)).then_inc(g_idx, 1)
                nc.gpsimd.tensor_copy(w_cur[0], col(wtab, j + NE)).then_inc(g_idx, 1)
                pool.wait_ge(g_idx, 3 * j + 3)
                if not first_extra(j):
                    passed()
                    gather(0, g_gath)
                    pool.wait_ge(g_gath, 16 * j)
                pool.wait_ge(g_dve, 3 * j + 3)
                passed()
                scatter(0, g_scat)
                pool.wait_ge(g_scat, 16 * j + 16)
                passed()

            n_ovf = pool.value_load(novf[0:1, 0:1].bitcast(I32), min_val=0, max_val=NOVF)
            extra_blocks(pool, n_ovf, ovf_block)
            pool.sem_inc(s_moe, 1)
            for t in range(NT):
                pool.wait_ge(s_3s, t + 1)
                rstd(rsx[:, t:t + 1], ssx[:, t:t + 1], 1.0 / D, s_3r, t + 1)

        @block.scalar
        def _(act):
            def square_sum(src, junk, out, signal):
                nc.scalar.activation(junk, src, ACT.Square, accum_out=out).then_inc(signal, 1)

            def junk_of(v, n):
                return v.bitcast(BF16)[:, 0:n]

            def x_square(t):
                act.wait_ge(s_x[t % 2], 16 * (t // 2 + 1))
                if t >= 1:
                    act.wait_ge(s_ss, t)
                square_sum(xb[t % 2], junk_of(qT, D), ssx[:, t:t + 1], s_ss)

            def x_hi(n, half, b):
                act.wait_ge(s_xt, 2 * n + half + 1)
                nc.scalar.activation(ahl[:, n % 2, 0, half * C:(half + 1) * C], bank(b), ACT.Copy).then_inc(s_xh, 1)

            x_square(0)
            mixer_hi(act, 0)
            mixer_hi(act, 1)
            act.wait_ge(s_stt, 1)
            nc.scalar.activation(uT[:, :, U_SAMPLE:U_SAMPLE + HALO], ps[:, 7, 0:KC * HALO].rearrange("p (c n) -> p c n", c=KC),
                                 ACT.Copy).then_inc(s_stt, 1)
            nc.scalar.activation(kcache[0:HD, :], ps[0:HD, 7, KC * HALO:KC * HALO + NKV * P], ACT.Copy).then_inc(s_stt, 1)
            nc.scalar.activation(convw.rearrange("p c j -> p (c j)"), ps[:, 7, TAPS_AT:TAPS_AT + KC * CROWS], ACT.Copy).then_inc(s_stt, 1)
            nc.scalar.activation(lnh, ps[:, 7, TAPS_AT:TAPS_AT + KC * CROWS].rearrange("p (c j) -> p c j", c=KC)[:, :, TAPS + 1:CROWS],
                                 ACT.Copy, scale=0.5).then_inc(s_stt, 1)
            x_hi(0, 0, 0)
            x_hi(0, 1, 1)
            x_square(1)
            mixer_hi(act, 2)
            mixer_hi(act, 3)
            for t in range(NT):
                if t + 2 < NT:
                    x_square(t + 2)
                    act.wait_ge(s_rs, t + 3)
                    act.wait_ge(s_ss, t + 3)
                    nc.scalar.activation(xb[t % 2], xb[t % 2], ACT.Copy, scale=rsx[:, t + 2:t + 3]).then_inc(s_xs, 1)
                if t + 1 < NT:
                    x_hi(t + 1, 0, 0)
                    x_hi(t + 1, 1, 1)
                if t == NT - 1:
                    for h in range(2):
                        x_hi(NT, h, h)
                    for j in range(J_QKV, J_PW):
                        mixer_hi(act, j)
                zb = 2 + 2 * (t % 2)
                act.wait_ge(s_z, t + 1)
                if t >= 1:
                    act.wait_ge(s_u, t)
                nc.scalar.activation(pT[:, 0:C], bank(zb + 1), ACT.Tanh, scale=0.5).then_inc(s_th, 1)
                act.wait_ge(s_ut, t + 1)
                at = HALO + t * P if t < TS else U_SAMPLE + HALO
                nc.scalar.activation(uT[:, :, at:at + rows_of(t)],
                                     bank(6).rearrange("p (c n) -> p c n", c=KC)[:, :, 0:rows_of(t)],
                                     ACT.Copy, scale=0.5).then_inc(s_uT, 1)
                if t >= TS - 1:
                    side = t - (TS - 1)
                    act.wait_ge(s_u, t + 1)
                    nc.scalar.activation(S[:, side * C:(side + 1) * C], u2, ACT.Copy, scale=0.5).then_inc(s_uout, 1)

            mixer_hi(act, J_PW)
            def square_qk(t):
                act.wait_ge(s_z, NT + t + 1)
                if t >= 1:
                    act.wait_ge(s_qkt, t)
                if t == TS:
                    act.wait_ge(s_kv, 16 * 4)
                nc.scalar.activation(qkn[:, 0:QW + KVW], banks2(2)[:, 0:QW + KVW], ACT.Square).then_inc(s_sq, 1)
                nc.scalar.activation(vb[:, t % 3, :], banks2(2)[:, QW + KVW:GLU0], ACT.Copy).then_inc(s_v, 1)

            def exps(t, hf):
                act.wait_ge(s_nm, 2 * t + hf + 1)
                lo = P if t == 0 else 0
                nc.scalar.activation(esink[t % 2][:, 4 * hf:4 * hf + 4], msink[:, 4 * hf:4 * hf + 4], ACT.Exp).then_inc(s_ex, 1)
                for i in range(4):
                    h = 4 * hf + i
                    s = S.rearrange("p (h k) -> p h k", h=4)[:, i, lo:2 * P]
                    nc.scalar.activation(s, s, ACT.Exp, bias=negm[:, h:h + 1], accum_out=den[t % 2][:, h:h + 1]).then_inc(s_ex, 1)

            def pt_copy(t, hf):
                act.wait_ge(s_pt, 2 * t + hf + 1)
                lo = P if t == 0 else 0
                act_out = pT.rearrange("p (h k) -> p h k", h=4)[:, :, lo:2 * P]
                nc.scalar.activation(act_out, banks2(4).rearrange("p (h k) -> p h k", h=4)[:, :, lo:2 * P], ACT.Copy).then_inc(s_pT, 1)

            square_qk(0)
            for t in range(NT + 1):
                if t + 1 < NT:
                    x_hi(NT + t + 1, 0, 0)
                if t >= 1:
                    exps(t - 1, 1)
                if t < NT:
                    act.wait_ge(s_qkt, t + 1)
                    nc.scalar.activation(qT[0:HD, :], banks2(4)[0:HD, :], ACT.Copy).then_inc(s_qT, 1)
                    src = ps[0:HD, 6, 0:NKV * P].rearrange("p (g k) -> p g k", g=NKV)
                    nc.scalar.activation(kTb[0:HD, t % 2, :, P:2 * P], src, ACT.Copy).then_inc(s_kT, 1)
                    if t < TS - 1:
                        nc.scalar.activation(kTb[0:HD, (t + 1) % 2, :, 0:P], src, ACT.Copy).then_inc(s_kT, 1)
                    if t == TS - 1:
                        nc.scalar.activation(kTb[0:HD, (t + 1) % 2, :, 0:P], kcache[0:HD, :].rearrange("p (g k) -> p g k", g=NKV),
                                             ACT.Copy).then_inc(s_kT, 1)
                if t + 1 < NT:
                    x_hi(NT + t + 1, 1, 0)
                if t >= 1:
                    pt_copy(t - 1, 1)
                if t < NT:
                    exps(t, 0)
                if t >= 1:
                    act.wait_ge(s_oe, t)
                    act.wait_ge(s_ors, t - 1)
                    square_sum(R[:, t - 1, 0:QW], junk_of(u2, QW), ss1, s_osq)
                if t + 1 < NT:
                    square_qk(t + 1)
                if t < NT:
                    pt_copy(t, 0)

            act.wait_ge(s_kv, 16 * 6)
            act.wait_ge(s_convs, 2)
            act.wait_ge(s_oe, NT)
            for i in range(3):
                for c in range(KC):
                    act.wait_ge(s_c1, KC * i + c + 1)
                    n = SPANS[i][1] * P
                    nc.scalar.activation(by_tile(c_sq[i][:, c * n:(c + 1) * n], i), span_view(i, c), ACT.Square).then_inc(s_cq, 1)
            for i in range(3):
                for c in range(KC):
                    n = SPANS[i][1] * P
                    act.wait_ge(s_cn, KC * i + c + 1)
                    nc.scalar.activation(by_tile(c_th[i][:, c * n:(c + 1) * n], i), span_view(i, c), ACT.Tanh,
                                         bias=lnh[:, c, 1:2], scale=lnh[:, c, 0:1]).then_inc(s_cth, 1)
            for i, (t0, nt) in enumerate(SPANS):
                for c in range(KC):
                    n = nt * P
                    b, at = swish_at(i, c)
                    act.wait_ge(s_c2, KC * i + c + 1)
                    if i >= 1:
                        act.wait_ge(s_pw, t0)
                    nc.scalar.activation(ahl[:, b, 0, at], c_th[i][:, c * n:(c + 1) * n], ACT.Copy).then_inc(s_ch, 1)
                mixer_hi(act, J_OUT + i)
                for t in range(t0, t0 + nt):
                    act.wait_ge(s_c3, t + 1)
                    if t >= 1:
                        act.wait_ge(s_c3s, t)
                    square_sum(R[:, t, C:2 * C], junk_of(junk3, C), ssx[:, t:t + 1], s_c3s)
            mixer_hi(act, SPLIT_JOBS - 1)
            for h in range(2):
                x_hi(2 * NT, h, h)
            for t in range(NT + 2):
                if t + 1 < NT:
                    for h in range(2):
                        x_hi(2 * NT + t + 1, h, h)
                if t >= 2:
                    if t >= 3:
                        act.wait_ge(s_rl, t - 2)
                    for h in range(2):
                        act.wait_ge(s_ht, 2 * (t - 2) + h + 1)
                        nc.scalar.activation(hT[:, (1 - h) * C:(2 - h) * C], bank(7 - h), ACT.Copy).then_inc(s_hT, 1)
                if t < NT:
                    act.wait_ge(s_x1, t + 1)
                    if t >= 1:
                        act.wait_ge(s_hr, t)
                    square_sum(R[:, t, :], junk_of(scr[:, P:2 * C], D), ss1, s_hs)
            act.wait_ge(s_rta, 1)
            nc.scalar.activation(eqc, dc, ACT.Exp).then_inc(s_rta, 1)
            act.wait_ge(s_rta, 3)
            nc.scalar.activation(e2, mt, ACT.Exp).then_inc(s_rta, 1)

            def expert_hi(J, slot, c, arrived, used):
                act.wait_ge(s_mraw[c], arrived)
                if used is not None:
                    act.wait_ge(s_use, used)
                nc.scalar.activation(whl[:, 0, slot * CH:(slot + 1) * CH], raw[c], ACT.Copy).then_inc(s_mhi, 1)

            def slots_hi(b, count):
                act.wait_ge(s_xst, count)
                nc.scalar.activation(ahl[:, b, 0, :], banks2(0), ACT.Copy).then_inc(s_xsh, 1)

            act.wait_ge(s_w, NT)
            for c in range(4):
                expert_hi(c, c, c, 16, None)
            slots_hi(0, 1)
            for signal in (s_y0, s_mth):
                act.sem_inc(signal, 1)
            with act.Fori(0, NE, 2) as e0:
                for b in range(2):
                    e = e0 + b
                    for c in (4, 5):
                        expert_hi(None, (6 * b + c) % 4, c, 16 * e + 16, 6 * e + (c - 3))
                    act.wait_ge(s_use, 6 * e + 2)
                    act.wait_ge(s_mht, e + 1)
                    nc.scalar.activation(th, bank(2), ACT.Tanh, scale=0.5).then_inc(s_mth, 1)
                    expert_hi(None, (6 * b + 6) % 4, 0, 16 * e + 32, 6 * e + 3)
                    act.wait_ge(s_mht, e + 2)
                    nc.scalar.activation(hhl[:, 0, :], bank(4), ACT.Copy).then_inc(s_hh, 1)
                    slots_hi(1 - b, e + 2)
                    for c in (1, 2, 3):
                        expert_hi(None, (6 * b + 6 + c) % 4, c, 16 * e + 32, 6 * e + 3 + c)
                    act.wait_ge(s_use, 6 * e + 6)
                    act.wait_ge(s_sc_d, 16 * e + 16)
                    act.wait_ge(s_idx, 3 * e + 3)
                    nc.scalar.activation(y[:, 0:C], bank(5), ACT.Copy, scale=w_cur[b]).then_inc(s_y0, 1)
            act.wait_ge(s_tab, 1)
            def ovf_block(j):
                if first_extra(j):
                    act.wait_ge(s_g[1], 16 * (NE // 2 + 1))
                act.wait_ge(g_pe, 2 * j + 1)
                nc.scalar.activation(xs[1], banks2(0), ACT.Copy).then_inc(g_act, 1)
                act.wait_ge(g_use, 6 * j + 5)
                nc.scalar.activation(th, bank(2), ACT.Tanh, scale=0.5).then_inc(g_act, 1)
                act.wait_ge(g_pe, 2 * j + 2)
                nc.scalar.activation(xs[0][:, 0:DE], bank(4), ACT.Copy).then_inc(g_act, 1)

            n_ovf = act.value_load(novf[0:1, 0:1].bitcast(I32), min_val=0, max_val=NOVF)
            extra_blocks(act, n_ovf, ovf_block)
            act.wait_ge(s_moe, 1)

            def x2_square(t):
                act.wait_ge(s_x2, t + 1)
                if t >= 1:
                    act.wait_ge(s_3s, t)
                square_sum(R[:, t, :], junk_of(th, D), ssx[:, t:t + 1], s_3s)

            def x2_hi(t):
                for h in range(2):
                    act.wait_ge(s_3t, 2 * t + h + 1)
                    nc.scalar.activation(ahl[:, t % 2, 0, h * C:(h + 1) * C], bank(h), ACT.Copy).then_inc(s_3h, 1)
                if t >= 1:
                    p_turned(t)

            def p_turned(t):
                act.wait_ge(s_3pt, t + 1)
                nc.scalar.activation(pT3[t % 2], bank(6, PLE), ACT.Copy).then_inc(s_3pT, 1)

            p_turned(0)
            x2_square(0)
            x2_hi(0)
            x2_square(1)
            x2_square(2)
            for t in range(NT):
                if t >= 1:
                    act.wait_ge(s_3g, t)
                    if t >= 3:
                        act.wait_ge(s_3f, t - 2)
                    nc.scalar.activation(tg[(t - 1) % 2], banks2(2), ACT.Tanh, scale=0.5).then_inc(s_3th, 1)
                if t + 1 < NT:
                    x2_hi(t + 1)
                if t + 3 < NT:
                    x2_square(t + 3)
            act.wait_ge(s_3g, NT)
            act.wait_ge(s_3f, NT - 2)
            nc.scalar.activation(tg[(NT - 1) % 2], banks2(2), ACT.Tanh, scale=0.5).then_inc(s_3th, 1)

        @block.vector
        def _(dve):
            def chain(ins):
                link(dve, "dve", ins)

            conv = conv_ops(dve)
            done = [0]

            def convs(n):
                for _ in range(n):
                    if done[0] < CONV_OPS:
                        next(conv)
                        done[0] += 1

            def dve_chunk(j):
                mixer_lo(dve, nc.vector, s_wlv, j, 0, lo_cut(j))

            def x_norm(n):
                dve.wait_ge(s_x[n % 2], 16 * (n // 2 + 1))
                if n < NT:
                    dve.wait_ge(s_rs, n + 1)
                if n == 0:
                    dve.wait_ge(s_gm, 16)
                t = n % NT
                nc.vector.scalar_tensor_tensor(xb[n % 2], xb[n % 2], rsx[:, t:t + 1], gmix, ALU.mult, ALU.mult).then_inc(s_xn, 1)

            def x_lo(n, half, b):
                dve.wait_ge(s_xh, 2 * n + half + 1)
                at = slice(half * C, (half + 1) * C)
                lo_part(nc.vector, ahl[:, n % 2, 1, at], ahl[:, n % 2, 0, at], bank(b)).then_inc(s_xl, 1)

            def ev(t):
                zb = 2 + 2 * (t % 2)
                dve.wait_ge(s_th, t + 1)
                if t >= 1:
                    dve.wait_ge(s_ut, t)
                if t == TS:
                    dve.wait_ge(s_uout, 1)
                nc.vector.scalar_tensor_tensor(u2, pT[:, 0:C], 1.0, bank(zb), ALU.add, ALU.mult).then_inc(s_u, 1)

            CONVS_BY_TILE = (0, 0, 26, 26, 26, 26, 26, 24, 18)
            x_norm(0)
            dve.wait_ge(s_const, 1)
            chain(nc.vector.scalar_tensor_tensor(bias[:, 0, :], bias[:, 0, :], -1.0, bias[:, 0, :], ALU.mult, ALU.min))
            for h in range(NH - 1, -1, -1):
                chain(nc.vector.tensor_scalar(bias[:, h, :], bias[:, 0, :], 2.0 ** (-8.0 * (h + 1) / NH), None, ALU.mult))
            chain(nc.vector.memset(bias[0:64, :, 192:256], NEG))
            chain(nc.vector.memset(bias[64:128, :, 0:64], NEG))
            dve_chunk(0)
            dve_chunk(1)
            x_lo(0, 0, 0)
            x_lo(0, 1, 1)
            x_norm(1)
            dve_chunk(2)
            dve_chunk(3)
            for t in range(NT):
                n = t + 1
                if t + 1 < NT:
                    x_lo(n, 0, 0)
                    x_lo(n, 1, 1)
                else:
                    x_lo(n, 0, 0)
                    x_lo(n, 1, 1)
                    for j in range(J_QKV, J_OUT - 1):
                        dve_chunk(j)
                if t + 2 == NT:
                    x_norm(NT)
                ev(t)
                if t + 2 > NT:
                    x_norm(t + 2)
                if t >= 2:
                    convs(CONVS_BY_TILE[t])
            dve_chunk(J_OUT - 1)

            def qk_sums(t):
                dve.wait_ge(s_sq, t + 1)
                nc.vector.tensor_reduce(ss10, qkn[:, 0:QW + KVW].rearrange("p (h d) -> p h d", d=HD), AX.X, ALU.add).then_inc(s_ssq, 1)

            def qk_norm(t):
                dve.wait_ge(s_r10, t + 1)
                dve.wait_ge(s_v, t + 1)
                dve.wait_ge(s_ssq, t + 1)
                nc.vector.tensor_tensor(qkn[:, 0:QW + KVW].rearrange("p (h d) -> p h d", d=HD),
                                        banks2(2)[:, 0:QW + KVW].rearrange("p (h d) -> p h d", d=HD),
                                        r10.unsqueeze(2).broadcast_to([P, NH + NKV, HD]), ALU.mult).then_inc(s_zev, 1)
                dve.wait_ge(s_zev, t + 1)
                nc.vector.tensor_tensor(qkn[:, 0:QW + KVW], qkn[:, 0:QW + KVW], gqk, ALU.mult).then_inc(s_qkn, 1)

            def biased(t, hf):
                lo = P if t == 0 else 0
                if t == 0 and hf == 0:
                    dve.wait_ge(s_uo, 16 * 2)
                dve.wait_ge(s_sc, 2 * t + hf + 1)
                if 2 * t + hf > 0:
                    dve.wait_ge(s_pt, 2 * t + hf)
                hs = slice(4 * hf, 4 * hf + 4)
                s = S.rearrange("p (h k) -> p h k", h=4)[:, :, lo:2 * P]
                nc.vector.scalar_tensor_tensor(s, banks2(6).rearrange("p (h k) -> p h k", h=4)[:, :, lo:2 * P],
                                               HD ** -0.5, bias[:, hs, lo:2 * P], ALU.mult, ALU.add).then_inc(s_sb, 1)
                dve.wait_ge(s_sb, 2 * t + hf + 1)
                chain(nc.vector.tensor_reduce(mx[:, hs], s, AX.X, ALU.max))
                chain(nc.vector.tensor_tensor(mx[:, hs], mx[:, hs], sink[:, hs], ALU.max))
                chain(nc.vector.tensor_tensor(msink[:, hs], sink[:, hs], mx[:, hs], ALU.subtract))
                nc.vector.tensor_scalar(negm[:, hs], mx[:, hs], -1.0, None, ALU.mult).then_inc(s_nm, 1)

            def attention_out(t):
                dve.wait_ge(s_ex, 10 * t + 10)
                chain(nc.vector.tensor_tensor(den[t % 2], den[t % 2], esink[t % 2], ALU.add))
                chain(nc.vector.reciprocal(rden, den[t % 2]))
                dve.wait_ge(s_pv, 2 * t + 2)
                nc.vector.tensor_tensor(R[:, t, 0:QW].rearrange("p (h d) -> p h d", d=HD),
                                        bank(1).rearrange("p (h d) -> p h d", d=HD),
                                        rden.unsqueeze(2).broadcast_to([P, NH, HD]), ALU.mult).then_inc(s_oe, 1)

            def attention_norm(t):
                dve.wait_ge(s_ors, t + 1)
                dve.wait_ge(s_oe, t + 1)
                nc.vector.scalar_tensor_tensor(R[:, t, 0:QW], R[:, t, 0:QW], r1, goa, ALU.mult, ALU.mult).then_inc(s_o, 1)

            dve.wait_ge(s_ld, 16 * LOADS)
            qk_sums(0)
            qk_norm(0)
            for t in range(NT + 1):
                if t == NT:
                    convs(CONV_OPS)
                if t + 1 < NT:
                    x_lo(NT + t + 1, 0, 0)
                    x_lo(NT + t + 1, 1, 0)
                if t + 2 < NT:
                    x_norm(NT + t + 2)
                convs(6)
                if t < NT:
                    biased(t, 0)
                if t >= 1:
                    attention_out(t - 1)
                convs(4)
                if t + 1 < NT:
                    qk_sums(t + 1)
                if t < NT:
                    biased(t, 1)
                if t + 1 < NT:
                    qk_norm(t + 1)
                if t >= 1:
                    attention_norm(t - 1)
            dve.wait_ge(s_ld2, 16 * 3)

            def centre(i):
                dve.wait_ge(s_cs, i + 1)
                for c in range(KC):
                    nc.vector.scalar_tensor_tensor(span_view(i, c), by_tile(bank((0, 2, 3)[i]), i), -1.0 / C, span_view(i, c),
                                                   ALU.mult, ALU.add).then_inc(s_c1, 1)

            def add_squares(i):
                n = SPANS[i][1] * P
                sq = c_sq[i]
                dve.wait_ge(s_cq, KC * (i + 1))
                nc.vector.tensor_tensor(sq[:, 0:n], sq[:, 0:n], sq[:, n:2 * n], ALU.add).then_inc(s_ca, 1)
                nc.vector.tensor_tensor(sq[:, 2 * n:3 * n], sq[:, 2 * n:3 * n], sq[:, 3 * n:4 * n], ALU.add).then_inc(s_ca, 1)
                dve.wait_ge(s_ca, 3 * i + 2)
                nc.vector.tensor_tensor(sq[:, 0:n], sq[:, 0:n], sq[:, 2 * n:3 * n], ALU.add).then_inc(s_ca, 1)

            centre(0)
            centre(1)
            add_squares(0)
            centre(2)
            add_squares(1)
            add_squares(2)
            for i, (t0, nt) in enumerate(SPANS):
                dve.wait_ge(s_cvv, i + 1)
                nc.vector.tensor_scalar(ssx[:, t0:t0 + nt], ps[:, 5 - i, t0:t0 + nt], 1.0 / C, EPS, ALU.mult, ALU.add).then_inc(s_cve, 1)
            for i, (t0, nt) in enumerate(SPANS):
                dve.wait_ge(s_crs, i + 1)
                for t in range(t0, t0 + nt):
                    nc.vector.tensor_scalar(c_rs[i][:, (t - t0) * P:(t - t0 + 1) * P], ident, rsx[:, t:t + 1], None,
                                            ALU.mult).then_inc(s_cdg, 1)

            def scale_rows(i):
                dve.wait_ge(s_cbc, i + 1)
                dve.wait_ge(s_cq, KC * (i + 1))
                dve.wait_ge(s_c1, KC * (i + 1))
                for c in range(KC):
                    nc.vector.tensor_tensor(span_view(i, c), span_view(i, c), by_tile(bank((6, 7, 1)[i]), i), ALU.mult).then_inc(s_cn, 1)

            def swish(i):
                n = SPANS[i][1] * P
                for c in range(KC):
                    dve.wait_ge(s_cth, KC * i + c + 1)
                    dve.wait_ge(s_cn, KC * i + c + 1)
                    nc.vector.tensor_scalar(span_view(i, c), span_view(i, c), lnh[:, c, 0:1], lnh[:, c, 1:2], ALU.mult, ALU.add).then_inc(s_cy, 1)
                for c in range(KC):
                    dve.wait_ge(s_cy, KC * i + c + 1)
                    th_c = by_tile(c_th[i][:, c * n:(c + 1) * n], i)
                    nc.vector.scalar_tensor_tensor(th_c, th_c, 1.0, span_view(i, c), ALU.add, ALU.mult).then_inc(s_c2, 1)

            def swish_lo(i):
                n = SPANS[i][1] * P
                for c in range(KC):
                    b, at = swish_at(i, c)
                    dve.wait_ge(s_ch, KC * i + c + 1)
                    lo_part(nc.vector, ahl[:, b, 1, at], ahl[:, b, 0, at], c_th[i][:, c * n:(c + 1) * n]).then_inc(s_cl, 1)

            scale_rows(0)
            scale_rows(1)
            swish(0)
            scale_rows(2)
            swish_lo(0)
            for i, (t0, nt) in enumerate(SPANS):
                if i >= 1:
                    swish_lo(i)
                else:
                    swish(1)
                    swish(2)
                    dve.wait_ge(s_c2, 3 * KC)
                dve_chunk(J_OUT + i)
                for t in range(t0, t0 + nt + 1):
                    if t < t0 + nt:
                        dve.wait_ge(s_pw, t + 1)
                        nc.vector.tensor_tensor(R[:, t, C:2 * C], bank(4 + t % 2), bpw, ALU.add).then_inc(s_c3, 1)
                    if t > t0:
                        dve.wait_ge(s_c3r, t)
                        nc.vector.scalar_tensor_tensor(R[:, t - 1, C:2 * C], R[:, t - 1, C:2 * C], rsx[:, t - 1:t], goc,
                                                       ALU.mult, ALU.mult).then_inc(s_c4, 1)
            dve_chunk(SPLIT_JOBS - 1)
            for h in range(2):
                x_lo(2 * NT, h, h)
            for t in range(NT + 2):
                if t + 1 < NT:
                    for h in range(2):
                        x_lo(2 * NT + t + 1, h, h)
                if t < NT:
                    dve.wait_ge(s_w, t + 1)
                    dve.wait_ge(s_x[t % 2], 16 * ((2 * NT + t) // 2 + 1))
                    nc.vector.tensor_tensor(R[:, t, :], banks2(2 + 2 * (t % 2)), xb[t % 2], ALU.add).then_inc(s_x1, 1)
                if t >= 2:
                    dve.wait_ge(s_rl, t - 1)
                    nc.vector.tensor_tensor(lg[:, t - 2, :], bank(6, NR), rbias, ALU.add).then_inc(s_lg, 1)
                if t < NT:
                    dve.wait_ge(s_hr, t + 1)
                    if t >= 2:
                        dve.wait_ge(s_hst[t % 2], 16 * (t // 2))
                        dve.wait_ge(s_ht, 2 * (t - 1))
                    dve.wait_ge(s_x1, t + 1)
                    nc.vector.scalar_tensor_tensor(hb[t % 2], R[:, t, :], r1, gffn, ALU.mult, ALU.mult).then_inc(s_h, 1)

            def r3(v, n):
                return v.rearrange("p (t n) -> p t n", n=n)

            def over(v, n):
                return v.unsqueeze(2).broadcast_to([P, v.shape[1], n])

            def rowof(v, t):
                return v.unsqueeze(1).broadcast_to([P, t, v.shape[1]])

            tt = nc.vector.tensor_tensor
            red = nc.vector.tensor_reduce
            dve.wait_ge(s_const, 6)
            dve.wait_ge(s_ones, 2)
            chain(nc.vector.tensor_copy(tri16, tri))
            chain(nc.vector.tensor_copy(ones16, ones))
            dve.wait_ge(s_lg, NT)
            dve.wait_ge(s_hst[0], 16 * 5)
            dve.wait_ge(s_hst[1], 16 * 4)
            lc, lf = lg[:, :, 0:NG], lg[:, :, NG:NR]
            chain(red(gmx, lc, AX.X, ALU.max))
            chain(tt(r3(dc, NG), lc, over(gmx, NG), ALU.subtract))
            dve.sem_inc(s_rta, 1)
            chain(nc.vector.tensor_scalar(og, dc, 0.0, None, ALU.is_ge))
            chain(tt(r3(og, NG), r3(og, NG), rowof(rev8[:, 4:8], NT), ALU.mult))
            chain(red(mt, r3(og, NG), AX.X, ALU.max))
            chain(tt(r3(og, NG), r3(og, NG), over(mt, NG), ALU.is_equal))
            def group_pick():
                return r3(og, NG).unsqueeze(3).broadcast_to([P, NT, NG, EPG])

            def by_group(v):
                return v.rearrange("p (t g e) -> p t g e", t=NT, g=NG)

            chain(tt(by_group(prod), lf.rearrange("p t (g e) -> p t g e", g=NG), group_pick(), ALU.mult))
            chain(red(r3(lsel, EPG), prod.rearrange("p (t g e) -> p t e g", t=NT, g=NG), AX.X, ALU.add))

            def best(m, one):
                chain(red(m, r3(lsel, EPG), AX.X, ALU.max))
                chain(tt(r3(eqf, EPG), r3(lsel, EPG), over(m, EPG), ALU.is_equal))
                chain(tt(r3(eqf, EPG), r3(eqf, EPG), rowof(rev8, NT), ALU.mult))
                chain(red(mt, r3(eqf, EPG), AX.X, ALU.max))
                chain(tt(r3(one, EPG), r3(eqf, EPG), over(mt, EPG), ALU.is_equal))

            best(m1, o1)
            chain(nc.vector.scalar_tensor_tensor(lsel, o1, -3e38, lsel, ALU.mult, ALU.add))
            best(m2, o2)
            chain(tt(mt, m2, m1, ALU.subtract))
            dve.wait_ge(s_rta, 2)
            dve.sem_inc(s_rta, 1)
            chain(red(se, r3(eqc, NG), AX.X, ALU.add))
            for A, one in ((A1, o1), (A2, o2)):
                chain(tt(by_group(A), r3(one, EPG).unsqueeze(2).broadcast_to([P, NT, NG, EPG]), group_pick(), ALU.mult))
            chain(nc.vector.memset(A1[SAMPLE:P, TS * NE:NT * NE], 0.0))
            chain(nc.vector.memset(A2[SAMPLE:P, TS * NE:NT * NE], 0.0))
            chain(nc.vector.memset(A12[:, NT * NE:(NT + 1) * NE], 0.0))
            nc.vector.tensor_tensor(A12[:, 0:NT * NE], A1, A2, ALU.add).then_inc(s_rt, 1)
            dve.wait_ge(s_rta, 4)
            chain(nc.vector.scalar_tensor_tensor(rw, e2, 1.0, se, ALU.add, ALU.mult))
            chain(nc.vector.reciprocal(rw, rw))
            chain(nc.vector.tensor_scalar(wk[0], rw, 0.5, None, ALU.mult))
            chain(tt(wk[1], wk[0], e2, ALU.mult))
            chain(nc.vector.memset(idmask, 1.0))
            chain(nc.vector.memset(idmask[SAMPLE:P, TS:NT], 0.0))
            for k in range(2):
                chain(tt(wk[k], wk[k], idmask, ALU.mult))
            chain(tt(idk[0], idk[0], idmask, ALU.mult))
            chain(nc.vector.scalar_tensor_tensor(idk[1], idmask, float(TOKENS), idk[0], ALU.mult, ALU.add))
            chain(tt(r3(lt, NE), over(iota[:, 0:NE], NE), rowof(iota[:, 0:NE], NE), ALU.is_gt))
            for k, A in enumerate((A1, A2)):
                chain(tt(r3(prod, NE), r3(A, NE), rowof(iota[:, 0:NE], NT), ALU.mult))
                chain(red(ek[k], r3(prod, NE), AX.X, ALU.add))
            dve.wait_ge(s_rtp, 1)
            chain(nc.vector.tensor_copy(pos, bank(0, (NT + 1) * NE)))
            cnt = pos[:, NT * NE:(NT + 1) * NE]
            chain(tt(r3(ovf8, 8), over(cnt, 8), rowof(thr8, NE), ALU.is_gt))
            chain(red(ovf, r3(ovf8, 8), AX.X, ALU.add))
            chain(tt(r3(lt, NE), r3(lt, NE), rowof(ovf, NE), ALU.mult))
            chain(red(start, r3(lt, NE), AX.X, ALU.add))
            chain(tt(end, start, ovf, ALU.add))
            chain(tt(rel, start, iota[:, 0:NE], ALU.subtract))
            for k, A in enumerate((A1, A2)):
                for dst, other in ((pk[k], r3(pos[:, 0:NT * NE], NE)), (stk[k], rowof(rel, NT))):
                    chain(tt(r3(prod, NE), r3(A, NE), other, ALU.mult))
                    chain(red(dst, r3(prod, NE), AX.X, ALU.add))
                chain(tt(r3(cmp9, 8), over(pk[k], 8), rowof(thr8, NT), ALU.is_ge))
                chain(red(bk[k], r3(cmp9, 8), AX.X, ALU.add))
                chain(nc.vector.scalar_tensor_tensor(sk[k], bk[k], -float(P), pk[k], ALU.mult, ALU.add))
                chain(tt(stk[k], stk[k], bk[k], ALU.add))
                chain(nc.vector.tensor_scalar(bk[k], bk[k], 0.0, None, ALU.is_gt))
                chain(nc.vector.scalar_tensor_tensor(vk[k], stk[k], float(NE - 1), bk[k], ALU.add, ALU.mult))
                chain(tt(vk[k], vk[k], ek[k], ALU.add))
                if k == 1:
                    dve.wait_ge(s_rtp, 2)
                chain(tt(r3(Ph, P), rowof(iota, NT), over(sk[k], P), ALU.is_equal))
                chain(tt(r3(oh, NBLK), rowof(iota[:, 0:NBLK], NT), over(vk[k], NBLK), ALU.is_equal))
                Vv = V.rearrange("p (t c v) -> p t c v", t=NT, c=2)
                chain(tt(Vv[:, :, 0, :], r3(oh, NBLK), over(idk[k], NBLK), ALU.mult))
                nc.vector.tensor_tensor(Vv[:, :, 1, :], r3(oh, NBLK), over(wk[k], NBLK), ALU.mult).then_inc(s_rt, 1)
            j16 = over(iota[:, 0:NOVF], NE)
            chain(tt(r3(eb, NE), rowof(start, NOVF), j16, ALU.is_le))
            chain(tt(r3(lt[:, 0:NOVF * NE], NE), rowof(end, NOVF), j16, ALU.is_gt))
            chain(tt(eb, eb, lt[:, 0:NOVF * NE], ALU.mult))
            chain(tt(r3(eb, NE), r3(eb, NE), rowof(iota[:, 0:NE], NOVF), ALU.mult))
            chain(red(tmp48[:, 0:NOVF], r3(eb, NE), AX.X, ALU.add))
            chain(nc.vector.tensor_copy(ebk.bitcast(I32), tmp48[:, 0:NOVF]))
            chain(nc.vector.tensor_copy(novf.bitcast(I32), end[:, NE - 1:NE]))
            dve.wait_ge(s_rtp, 3)
            chain(nc.vector.tensor_copy(tab, bank(2, 2 * NBLK)))
            ids, wts = tab[:, 0:NBLK], tab[:, NBLK:2 * NBLK]
            chain(nc.vector.tensor_copy(wtab, wts))
            chain(nc.vector.tensor_scalar(tmp48, ids, 0.0, 4096.0, ALU.is_equal, ALU.mult))
            chain(nc.vector.scalar_tensor_tensor(tmp48, ids, -1.0, tmp48, ALU.add, ALU.add))
            chain(nc.vector.tensor_copy(idx_scatter.bitcast(I32), tmp48))
            chain(nc.vector.tensor_scalar(eb[:, 0:NBLK], ids, float(TOKENS), -float(TOKENS), ALU.is_gt, ALU.mult))
            chain(nc.vector.tensor_tensor(tmp48, tmp48, eb[:, 0:NBLK], ALU.add))
            nc.vector.tensor_copy(idx_gather.bitcast(I32), tmp48).then_inc(s_tab, 1)

            def expert_lo(J, slot, c):
                dve.wait_ge(s_mhi, J + 1)
                lo_part(nc.vector, whl[:, 1, slot * CH:slot * CH + LOV], whl[:, 0, slot * CH:slot * CH + LOV],
                        raw[c][:, 0:LOV]).then_inc(s_mlv, 1)

            def slots_lo(b, count):
                dve.wait_ge(s_xsh, count)
                lo_part(nc.vector, ahl[:, b, 1, :], ahl[:, b, 0, :], banks2(0)).then_inc(s_xsl, 1)

            slots_lo(0, 1)
            for signal in (s_mg, s_mh, s_hl, s_y1):
                dve.sem_inc(signal, 1)
            with dve.Fori(0, NE, 2) as e0:
                for b in range(2):
                    e = e0 + b
                    for c in (4, 5):
                        expert_lo(6 * e + c, (6 * b + c) % 4, c)
                    dve.wait_ge(s_mth, e + 2)
                    nc.vector.scalar_tensor_tensor(th, th, 1.0, bank(2), ALU.add, ALU.mult).then_inc(s_mg, 1)
                    dve.wait_ge(s_use, 6 * e + 4)
                    dve.wait_ge(s_mg, e + 2)
                    nc.vector.tensor_tensor(th, th, bank(3), ALU.mult).then_inc(s_mh, 1)
                    dve.wait_ge(s_hh, e + 1)
                    lo_part(nc.vector, hhl[:, 1, :], hhl[:, 0, :], bank(4)).then_inc(s_hl, 1)
                    expert_lo(6 * e + 6, (6 * b + 6) % 4, 0)
                    slots_lo(1 - b, e + 2)
                    for c in (1, 2, 3):
                        expert_lo(6 * e + 6 + c, (6 * b + 6 + c) % 4, c)
                    dve.wait_ge(s_use, 6 * e + 6)
                    dve.wait_ge(s_sc_d, 16 * e + 16)
                    dve.wait_ge(s_idx, 3 * e + 3)
                    nc.vector.tensor_scalar(y[:, C:2 * C], bank(6), w_cur[b], None, ALU.mult).then_inc(s_y1, 1)
            def ovf_block(j):
                dve.wait_ge(g_act, 3 * j + 2)
                dve.wait_ge(g_use, 6 * j + 5)
                nc.vector.scalar_tensor_tensor(th, th, 1.0, bank(2), ALU.add, ALU.mult).then_inc(g_dve, 1)
                dve.wait_ge(g_dve, 3 * j + 1)
                dve.wait_ge(g_use, 6 * j + 7)
                nc.vector.tensor_tensor(th, th, bank(3), ALU.mult).then_inc(g_dve, 1)
                dve.wait_ge(g_use, 6 * j + 9)
                dve.wait_ge(g_idx, 3 * j + 3)
                nc.vector.tensor_scalar(y, banks2(5), w_cur[0], None, ALU.mult).then_inc(g_dve, 1)

            n_ovf = dve.value_load(novf[0:1, 0:1].bitcast(I32), min_val=0, max_val=NOVF)
            extra_blocks(dve, n_ovf, ovf_block)
            dve.wait_ge(s_gm, 32)

            def add_experts(t):
                dve.wait_ge(s_y[t % 3], 32 * (t // 3 + 1))
                chain(tt(R[:, t, :], R[:, t, :], yb[t % 3][0], ALU.add))
                nc.vector.tensor_tensor(R[:, t, :], R[:, t, :], yb[t % 3][1], ALU.add).then_inc(s_x2, 1)

            def x2_norm(t):
                dve.wait_ge(s_3r, t + 1)
                dve.wait_ge(s_x2, t + 1)
                if t >= 2:
                    dve.wait_ge(s_3t, 2 * (t - 1))
                nc.vector.scalar_tensor_tensor(xn3[t % 2], R[:, t, :], rsx[:, t:t + 1], gple, ALU.mult, ALU.mult).then_inc(s_3n, 1)

            def x2_lo(t):
                for h in range(2):
                    dve.wait_ge(s_3h, 2 * t + h + 1)
                    at = slice(h * C, (h + 1) * C)
                    lo_part(nc.vector, ahl[:, t % 2, 1, at], ahl[:, t % 2, 0, at], bank(h)).then_inc(s_3l, 1)

            def add_ple(t):
                dve.wait_ge(s_3th, t + 1)
                dve.wait_ge(s_3p, t + 1)
                nc.vector.scalar_tensor_tensor(tg[t % 2], tg[t % 2], 1.0, banks2(4), ALU.add, ALU.mult).then_inc(s_3m, 1)
                dve.wait_ge(s_3m, t + 1)
                if t >= 2:
                    dve.wait_ge(s_out[t % 2], 16 * (t // 2))
                nc.vector.scalar_tensor_tensor(fin[t % 2], tg[t % 2], 0.5, R[:, t, :], ALU.mult, ALU.add).then_inc(s_3f, 1)

            add_experts(0)
            x2_norm(0)
            add_experts(1)
            x2_lo(0)
            x2_norm(1)
            add_experts(2)
            for t in range(NT + 1):
                if t + 1 < NT:
                    x2_lo(t + 1)
                if t >= 1:
                    add_ple(t - 1)
                if t + 2 < NT:
                    x2_norm(t + 2)
                if t + 3 < NT:
                    add_experts(t + 3)

        @block.tensor
        def _(pe):
            def transposes(n, half, src, b, free=None):
                for i in range(4):
                    k = 4 * half + i
                    last = nc.tensor.transpose(ps[:, b, i * P:(i + 1) * P], src[:, k * P:(k + 1) * P], ident)
                return last

            def x_normed(n):
                return (s_xnp, n - 1) if 2 <= n < NT else (s_xn, n + 1 if n < 2 else n + 1 - (NT - 2))

            def x_transpose(n, half, b, src):
                pe.wait_ge(*x_normed(n))
                pe.wait_ge(s_xl, 2 * n + half if n > NT else max(0, 2 * n + half - 1))
                transposes(n, half, src, b).then_inc(s_xt, 1)

            pe.wait_ge(s_id, 1)
            pe.wait_ge(s_st, 16 * 6)
            for c in range(KC):
                nc.tensor.transpose(ps[:, 7, c * HALO:(c + 1) * HALO], S[0:HALO, c * P:(c + 1) * P], ident[0:HALO, 0:HALO])
                nc.tensor.transpose(ps[:, 7, TAPS_AT + c * CROWS:TAPS_AT + (c + 1) * CROWS], u2[0:CROWS, c * P:(c + 1) * P],
                                    ident[0:CROWS, 0:CROWS])
            for g in range(NKV):
                last = nc.tensor.transpose(ps[0:HD, 7, KC * HALO + g * P:KC * HALO + (g + 1) * P], S[:, C + g * HD:C + (g + 1) * HD], ident)
            last.then_inc(s_stt, 1)
            for h in range(2):
                x_transpose(0, h, h, xb[0])
            for t in range(NT):
                if t + 1 < NT:
                    for h in range(2):
                        x_transpose(t + 1, h, h, xb[(t + 1) % 2])
                else:
                    for h in range(2):
                        x_transpose(NT, h, h, xb[NT % 2])
                zb = 2 + 2 * (t % 2)
                if t >= 2:
                    pe.wait_ge(s_u, t - 1)
                for k in range(KD):
                    if t == 0 and k % 2 == 0:
                        weights_ready(pe, k // 2)
                    if k % 4 == 0:
                        pe.wait_ge(s_xl, 2 * t + k // 4 + 1)
                    hi, lo = act_tile(t % 2, k)
                    for n in range(2):
                        last = split_product(bank(zb + n), hi, lo, slice(k * D + n * C, k * D + (n + 1) * C), k == 0, k == KD - 1)
                    if t == NT - 1 and k % 2 == 1:
                        last.then_inc(s_zk, 1)
                if t < NT - 1:
                    last.then_inc(s_z, 1)
                else:
                    pe.wait_ge(s_zk, 4)
                    pe.sem_inc(s_z, 1)
                pe.wait_ge(s_u, t + 1)
                if t >= 1:
                    pe.wait_ge(s_uT, t)
                transposes(t, 0, u2, 6).then_inc(s_ut, 1)

            def qkv(t, half):
                n = NT + t
                if half == 0:
                    if t == 0:
                        pe.wait_ge(s_u, NT)
                    else:
                        pe.wait_ge(s_zev, t)
                        pe.wait_ge(s_v, t)
                pe.wait_ge(s_xl, 2 * n + half + 1)
                for k in range(4 * half, 4 * half + 4):
                    if t == 0 and k % 2 == 0:
                        weights_ready(pe, J_QKV + k // 2)
                    hi, lo = act_tile(n % 2, k)
                    for c0, c1_ in ((0, QW), (QW, GLU0)):
                        last = split_product(banks2(2)[:, c0:c1_], hi, lo, slice(k * GLU0 + c0, k * GLU0 + c1_), k == 0, k == KD - 1)
                if half == 1:
                    last.then_inc(s_z, 1)

            def score(t, hf):
                pe.wait_ge(s_kT, 2 * t + 2 if t < TS else 2 * t + 1)
                pe.wait_ge(s_qT, t + 1)
                if 2 * t + hf > 0:
                    pe.wait_ge(s_sb, 2 * t + hf)
                lo = P if t == 0 else 0
                for i in range(4):
                    h = 4 * hf + i
                    last = nc.tensor.matmul(banks2(6)[:, i * 2 * P + lo:(i + 1) * 2 * P], qT[0:HD, h * P:(h + 1) * P],
                                            kTb[0:HD, t % 2, hf, lo:2 * P], start=True, stop=True)
                last.then_inc(s_sc, 1)

            def prob_transpose(t, hf):
                pe.wait_ge(s_ex, 10 * t + 5 * hf + 5)
                pe.wait_ge(s_qT, min(t + hf + 1, NT))
                if 2 * t + hf > 0:
                    pe.wait_ge(s_pT, 2 * t + hf)
                for i in range(4):
                    for s in range(1 if t == 0 else 0, 2):
                        at = (2 * i + s) * P
                        last = nc.tensor.transpose(banks2(4)[:, at:at + P], S[:, at:at + P], ident)
                last.then_inc(s_pt, 1)

            def attend(t, hf):
                pe.wait_ge(s_pT, 2 * t + hf + 1)
                pe.wait_ge(s_v, t + 1)
                if t == TS:
                    pe.wait_ge(s_cv, 16)
                if hf == 0 and t >= 1:
                    pe.wait_ge(s_oe, t)
                before = 3 if t == TS else (t - 1) % 3
                for i in range(4):
                    h = 4 * hf + i
                    for s in range(1 if t == 0 else 0, 2):
                        slot = t % 3 if s else before
                        last = nc.tensor.matmul(bank(1)[:, h * HD:(h + 1) * HD], pT[:, (2 * i + s) * P:(2 * i + s + 1) * P],
                                                vb[:, slot, hf * HD:(hf + 1) * HD],
                                                start=(s == 0 or t == 0), stop=(s == 1))
                last.then_inc(s_pv, 1)

            def channel_sums(i):
                pe.wait_ge(s_ones, 1)
                if i == 0:
                    pe.wait_ge(s_conv, CONV_FIRST)
                    pe.wait_ge(s_convs, 1)
                    pe.wait_ge(s_xl, 4 * NT)
                    pe.wait_ge(s_zev, NT)
                    pe.wait_ge(s_v, NT)
                for c in range(KC):
                    last = nc.tensor.matmul(bank((0, 2, 3)[i], SPANS[i][1] * P), c_ones, span_view(i, c), start=(c == 0), stop=(c == KC - 1))
                last.then_inc(s_cs, 1)

            qkv(0, 0)
            qkv(0, 1)
            for t in range(NT + 1):
                if t + 1 < NT:
                    x_transpose(NT + t + 1, 0, 0, xb[(NT + t + 1) % 2])
                if t < NT:
                    pe.wait_ge(s_qkn, t + 1)
                    if t >= 1:
                        pe.wait_ge(s_pT, 2 * t - 1)
                        pe.wait_ge(s_sb, 2 * t)
                    for h in range(NH):
                        nc.tensor.transpose(banks2(4)[0:HD, h * P:(h + 1) * P], qkn[:, h * HD:(h + 1) * HD], ident)
                    for g in range(NKV):
                        last = nc.tensor.transpose(ps[0:HD, 6, g * P:(g + 1) * P], qkn[:, QW + g * HD:QW + (g + 1) * HD], ident)
                    last.then_inc(s_qkt, 1)
                if t + 1 < NT:
                    x_transpose(NT + t + 1, 1, 0, xb[(NT + t + 1) % 2])
                    qkv(t + 1, 0)
                if t == NT:
                    channel_sums(0)
                if t >= 1:
                    prob_transpose(t - 1, 1)
                if t < NT:
                    score(t, 0)
                if t >= 1:
                    attend(t - 1, 1)
                if t + 1 < NT:
                    qkv(t + 1, 1)
                if t < NT:
                    prob_transpose(t, 0)
                    score(t, 1)
                    attend(t, 0)

            pe.wait_ge(s_oe, NT)
            pe.wait_ge(s_conv, CONV_OPS)
            pe.wait_ge(s_convs, 2)
            channel_sums(1)
            channel_sums(2)
            for i in range(3):
                t0, nt = SPANS[i]
                n = nt * P
                pe.wait_ge(s_ca, 3 * (i + 1))
                for t in range(nt):
                    last = nc.tensor.matmul(ps[:, 5 - i, t0 + t:t0 + t + 1], c_sq[i][:, t * P:(t + 1) * P], c_ones[:, 0:1],
                                            start=True, stop=True)
                last.then_inc(s_cvv, 1)
            for i, (t0, nt) in enumerate(SPANS):
                pe.wait_ge(s_cdg, t0 + nt)
                pe.wait_ge(s_c1, KC * (i + 1))
                nc.tensor.matmul(bank((6, 7, 1)[i], nt * P), c_ones, c_rs[i][:, 0:nt * P], start=True, stop=True).then_inc(s_cbc, 1)
            weights_ready(pe, J_PW)
            pe.wait_ge(s_cve, 3)
            for i, (t0, nt) in enumerate(SPANS):
                pe.wait_ge(s_cl, KC * (i + 1))
                for t in range(t0, t0 + nt):
                    if t >= 2:
                        pe.wait_ge(s_c3, t - 1)
                    for c in range(KC):
                        b, at = swish_at(i, c)
                        at = slice(at.start + (t - t0) * P, at.start + (t - t0 + 1) * P)
                        last = split_product(bank(4 + t % 2), ahl[:, b, 0, at], ahl[:, b, 1, at], slice(PW0 + c * C, PW0 + (c + 1) * C),
                                             c == 0, c == KC - 1)
                    last.then_inc(s_pw, 1)

            pe.wait_ge(s_c1, 3 * KC)
            pe.wait_ge(s_cn, 3 * KC)
            pe.wait_ge(s_c3, NT)
            pe.wait_ge(s_o, NT)
            for h in range(2):
                pe.wait_ge(s_c4, 1)
                transposes(0, h, R[:, 0, :], h).then_inc(s_xt, 1)
            for t in range(NT + 2):
                n = 2 * NT + t + 1
                if t + 1 < NT:
                    pe.wait_ge(s_c4, t + 2)
                    for h in range(2):
                        pe.wait_ge(s_xl, 2 * n - 1 + h)
                        transposes(0, h, R[:, t + 1, :], h).then_inc(s_xt, 1)
                if t >= 2:
                    q = t - 2
                    pe.wait_ge(s_h, q + 1)
                    pe.wait_ge(s_hT, 2 * q)
                    transposes(0, 1, hb[q % 2], 7).then_inc(s_ht, 1)
                    pe.wait_ge(s_lg, q)
                    transposes(0, 0, hb[q % 2], 6).then_inc(s_ht, 1)
                if t < NT:
                    zb = 2 + 2 * (t % 2)
                    if t >= 2:
                        pe.wait_ge(s_x1, t - 1)
                    for k in range(KD):
                        if t == 0 and k % 2 == 0:
                            weights_ready(pe, J_OUT + k // 2)
                        if k % 4 == 0:
                            pe.wait_ge(s_xl, 2 * (n - 1) + k // 4 + 1)
                        hi, lo = act_tile((n - 1) % 2, k)
                        for i in range(2):
                            last = split_product(bank(zb + i), hi, lo, slice(k * D + i * C, k * D + (i + 1) * C), k == 0, k == KD - 1)
                    last.then_inc(s_w, 1)
                if t >= 2:
                    pe.wait_ge(s_hT, 2 * q + 2)
                    for k in range(KD):
                        last = nc.tensor.matmul(bank(6, NR), hT[:, k * P:(k + 1) * P], wr[:, k, :], start=(k == 0), stop=(k == KD - 1))
                    last.then_inc(s_rl, 1)

            pe.wait_ge(s_ld, 16 * LOADS)
            pe.wait_ge(s_rt, 1)
            pe.wait_ge(s_const, 6)
            nc.tensor.matmul(bank(0, NE), tri16, A12[:, 0:NE], start=True, stop=True)
            nc.tensor.matmul(ps[:, 0, NE:(NT + 1) * NE], tri16, A12[:, NE:(NT + 1) * NE], start=True, stop=False)
            for t in range(NT - 1, -1, -1):
                later = A12[:, t * NE:(t + 1) * NE].unsqueeze(1).broadcast_to([P, NT - t, NE])
                last = nc.tensor.matmul(ps[:, 0, (t + 1) * NE:(NT + 1) * NE].rearrange("p (t n) -> p t n", n=NE), ones16, later,
                                        start=False, stop=(t == 0), skip_group_check=(t > 0))
            last.then_inc(s_rtp, 1)
            for k in range(2):
                pe.wait_ge(s_rt, 2 + k)
                for t in range(NT):
                    last = nc.tensor.matmul(bank(2, 2 * NBLK), Ph[:, t * P:(t + 1) * P], V[:, t * 2 * NBLK:(t + 1) * 2 * NBLK],
                                            start=(k == 0 and t == 0), stop=(k == 1 and t == NT - 1))
                last.then_inc(s_rtp, 1)

            def slot_transpose(b, half, gathered=None, evacuated=None):
                if gathered is not None:
                    pe.wait_ge(s_g[b], gathered)
                if evacuated is not None:
                    pe.wait_ge(s_xsl, evacuated)
                last = transposes(0, half, xs[b], half)
                if half == 1:
                    last.then_inc(s_xst, 1)

            def expert_product(J, slot, blocks):
                pe.wait_ge(s_mlv, J + 1)
                pe.wait_ge(s_mlp, J + 1)
                for i, (b, hi, lo, first, last) in enumerate(blocks):
                    ins = split_product(bank(b), hi, lo, slice(slot * CH + i * C, slot * CH + (i + 1) * C), first, last)
                return ins

            pe.wait_ge(s_tab, 1)
            slot_transpose(0, 0, gathered=16)
            slot_transpose(0, 1)
            pe.sem_inc(s_mht, 1)
            with pe.Fori(0, NE, 2) as e0:
                for b in range(2):
                    e = e0 + b
                    slot = lambda c: (6 * b + c) % 4
                    pe.wait_ge(s_xsl, e + 1)
                    pe.wait_ge(s_mg, e + 1)
                    for c in (0, 1):
                        expert_product(6 * e + c, slot(c), [(2, *act_tile(b, 4 * c + i), c + i == 0, c == 1 and i == 3) for i in range(4)]
                                       ).then_inc(s_use, 1)
                    pe.wait_ge(s_mh, e + 1)
                    for c in (2, 3):
                        expert_product(6 * e + c, slot(c), [(3, *act_tile(b, 4 * (c - 2) + i), c + i == 2, c == 3 and i == 3) for i in range(4)]
                                       ).then_inc(s_use, 1)
                    slot_transpose(1 - b, 0, gathered=8 * e0 + 16 * (1 + b), evacuated=e + 1)
                    pe.wait_ge(s_mh, e + 2)
                    pe.wait_ge(s_hl, e + 1)
                    transposes(0, 0, th, 4).then_inc(s_mht, 1)
                    slot_transpose(1 - b, 1)
                    pe.wait_ge(s_hl, e + 2)
                    pe.wait_ge(s_y0, e + 1)
                    pe.wait_ge(s_y1, e + 1)
                    for c in (4, 5):
                        blocks = []
                        for i in range(4):
                            k = 2 * (c - 4) + i // 2
                            at = slice(k * P, (k + 1) * P)
                            blocks.append((5 + i % 2, hhl[:, 0, at], hhl[:, 1, at], k == 0, k == KE - 1))
                        expert_product(6 * e + c, slot(c), blocks).then_inc(s_use, 1)
            def ovf_block(j):
                if first_extra(j):
                    pe.wait_ge(s_xsl, NE + 1)
                else:
                    pe.wait_ge(g_gath, 16 * j)
                transposes(0, 0, xs[0], 0)
                transposes(0, 1, xs[0], 1).then_inc(g_pe, 1)
                pe.wait_ge(g_act, 3 * j + 1)
                for c in range(4):
                    pe.wait_ge(g_raw[c % 3], 32 * j + 16 * (c // 3 + 1))
                    for i in range(4):
                        k = 4 * (c % 2) + i
                        last = nc.tensor.matmul(bank(2 + c // 2), xs[1][:, k * P:(k + 1) * P], gbuf[c % 3][:, i * C:(i + 1) * C],
                                                start=(k == 0), stop=(k == KD - 1))
                    last.then_inc(g_use, 1)
                pe.wait_ge(g_dve, 3 * j + 2)
                transposes(0, 0, th, 4).then_inc(g_pe, 1)
                pe.wait_ge(g_act, 3 * j + 3)
                for c in range(2):
                    pe.wait_ge(g_raw[(c + 4) % 3], 32 * j + 16 * 2)
                    for i in range(4):
                        k = 2 * c + i // 2
                        last = nc.tensor.matmul(bank(5 + i % 2), xs[0][:, k * P:(k + 1) * P], gbuf[(c + 4) % 3][:, i * C:(i + 1) * C],
                                                start=(k == 0), stop=(k == KE - 1))
                    last.then_inc(g_use, 1)

            n_ovf = pe.value_load(novf[0:1, 0:1].bitcast(I32), min_val=0, max_val=NOVF)
            pe.sem_inc(g_use, 3)
            extra_blocks(pe, n_ovf, ovf_block)

            def p_transpose(t):
                pe.wait_ge(s_p[t % 2], 16 * (t // 2 + 1))
                pe.wait_ge(s_3pT, t)
                for k in range(PLE // P):
                    last = nc.tensor.transpose(ps[:, 6, k * P:(k + 1) * P], pin[t % 2][:, k * P:(k + 1) * P], ident)
                last.then_inc(s_3pt, 1)

            def x2_transpose(t):
                pe.wait_ge(s_3n, t + 1)
                for h in range(2):
                    if t >= 1:
                        pe.wait_ge(s_3l, 2 * t + h - 1)
                    transposes(0, h, xn3[t % 2], h).then_inc(s_3t, 1)

            def ple_project(t):
                pe.wait_ge(s_3pT, t + 1)
                pe.wait_ge(s_3m, t)
                for k in range(PLE // P):
                    for i in range(2):
                        last = nc.tensor.matmul(bank(4 + i), pT3[t % 2][:, k * P:(k + 1) * P], wproj[:, k * D + i * C:k * D + (i + 1) * C],
                                                start=(k == 0), stop=(k == PLE // P - 1))
                last.then_inc(s_3p, 1)

            pe.wait_ge(s_moe, 1)
            pe.wait_ge(s_gp, 16)
            p_transpose(0)
            ple_project(0)
            x2_transpose(0)
            for t in range(NT):
                if 1 <= t < NT - 1:
                    x2_transpose(t + 1)
                    p_transpose(t + 1)
                pe.wait_ge(s_3th, t)
                for k in range(KD):
                    if t == 0 and k == KD // 2:
                        x2_transpose(1)
                        p_transpose(1)
                    if t == 0 and k % 2 == 0:
                        pe.wait_ge(s_mlv, 6 * NE + k // 2 + 1)
                        pe.wait_ge(s_mlp, 6 * NE + k // 2 + 1)
                    if k % 4 == 0:
                        pe.wait_ge(s_3l, 2 * t + k // 4 + 1)
                    hi, lo = act_tile(t % 2, k)
                    for i in range(2):
                        last = split_product(bank(2 + i), hi, lo, slice(k * D + i * C, k * D + (i + 1) * C), k == 0, k == KD - 1)
                last.then_inc(s_3g, 1)
                if t >= 1:
                    ple_project(t)


_INS = ['x_prompt', 'x_sample', 'p_prompt', 'p_sample', 'cache_k', 'cache_v', 'state_conv', 'g_mix', 'w_in', 'g_q', 'g_k',
        'sinks', 'w_dw', 'b_dw', 'g_cn', 'b_cn', 'w_pw', 'b_pw', 'g_oa', 'g_oc', 'w_out', 'g_ffn', 'w_coarse', 'b_coarse',
        'w_fine', 'b_fine', 'w_e_gate', 'w_e_up', 'w_e_down', 'g_ple', 'w_ple_gate', 'w_ple_proj']
_OUTS = [('y_prompt', (1, SEQ, D)), ('y_sample', (1, SAMPLE, D)),
         ('new_k_prompt', (1, 1, P, NKV, HD)), ('new_v_prompt', (1, 1, P, NKV, HD)), ('new_conv_prompt', (1, 1, HALO, C)),
         ('new_k_sample', (1, 1, P, NKV, HD)), ('new_v_sample', (1, 1, P, NKV, HD)), ('new_conv_sample', (1, 1, HALO, C))]


def kernel(**inputs):
    import numpy as _np
    import concourse.bacc as _bacc
    from concourse import mybir as _mybir
    from concourse.bass_utils import run_bass_kernel_spmd as _run

    nc = _bacc.Bacc("TRN2", target_bir_lowering=False, num_devices=1)
    arrays, ins, outs = {}, {}, {}
    for name in _INS:
        arr = _np.ascontiguousarray(inputs[name])
        arrays[f"in_{name}"] = arr
        ins[name] = nc.dram_tensor(f"in_{name}", arr.shape, _mybir.dt.from_np(arr.dtype), kind="ExternalInput").ap()
    for name, shape in _OUTS:
        outs[name] = nc.dram_tensor(f"out_{name}", shape, F32, kind="ExternalOutput").ap()
    build_step(nc, ins, outs)
    r = _run(nc, [arrays], core_ids=[0])
    return tuple(r.results[0][f"out_{name}"] for name, _ in _OUTS)
```
